# Optimizing a Trainium2 kernel written in Bass

```python
import jax
import jax.numpy as jnp
from jax import lax
import numpy as np

D_MODEL = 1024
BATCH = 1
SEQ = 512
DEPTH = 2

GRID_W = 64
CTX_LEN = 256

FNET_GROUPS = 4
FNET_GROUP_DIM = 128
FNET_WIDTH = FNET_GROUPS * FNET_GROUP_DIM

NA_HEADS = 8
NA_HEAD_DIM = 64
NA_WIDTH = NA_HEADS * NA_HEAD_DIM
NA_KH = 8
NA_KW = 16
NA_SCALE = NA_HEAD_DIM ** -0.5

MLA_HEADS = 8
MLA_Q_LORA = 256
MLA_KV_LORA = 128
MLA_NOPE_DIM = 64
MLA_ROPE_DIM = 32
MLA_V_DIM = 64
MLA_WIDTH = MLA_HEADS * MLA_V_DIM
MLA_SCALE = (MLA_NOPE_DIM + MLA_ROPE_DIM) ** -0.5
ATTN_BLOCK = 128
ROPE_BASE = 10000.0

N_BRANCH = 3
BRANCH_DIM = 512

FFN_HIDDEN = -(-8 * D_MODEL // (3 * 256)) * 256

NORM_EPS = 1e-5
DEEPNORM_ALPHA = (2 * DEPTH) ** 0.25
DEEPNORM_BETA = (8 * DEPTH) ** -0.25

IN_SIZES = (FNET_WIDTH, NA_WIDTH, NA_WIDTH, NA_WIDTH, MLA_Q_LORA, MLA_KV_LORA, MLA_ROPE_DIM, N_BRANCH * D_MODEL)
IN_DIM = int(sum(IN_SIZES))
IN_OFFSETS = [int(v) for v in np.cumsum(IN_SIZES)[:-1]]


def layer_norm(x, g, b):
    xf = x.astype(jnp.float32)
    mu = jnp.mean(xf, axis=-1, keepdims=True)
    var = jnp.mean(jnp.square(xf - mu), axis=-1, keepdims=True)
    y = (xf - mu) * lax.rsqrt(var + NORM_EPS) * g.astype(jnp.float32) + b.astype(jnp.float32)
    return y.astype(x.dtype)

def rms_norm(x, g):
    xf = x.astype(jnp.float32)
    y = xf * lax.rsqrt(jnp.mean(jnp.square(xf), axis=-1, keepdims=True) + NORM_EPS) * g.astype(jnp.float32)
    return y.astype(x.dtype)

def rope_tables(n):
    t = jnp.arange(n, dtype=jnp.int32)
    rows = (t // GRID_W).astype(jnp.float32)
    cols = (t % GRID_W).astype(jnp.float32)
    n_freq = MLA_ROPE_DIM // 4
    inv_freq = ROPE_BASE ** (-jnp.arange(n_freq, dtype=jnp.float32) / n_freq)
    ang = jnp.concatenate([rows[:, None] * inv_freq, cols[:, None] * inv_freq], axis=-1)
    return jnp.cos(ang), jnp.sin(ang)

def axial_rope(x, cos, sin):
    xf = x.astype(jnp.float32)
    half = x.shape[-1] // 2
    x1, x2 = xf[..., :half], xf[..., half:]
    return jnp.concatenate([x1 * cos - x2 * sin, x2 * cos + x1 * sin], axis=-1).astype(x.dtype)

def split_heads(z, n_heads):
    b, n, w = z.shape
    return z.reshape(b, n, n_heads, w // n_heads)

def fourier_mix(z):
    b, n, _ = z.shape
    zg = z.reshape(b, n, FNET_GROUPS, FNET_GROUP_DIM).astype(jnp.float32)
    y = jnp.fft.fft2(zg, axes=(1, 3), norm='ortho').real
    return y.reshape(b, n, FNET_WIDTH).astype(z.dtype)

def softmax_attend(q, k, v, scale):
    s = jnp.einsum('bqhd,bkhd->bhqk', q, k, preferred_element_type=jnp.float32) * scale
    p = jax.nn.softmax(s, axis=-1).astype(v.dtype)
    return jnp.einsum('bhqk,bkhd->bqhd', p, v)

def blocked_attend(q, k, v, scale):
    b, n, h, dq = q.shape
    qb = q.reshape(b, n // ATTN_BLOCK, ATTN_BLOCK, h, dq).transpose(1, 0, 2, 3, 4)
    out = lax.map(lambda qi: softmax_attend(qi, k, v, scale), qb)
    return out.transpose(1, 0, 2, 3, 4).reshape(b, n, h, v.shape[-1])

def neighbourhood_attention(q, k, v, k_ctx, v_ctx, rpb, n_rows):
    b, n, h, dh = q.shape
    kh = min(NA_KH, n_rows)
    kw = NA_KW
    qg = q.reshape(b, n_rows, GRID_W, h, dh).transpose(1, 0, 2, 3, 4)
    kg = k.reshape(b, n_rows, GRID_W, h, dh)
    vg = v.reshape(b, n_rows, GRID_W, h, dh)
    cols = jnp.arange(GRID_W, dtype=jnp.int32)
    col_start = jnp.clip(cols - kw // 2, 0, GRID_W - kw)
    col_idx = col_start[:, None] + jnp.arange(kw, dtype=jnp.int32)
    dc = col_idx - cols[:, None] + (NA_KW - 1)
    rpb_c = rpb.astype(jnp.float32)[:, :, dc]
    n_loc = kh * kw

    def row_fn(args):
        r, q_r = args
        rs = jnp.clip(r - kh // 2, 0, n_rows - kh)
        k_rows = lax.dynamic_slice_in_dim(kg, rs, kh, axis=1)
        v_rows = lax.dynamic_slice_in_dim(vg, rs, kh, axis=1)
        k_win = k_rows[:, :, col_idx]
        v_win = v_rows[:, :, col_idx]
        dr = rs + jnp.arange(kh, dtype=jnp.int32) - r + (NA_KH - 1)
        bias = jnp.take(rpb_c, dr, axis=1).transpose(0, 2, 1, 3)
        s_loc = jnp.einsum('bwhd,bkwjhd->bhwkj', q_r, k_win, preferred_element_type=jnp.float32) * NA_SCALE + bias[None]
        s_ctx = jnp.einsum('bwhd,bchd->bhwc', q_r, k_ctx, preferred_element_type=jnp.float32) * NA_SCALE
        s = jnp.concatenate([s_loc.reshape(b, h, GRID_W, n_loc), s_ctx], axis=-1)
        p = jax.nn.softmax(s, axis=-1).astype(v.dtype)
        p_loc = p[..., :n_loc].reshape(b, h, GRID_W, kh, kw)
        p_ctx = p[..., n_loc:]
        return (jnp.einsum('bhwkj,bkwjhd->bwhd', p_loc, v_win)
                + jnp.einsum('bhwc,bchd->bwhd', p_ctx, v_ctx))

    out = lax.map(row_fn, (jnp.arange(n_rows, dtype=jnp.int32), qg))
    return out.transpose(1, 0, 2, 3, 4).reshape(b, n, h * dh)

def mla_queries(cq, g_q, w_uq, w_qr, rope):
    b, n, _ = cq.shape
    cq = rms_norm(cq, g_q)
    q_nope = (cq @ w_uq).reshape(b, n, MLA_HEADS, MLA_NOPE_DIM)
    q_rope = (cq @ w_qr).reshape(b, n, MLA_HEADS, MLA_ROPE_DIM)
    if rope is not None:
        q_rope = axial_rope(q_rope, rope[0][:, None, :], rope[1][:, None, :])
    return jnp.concatenate([q_nope, q_rope], axis=-1)

def mla_keys_values(ckv, kr, g_kv, w_uk, w_uv, rope):
    b, n, _ = ckv.shape
    ckv = rms_norm(ckv, g_kv)
    k_nope = (ckv @ w_uk).reshape(b, n, MLA_HEADS, MLA_NOPE_DIM)
    v = (ckv @ w_uv).reshape(b, n, MLA_HEADS, MLA_V_DIM)
    if rope is not None:
        kr = axial_rope(kr, rope[0], rope[1])
    k_rope = jnp.broadcast_to(kr[:, :, None, :], (b, n, MLA_HEADS, MLA_ROPE_DIM))
    return jnp.concatenate([k_nope, k_rope], axis=-1), v

def merge_branches(ys, g, w_branch, w_out):
    b, n, _ = g.shape
    y = jnp.stack(ys, axis=2)
    proj = jnp.einsum('bngi,gio->bngo', y, w_branch)
    gate = jax.nn.sigmoid(g.reshape(b, n, N_BRANCH, D_MODEL).astype(jnp.float32)).astype(proj.dtype)
    return jnp.sum(gate * proj, axis=2) @ w_out

def mixer(h, hc, lp, rope, n_rows, need_ctx):
    b, n, _ = h.shape
    f, nq, nk, nv, cq, ckv, kr, g = jnp.split(h @ lp['w_in'], IN_OFFSETS, axis=-1)
    fc, nqc, nkc, nvc, cqc, ckvc, krc, gc = jnp.split(hc @ lp['w_in'], IN_OFFSETS, axis=-1)
    na_kc, na_vc = split_heads(nkc, NA_HEADS), split_heads(nvc, NA_HEADS)
    mla_kc, mla_vc = mla_keys_values(ckvc, krc, lp['g_kv'], lp['w_uk'], lp['w_uv'], None)
    y_f = fourier_mix(f)
    y_na = neighbourhood_attention(split_heads(nq, NA_HEADS), split_heads(nk, NA_HEADS), split_heads(nv, NA_HEADS),
                                   na_kc, na_vc, lp['rpb'], n_rows)
    mla_k, mla_v = mla_keys_values(ckv, kr, lp['g_kv'], lp['w_uk'], lp['w_uv'], rope)
    mla_q = mla_queries(cq, lp['g_q'], lp['w_uq'], lp['w_qr'], rope)
    y_mla = blocked_attend(mla_q, jnp.concatenate([mla_kc, mla_k], axis=1),
                           jnp.concatenate([mla_vc, mla_v], axis=1), MLA_SCALE).reshape(b, n, MLA_WIDTH)
    out = merge_branches([y_f, y_na, y_mla], g, lp['w_branch'], lp['w_out'])
    if not need_ctx:
        return out, None
    n_ctx = hc.shape[1]
    yc_f = fourier_mix(fc)
    yc_na = softmax_attend(split_heads(nqc, NA_HEADS), na_kc, na_vc, NA_SCALE).reshape(b, n_ctx, NA_WIDTH)
    mla_qc = mla_queries(cqc, lp['g_q'], lp['w_uq'], lp['w_qr'], None)
    yc_mla = softmax_attend(mla_qc, mla_kc, mla_vc, MLA_SCALE).reshape(b, n_ctx, MLA_WIDTH)
    out_c = merge_branches([yc_f, yc_na, yc_mla], gc, lp['w_branch'], lp['w_out'])
    return out, out_c

def swiglu(h, w_gate, w_up, w_down):
    return (jax.nn.silu(h @ w_gate) * (h @ w_up)) @ w_down

def first_inputs(seed: int = 0) -> dict:
    key = jax.random.key(seed)
    ks = jax.random.split(key, 32)

    def nrm(k, shape, scale):
        return jax.random.normal(k, shape, dtype=jnp.float32) * scale

    L, D, F = DEPTH, D_MODEL, FFN_HIDDEN
    return {
        'x': nrm(ks[0], (BATCH, SEQ, D), 1.0),
        'c': nrm(ks[1], (BATCH, D), 1.0),
        'ctx': nrm(ks[2], (BATCH, CTX_LEN, D), 1.0),
        'c_ctx': nrm(ks[3], (D,), 1.0),
        'ln_in_g': 1.0 + nrm(ks[4], (D,), 0.02),
        'ln_in_b': nrm(ks[5], (D,), 0.02),
        'w_mod': nrm(ks[6], (L, D, 6 * D), 0.1 * D ** -0.5),
        'b_mod': nrm(ks[7], (L, 6 * D), 0.02),
        'w_in': nrm(ks[8], (L, D, IN_DIM), D ** -0.5),
        'mla_q_norm_g': 1.0 + nrm(ks[9], (L, MLA_Q_LORA), 0.02),
        'mla_kv_norm_g': 1.0 + nrm(ks[10], (L, MLA_KV_LORA), 0.02),
        'w_uq': nrm(ks[11], (L, MLA_Q_LORA, MLA_HEADS * MLA_NOPE_DIM), MLA_Q_LORA ** -0.5),
        'w_qr': nrm(ks[12], (L, MLA_Q_LORA, MLA_HEADS * MLA_ROPE_DIM), MLA_Q_LORA ** -0.5),
        'w_uk': nrm(ks[13], (L, MLA_KV_LORA, MLA_HEADS * MLA_NOPE_DIM), MLA_KV_LORA ** -0.5),
        'w_uv': nrm(ks[14], (L, MLA_KV_LORA, MLA_HEADS * MLA_V_DIM), MLA_KV_LORA ** -0.5),
        'na_rpb': nrm(ks[15], (L, NA_HEADS, 2 * NA_KH - 1, 2 * NA_KW - 1), 0.1),
        'w_branch': nrm(ks[16], (L, N_BRANCH, BRANCH_DIM, D), BRANCH_DIM ** -0.5),
        'w_out': nrm(ks[17], (L, D, D), DEEPNORM_BETA * D ** -0.5),
        'ln1_g': 1.0 + nrm(ks[18], (L, D), 0.02),
        'ln1_b': nrm(ks[19], (L, D), 0.02),
        'ln2_g': 1.0 + nrm(ks[20], (L, D), 0.02),
        'ln2_b': nrm(ks[21], (L, D), 0.02),
        'w_ffn_gate': nrm(ks[22], (L, D, F), D ** -0.5),
        'w_ffn_up': nrm(ks[23], (L, D, F), D ** -0.5),
        'w_ffn_down': nrm(ks[24], (L, F, D), DEEPNORM_BETA * F ** -0.5),
    }

def first_block(x, c, ctx, c_ctx, ln_in_g, ln_in_b, w_mod, b_mod, w_in, mla_q_norm_g, mla_kv_norm_g,
              w_uq, w_qr, w_uk, w_uv, na_rpb, w_branch, w_out, ln1_g, ln1_b, ln2_g, ln2_b,
              w_ffn_gate, w_ffn_up, w_ffn_down):
    n = x.shape[1]
    n_rows = n // GRID_W
    rope = rope_tables(n)
    x_lat = layer_norm(x, ln_in_g, ln_in_b)
    x_ctx = layer_norm(ctx, ln_in_g, ln_in_b)
    silu_c = jax.nn.silu(c)
    silu_cc = jax.nn.silu(c_ctx)
    for l in range(DEPTH):
        last = l == DEPTH - 1
        lp = {'w_in': w_in[l], 'g_q': mla_q_norm_g[l], 'g_kv': mla_kv_norm_g[l], 'w_uq': w_uq[l],
              'w_qr': w_qr[l], 'w_uk': w_uk[l], 'w_uv': w_uv[l], 'rpb': na_rpb[l],
              'w_branch': w_branch[l], 'w_out': w_out[l]}
        sh1, sc1, g1, sh2, sc2, g2 = [m[:, None, :] for m in jnp.split(silu_c @ w_mod[l] + b_mod[l], 6, axis=-1)]
        csh1, csc1, cg1, csh2, csc2, cg2 = jnp.split(silu_cc @ w_mod[l] + b_mod[l], 6, axis=-1)
        a_lat = x_lat * (1 + sc1) + sh1
        a_ctx = x_ctx * (1 + csc1) + csh1
        m_lat, m_ctx = mixer(a_lat, a_ctx, lp, rope, n_rows, not last)
        x_lat = layer_norm(DEEPNORM_ALPHA * x_lat + (1 + g1) * m_lat, ln1_g[l], ln1_b[l])
        f_lat = swiglu(x_lat * (1 + sc2) + sh2, w_ffn_gate[l], w_ffn_up[l], w_ffn_down[l])
        x_lat = layer_norm(DEEPNORM_ALPHA * x_lat + (1 + g2) * f_lat, ln2_g[l], ln2_b[l])
        if not last:
            x_ctx = layer_norm(DEEPNORM_ALPHA * x_ctx + (1 + cg1) * m_ctx, ln1_g[l], ln1_b[l])
            f_ctx = swiglu(x_ctx * (1 + csc2) + csh2, w_ffn_gate[l], w_ffn_up[l], w_ffn_down[l])
            x_ctx = layer_norm(DEEPNORM_ALPHA * x_ctx + (1 + cg2) * f_ctx, ln2_g[l], ln2_b[l])
    return x_lat


DEPTH_2 = 1

HEAD_DIM = 64
BLOCK = 128
SWA_Q_HEADS = 8
SWA_KV_HEADS = 2
SWA_GROUP = SWA_Q_HEADS // SWA_KV_HEADS
WINDOW = 128
SWA_WIDTH = SWA_Q_HEADS * HEAD_DIM
KV_WIDTH = SWA_KV_HEADS * HEAD_DIM
LRU_WIDTH = D_MODEL // 4
LRU_BLOCKS = 8
LRU_BLOCK_W = LRU_WIDTH // LRU_BLOCKS
CONV_WIDTH = 4
LRU_C = 8.0
FOX_HEADS = 4
FOX_WIDTH = FOX_HEADS * HEAD_DIM
D_MIX = SWA_WIDTH + LRU_WIDTH + FOX_WIDTH
OFF_KA = SWA_WIDTH
OFF_VA = OFF_KA + KV_WIDTH
OFF_XB = OFF_VA + KV_WIDTH
OFF_GB = OFF_XB + LRU_WIDTH
OFF_QC = OFF_GB + LRU_WIDTH
OFF_KC = OFF_QC + FOX_WIDTH
OFF_VC = OFF_KC + FOX_WIDTH
OFF_FC = OFF_VC + FOX_WIDTH
IN_COLS = OFF_FC + FOX_HEADS
IN_SPLITS = (OFF_KA, OFF_VA, OFF_XB, OFF_GB, OFF_QC, OFF_KC, OFF_VC, OFF_FC)
N_GROUPS = 4
EXPERTS_PER_GROUP = 4
N_EXPERTS = N_GROUPS * EXPERTS_PER_GROUP
TOP_K = 2
D_EXPERT = 256
EPS = 1e-6
F32 = jnp.float32


def rms_normalize(x):
    xf = x.astype(F32)
    return xf * lax.rsqrt(jnp.mean(xf * xf, axis=-1, keepdims=True) + EPS)

def rms_norm_2(x, gain):
    return (rms_normalize(x) * gain.astype(F32)).astype(x.dtype)

def modulate(h, shift, scale):
    return h * (1.0 + scale[:, None, :]) + shift[:, None, :]

def alibi_slopes(n_heads):
    return jnp.exp2(-8.0 * jnp.arange(1, n_heads + 1, dtype=F32) / n_heads)

def sliding_window_sink_attention(q, k, v, sinks):
    b, s, _, dh = q.shape
    nb = s // BLOCK
    qb = q.reshape(b, nb, BLOCK, SWA_KV_HEADS, SWA_GROUP, dh)

    def band(t):
        tb = t.reshape(b, nb, BLOCK, SWA_KV_HEADS, dh)
        prev = jnp.pad(tb[:, :-1], ((0, 0), (1, 0), (0, 0), (0, 0), (0, 0)))
        return jnp.concatenate([prev, tb], axis=2)

    kb, vb = band(k), band(v)
    scores = jnp.einsum('bnqhgd,bnkhd->bnhgqk', qb, kb).astype(F32) * (dh ** -0.5)
    q_pos = BLOCK + jnp.arange(BLOCK)
    k_pos = jnp.arange(2 * BLOCK)
    dist = q_pos[:, None] - k_pos[None, :]
    in_window = (dist >= 0) & (dist < WINDOW)
    block_exists = (jnp.arange(nb)[:, None, None] > 0) | (k_pos[None, None, :] >= BLOCK)
    valid = in_window[None] & block_exists
    slopes = alibi_slopes(SWA_Q_HEADS).reshape(SWA_KV_HEADS, SWA_GROUP)
    scores = scores - slopes[:, :, None, None] * dist.astype(F32)
    scores = jnp.where(valid[None, :, None, None], scores, -jnp.inf)
    sink = jnp.broadcast_to(sinks.astype(F32).reshape(SWA_KV_HEADS, SWA_GROUP, 1, 1),
                            scores.shape[:-1] + (1,))
    probs = jax.nn.softmax(jnp.concatenate([scores, sink], axis=-1), axis=-1)[..., :-1]
    out = jnp.einsum('bnhgqk,bnkhd->bnqhgd', probs.astype(v.dtype), vb)
    return out.reshape(b, s, SWA_Q_HEADS * dh)

def causal_depthwise_conv(x, w, bias):
    s = x.shape[1]
    xp = jnp.pad(x, ((0, 0), (CONV_WIDTH - 1, 0), (0, 0)))
    y = bias
    for k in range(CONV_WIDTH):
        y = y + xp[:, k:k + s] * w[k]
    return y

def rg_lru(x, w_a, b_a, w_x, b_x, lam):
    b, s, w = x.shape
    xb = x.reshape(b, s, LRU_BLOCKS, LRU_BLOCK_W)
    gate_a = jnp.einsum('bsnc,ncd->bsnd', xb, w_a).reshape(b, s, w) + b_a
    gate_x = jnp.einsum('bsnc,ncd->bsnd', xb, w_x).reshape(b, s, w) + b_x
    r = jax.nn.sigmoid(gate_a.astype(F32))
    i = jax.nn.sigmoid(gate_x.astype(F32))
    log_a = -LRU_C * r * jax.nn.softplus(-lam.astype(F32))
    a = jnp.exp(log_a)
    u = jnp.sqrt(-jnp.expm1(2.0 * log_a)) * (i * x.astype(F32))

    def combine(left, right):
        a_l, u_l = left
        a_r, u_r = right
        return a_l * a_r, a_r * u_l + u_r

    _, hs = lax.associative_scan(combine, (a, u), axis=1)
    return hs.astype(x.dtype)

def forgetting_attention(q, k, v, log_f):
    b, s, h, dh = q.shape
    nb = s // BLOCK
    cum = jnp.cumsum(log_f, axis=1).transpose(0, 2, 1)
    q_blocks = q.reshape(b, nb, BLOCK, h, dh).transpose(1, 0, 2, 3, 4)
    cum_q = cum.reshape(b, h, nb, BLOCK).transpose(2, 0, 1, 3)
    k_pos = jnp.arange(s)

    def attend_block(args):
        n, q_n, cq_n = args
        logits = jnp.einsum('bqhd,bkhd->bhqk', q_n, k).astype(F32) * (dh ** -0.5)
        logits = logits + (cq_n[..., :, None] - cum[:, :, None, :])
        q_pos = n * BLOCK + jnp.arange(BLOCK)
        causal = k_pos[None, :] <= q_pos[:, None]
        logits = jnp.where(causal, logits, -jnp.inf)
        probs = jax.nn.softmax(logits, axis=-1)
        return jnp.einsum('bhqk,bkhd->bqhd', probs.astype(v.dtype), v)

    out = lax.map(attend_block, (jnp.arange(nb), q_blocks, cum_q))
    return out.transpose(1, 0, 2, 3, 4).reshape(b, s, h * dh)

def hybrid_mixer(h, w_in, w_out, out_gain, sinks, conv_w, conv_b,
                 lru_wa, lru_ba, lru_wx, lru_bx, lru_lam, fox_bf):
    b, s, _ = h.shape
    proj = jnp.einsum('bsd,de->bse', h, w_in)
    q_a, k_a, v_a, x_b, g_b, q_c, k_c, v_c, f_c = jnp.split(proj, IN_SPLITS, axis=-1)
    y_a = sliding_window_sink_attention(
        q_a.reshape(b, s, SWA_Q_HEADS, HEAD_DIM),
        k_a.reshape(b, s, SWA_KV_HEADS, HEAD_DIM),
        v_a.reshape(b, s, SWA_KV_HEADS, HEAD_DIM), sinks)
    x_conv = causal_depthwise_conv(x_b, conv_w, conv_b)
    y_b = rg_lru(x_conv, lru_wa, lru_ba, lru_wx, lru_bx, lru_lam) * jax.nn.gelu(g_b)
    log_f = jax.nn.log_sigmoid(f_c.astype(F32) + fox_bf.astype(F32))
    y_c = forgetting_attention(
        q_c.reshape(b, s, FOX_HEADS, HEAD_DIM),
        k_c.reshape(b, s, FOX_HEADS, HEAD_DIM),
        v_c.reshape(b, s, FOX_HEADS, HEAD_DIM), log_f)
    y = jnp.concatenate([rms_normalize(y_a), rms_normalize(y_b), rms_normalize(y_c)], axis=-1)
    y = (y * out_gain.astype(F32)).astype(h.dtype)
    return jnp.einsum('bse,ed->bsd', y, w_out)

def hierarchical_moe(h, w_rg, b_rg, w_re, b_re, w_gate, w_up, w_down):
    b, s, _ = h.shape
    group_logits = (jnp.einsum('bsd,dg->bsg', h, w_rg) + b_rg).astype(F32)
    group_prob = jax.nn.softmax(group_logits, axis=-1)
    group_p, group_idx = lax.top_k(group_prob, 1)
    expert_logits = (jnp.einsum('bsd,de->bse', h, w_re) + b_re).astype(F32)
    expert_logits = expert_logits.reshape(b, s, N_GROUPS, EXPERTS_PER_GROUP)
    in_group = jnp.take_along_axis(expert_logits, group_idx[..., None], axis=2)[:, :, 0]
    expert_prob = jax.nn.softmax(in_group, axis=-1)
    top_p, top_local = lax.top_k(expert_prob, TOP_K)
    weights = group_p * top_p / jnp.sum(top_p, axis=-1, keepdims=True)
    expert_idx = group_idx * EXPERTS_PER_GROUP + top_local
    combine = jnp.sum(jax.nn.one_hot(expert_idx, N_EXPERTS, dtype=F32) * weights[..., None], axis=-2)
    combine = combine.astype(h.dtype)
    y = jnp.zeros_like(h)
    for e in range(N_EXPERTS):
        hidden = jax.nn.silu(h @ w_gate[e]) * (h @ w_up[e])
        y = y + combine[..., e:e + 1] * (hidden @ w_down[e])
    return y

def second_inputs(seed: int = 0) -> dict:
    key = jax.random.key(seed)
    ks = jax.random.split(key, 26)
    L, D = DEPTH_2, D_MODEL

    def nrm(k, shape, scale):
        return scale * jax.random.normal(k, shape, F32)

    gate_offset = jnp.concatenate([jnp.zeros((2 * D,), F32), jnp.ones((D,), F32),
                                   jnp.zeros((2 * D,), F32), jnp.ones((D,), F32)])
    u = jax.random.uniform(ks[16], (L, LRU_WIDTH), F32, 0.9, 0.999)
    root = u ** (1.0 / LRU_C)
    lru_lam = jnp.log(root) - jnp.log1p(-root)
    return {
        'x': nrm(ks[0], (BATCH, SEQ, D), 1.0),
        'c': nrm(ks[1], (BATCH, D), 1.0),
        'w_mod': nrm(ks[2], (L, D, 6 * D), 0.25 * D ** -0.5),
        'b_mod': nrm(ks[3], (L, 6 * D), 0.1) + gate_offset,
        'norm_mix': 1.0 + nrm(ks[4], (L, D), 0.1),
        'norm_ffn': 1.0 + nrm(ks[5], (L, D), 0.1),
        'w_in': nrm(ks[6], (L, D, IN_COLS), D ** -0.5),
        'w_out': nrm(ks[7], (L, D_MIX, D), D_MIX ** -0.5),
        'out_gain': 1.0 + nrm(ks[8], (L, D_MIX), 0.1),
        'sinks': nrm(ks[9], (L, SWA_Q_HEADS), 0.5),
        'conv_w': nrm(ks[10], (L, CONV_WIDTH, LRU_WIDTH), CONV_WIDTH ** -0.5),
        'conv_b': nrm(ks[11], (L, LRU_WIDTH), 0.02),
        'lru_wa': nrm(ks[12], (L, LRU_BLOCKS, LRU_BLOCK_W, LRU_BLOCK_W), LRU_BLOCK_W ** -0.5),
        'lru_ba': nrm(ks[13], (L, LRU_WIDTH), 0.02),
        'lru_wx': nrm(ks[14], (L, LRU_BLOCKS, LRU_BLOCK_W, LRU_BLOCK_W), LRU_BLOCK_W ** -0.5),
        'lru_bx': nrm(ks[15], (L, LRU_WIDTH), 0.02),
        'lru_lam': lru_lam,
        'fox_bf': jax.random.uniform(ks[17], (L, FOX_HEADS), F32, 1.0, 5.0),
        'w_router_group': nrm(ks[18], (L, D, N_GROUPS), D ** -0.5),
        'b_router_group': nrm(ks[19], (L, N_GROUPS), 0.01),
        'w_router_expert': nrm(ks[20], (L, D, N_EXPERTS), D ** -0.5),
        'b_router_expert': nrm(ks[21], (L, N_EXPERTS), 0.01),
        'w_gate': nrm(ks[22], (L, N_EXPERTS, D, D_EXPERT), D ** -0.5),
        'w_up': nrm(ks[23], (L, N_EXPERTS, D, D_EXPERT), D ** -0.5),
        'w_down': nrm(ks[24], (L, N_EXPERTS, D_EXPERT, D), D_EXPERT ** -0.5),
        'norm_final': 1.0 + nrm(ks[25], (D,), 0.1),
    }

def second_block(x, c, w_mod, b_mod, norm_mix, norm_ffn, w_in, w_out, out_gain, sinks,
              conv_w, conv_b, lru_wa, lru_ba, lru_wx, lru_bx, lru_lam, fox_bf,
              w_router_group, b_router_group, w_router_expert, b_router_expert,
              w_gate, w_up, w_down, norm_final):
    c_act = jax.nn.silu(c)
    for l in range(DEPTH_2):
        mod = c_act @ w_mod[l] + b_mod[l]
        shift_m, scale_m, gate_m, shift_f, scale_f, gate_f = jnp.split(mod, 6, axis=-1)
        h = modulate(rms_norm_2(x, norm_mix[l]), shift_m, scale_m)
        x = x + gate_m[:, None, :] * hybrid_mixer(
            h, w_in[l], w_out[l], out_gain[l], sinks[l], conv_w[l], conv_b[l],
            lru_wa[l], lru_ba[l], lru_wx[l], lru_bx[l], lru_lam[l], fox_bf[l])
        h = modulate(rms_norm_2(x, norm_ffn[l]), shift_f, scale_f)
        x = x + gate_f[:, None, :] * hierarchical_moe(
            h, w_router_group[l], b_router_group[l], w_router_expert[l], b_router_expert[l],
            w_gate[l], w_up[l], w_down[l])
    return rms_norm_2(x, norm_final)


def setup_inputs(seed=0):
    out = dict(first_inputs(seed))
    for name, value in second_inputs(seed + 1).items():
        if name != "x":
            out[name + "_2"] = value
    return out


def reference(
    x, c, ctx, c_ctx, ln_in_g, ln_in_b, w_mod, b_mod, w_in, mla_q_norm_g, mla_kv_norm_g, w_uq,
    w_qr, w_uk, w_uv, na_rpb, w_branch, w_out, ln1_g, ln1_b, ln2_g, ln2_b, w_ffn_gate, w_ffn_up,
    w_ffn_down, c_2, w_mod_2, b_mod_2, norm_mix_2, norm_ffn_2, w_in_2, w_out_2, out_gain_2,
    sinks_2, conv_w_2, conv_b_2, lru_wa_2, lru_ba_2, lru_wx_2, lru_bx_2, lru_lam_2, fox_bf_2,
    w_router_group_2, b_router_group_2, w_router_expert_2, b_router_expert_2, w_gate_2, w_up_2,
    w_down_2, norm_final_2,
):
    x = first_block(
        x, c, ctx, c_ctx, ln_in_g, ln_in_b, w_mod, b_mod, w_in, mla_q_norm_g, mla_kv_norm_g,
        w_uq, w_qr, w_uk, w_uv, na_rpb, w_branch, w_out, ln1_g, ln1_b, ln2_g, ln2_b, w_ffn_gate,
        w_ffn_up, w_ffn_down,
    )
    return second_block(
        x, c_2, w_mod_2, b_mod_2, norm_mix_2, norm_ffn_2, w_in_2, w_out_2, out_gain_2, sinks_2,
        conv_w_2, conv_b_2, lru_wa_2, lru_ba_2, lru_wx_2, lru_bx_2, lru_lam_2, fox_bf_2,
        w_router_group_2, b_router_group_2, w_router_expert_2, b_router_expert_2, w_gate_2,
        w_up_2, w_down_2, norm_final_2,
    )


_drawn_inputs = setup_inputs


def setup_inputs(seed=0):
    import zlib

    import numpy as np

    out = dict(_drawn_inputs(seed))
    spreads = {}
    factors = {'mla_q_norm_g': 8.0,
     'mla_kv_norm_g': 8.0,
     'w_qr': 3.197,
     'na_rpb': 8.0,
     'lru_ba_2': 27.328,
     'lru_bx_2': 6.132,
     'b_router_group_2': 4.522,
     'b_router_expert_2': 8.0}
    for name, (base, spread) in spreads.items():
        noise = np.random.default_rng([zlib.crc32(name.encode()), seed]).standard_normal(out[name].shape)
        drawn = base * np.exp(spread * noise) if base else spread * noise
        out[name] = jnp.asarray(drawn.astype(out[name].dtype))
    for name, factor in factors.items():
        out[name] = (out[name] * factor).astype(out[name].dtype)
    return out
```

```python
from contextlib import ExitStack

import numpy as np

import concourse.bass as bass
from concourse import mybir

F32 = mybir.dt.float32
F32R = mybir.dt.float32r
ALU = mybir.AluOpType
ACT = mybir.ActivationFunctionType
AX = mybir.AxisListType.X

P = 128
D = 1024
KT = D // P
LAT, CTX = 512, 256
ALL = LAT + CTX
DEPTH = 2
GRID_W = 64
ROWS = LAT // GRID_W
FNET_W, NA_W = 512, 512
HEADS = 8
HD = 64
KH, KW = 8, 16
Q_LORA, KV_LORA, ROPE = 256, 128, 32
MLA_K = HD + ROPE
MLA_SCALE = float(MLA_K) ** -0.5
NA_SCALE = float(HD) ** -0.5
FFN = 2816
ALPHA = float((2 * DEPTH) ** 0.25)
LN_EPS = 1e-5
RMS_EPS = 1e-6
GATE_COL = FNET_W + 3 * NA_W + Q_LORA + KV_LORA + ROPE
MASKED = -1.0e30
N_EXP, D_EXP = 16, 256
FOX_H, SWA_H = 4, 8
LRU_W = 256
BANK = 512

T_F, T_NQ, T_NK, T_NV, T_CQ, T_CKV, T_KR = 0, 4, 8, 12, 16, 18, 19
T_Y = (0, 4, 8)
T_M = 12
S_QA, S_KA, S_VA, S_XB, S_GB, S_QC, S_KC, S_VC = 0, 4, 5, 6, 8, 10, 12, 14


class Tally:

    def __init__(self, sem):
        self.sem, self.base = sem, 0


class Chain:

    def __init__(self, eng, tally):
        self.eng, self.tally, self.n, self.i, self.per = eng, tally, 0, None, 0

    def value(self):
        v = self.tally.base + self.n
        return v if self.i is None else self.i * self.per + v

    def mark(self, ins):
        ins.then_inc(self.tally.sem, 1)
        self.n += 1
        return ins

    def link(self, ins):
        self.mark(ins)
        self.eng.wait_ge(self.tally.sem, self.value())

    def open(self, i, per):
        self.i, self.per, self.start = i, per, self.n

    def close(self, trips):
        assert self.n - self.start == self.per, (self.n - self.start, self.per)
        self.n += (trips - 1) * self.per
        self.i = None

    def done(self):
        self.tally.final = self.n


def groups(T):
    return [(0, min(T, LAT))] + ([(LAT, T - LAT)] if T > LAT else [])


def program(nc, g, out):
    root = ExitStack()
    with root:
        names = [0]

        def sb(ctx, name, shape, dt=F32):
            names[0] += 1
            return ctx.enter_context(nc.sbuf_tensor(f"{name}_{names[0]}", shape, dt))

        def tally(name):
            return Tally(root.enter_context(nc.semaphore(name)))

        ps = root.enter_context(nc.psum_tensor("ps", [P, 8 * BANK], F32))

        w_loaded = [tally(f"w_loaded{j}") for j in range(2)]
        hi_ready = [tally(f"hi_ready{j}") for j in range(2)]
        lo_ready = [tally(f"lo_ready{j}") for j in range(2)]
        mm_done = [tally(f"mm_done{j}") for j in range(2)]
        psum_free = [tally(f"psum_free{j}") for j in range(2)]
        h_scaled, h_hi_ready, gated = tally("h_scaled"), tally("h_hi_ready"), tally("gated")
        dve_chain, act_chain, pool_chain, pe_chain = (tally(n) for n in ("dve_chain", "act_chain", "pool_chain", "pe_chain"))
        ld = [tally(f"ld{n}") for n in range(16)]
        s_done, nm_done, p_done, pn_done, t_done, pt_done, pv_done, o_done = (
            tally(n) for n in ("s_done", "nm_done", "p_done", "pn_done", "t_done", "pt_done", "pv_done", "o_done"))
        qk_staged, v_staged, prep_mm, prep_out, prep_rope = (tally(n) for n in ("qk_staged", "v_staged", "prep_mm", "prep_out", "prep_rope"))
        head_w = [tally(f"head_w{j}") for j in range(2)]
        bias_masked = tally("bias_masked")
        norm_mean, norm_c, norm_sq, norm_var, norm_rstd = (tally(n) for n in ("norm_mean", "norm_c", "norm_sq", "norm_var", "norm_rstd"))
        norm_sqrt, norm_x, norm_g, norm_hi = (tally(n) for n in ("norm_sqrt", "norm_x", "norm_g", "norm_hi"))

        def finish(*tallies):
            for t in tallies:
                t.base += t.final
                t.final = 0

        ident = sb(root, "ident", [P, P])
        ones = sb(root, "ones", [P, P])
        vec1 = sb(root, "vec1", [P, 128])
        vec2 = sb(root, "vec2", [P, 96])
        vec3 = sb(root, "vec3", [P, 78])
        csilu = sb(root, "csilu", [P, 3, KT])
        mod = sb(root, "mod", [P, 2, 48])
        x = sb(root, "x", [P, KT, ALL])
        scale_row = sb(root, "scale_row", [P, 1])

        V_LN_IN_G, V_LN_IN_B = 0, 8
        V_LN1_G, V_LN1_B, V_LN2_G, V_LN2_B = 16, 32, 48, 64
        V_C, V_MIX, V_FFN, V_FINAL = 80, 104, 112, 120
        V3_QN, V3_KVN, V3_GAIN, V3_CONVW, V3_CONVB, V3_BA, V3_BX, V3_LAM = 48, 52, 54, 62, 70, 72, 74, 76

        def col(v, n):
            return v[:, n:n + 1]

        def setup():
            with ExitStack() as c:
                rows = sb(c, "rows", [P, 3, P])
                xin = sb(c, "xin", [P, 6, D])
                block = c.enter_context(nc.Block())

                @block.sync
                def _(sp):
                    sp.dma_start(ident[:], g["k_ident"]).then_inc(ld[0].sem, 16)
                    at = 0

                    def put(tile, src, n):
                        nonlocal at
                        sp.dma_start(rows[at:at + n, tile, :], src).then_inc(ld[1].sem, 16)
                        at += n

                    r8 = lambda a: a.rearrange("(k p) -> k p", p=P)
                    r2 = lambda a: a.rearrange("l (k p) -> (l k) p", p=P)
                    for a in ("ln_in_g", "ln_in_b"):
                        put(0, r8(g[a]), 8)
                    for a in ("ln1_g", "ln1_b", "ln2_g", "ln2_b"):
                        put(0, r2(g[a]), 16)
                    put(0, r2(g["c"]), 8)
                    put(0, r8(g["c_ctx"]), 8)
                    put(0, r2(g["c_2"]), 8)
                    put(0, r2(g["norm_mix_2"]), 8)
                    put(0, r2(g["norm_ffn_2"]), 8)
                    put(0, r8(g["norm_final_2"]), 8)
                    at = 0
                    put(1, r2(g["b_mod"]), 96)
                    at = 0
                    put(2, r2(g["b_mod_2"]), 48)
                    put(2, r2(g["mla_q_norm_g"]), 4)
                    put(2, r2(g["mla_kv_norm_g"]), 2)
                    put(2, r2(g["out_gain_2"]), 8)
                    put(2, g["conv_w_2"].rearrange("l w (k p) -> (l w k) p", p=P), 8)
                    for a in ("conv_b_2", "lru_ba_2", "lru_bx_2", "lru_lam_2"):
                        put(2, r2(g[a]), 2)
                    for t in range(4):
                        sp.dma_start(xin[:, t, :], g["x"][0, t * P:(t + 1) * P, :]).then_inc(ld[2].sem, 16)
                    for t in range(2):
                        sp.dma_start(xin[:, 4 + t, :], g["ctx"][0, t * P:(t + 1) * P, :]).then_inc(ld[2].sem, 16)

                n_rows = 12 + 1 + 9

                @block.tensor
                def _(pe):
                    pe.wait_ge(ld[0].sem, 16)
                    pe.wait_ge(ld[1].sem, 16 * n_rows)
                    for t, n in enumerate((128, 96, 78)):
                        m = pe.transpose(ps[:, t * P:t * P + n], rows[0:n, t, :], ident[0:n, 0:n])
                    m.then_inc(pe_chain.sem, 1)
                    pe.wait_ge(ld[2].sem, 96)
                    for u in range(12):
                        k, half = u // 2, u % 2
                        if u >= 4:
                            pe.wait_ge(act_chain.sem, 1 + u - 3)
                        for q in range(4):
                            m = pe.transpose(ps[:, BANK * (1 + u % 4) + q * P:BANK * (1 + u % 4) + (q + 1) * P],
                                             xin[:, u // 2, (4 * half + q) * P:(4 * half + q + 1) * P], ident[:])
                        m.then_inc(pe_chain.sem, 1)

                @block.vector
                def _(dve):
                    dve.memset(ones[:], 1.0)
                    dve.memset(scale_row[:], NA_SCALE)
                    dve.wait_ge(pe_chain.sem, 1)
                    for t, (v, n) in enumerate(((vec1, 128), (vec2, 96), (vec3, 78))):
                        m = dve.tensor_copy(v[:], ps[:, t * P:t * P + n])
                    m.then_inc(dve_chain.sem, 1)

                @block.scalar
                def _(act):
                    act.wait_ge(dve_chain.sem, 1)
                    act.activation(csilu[:].rearrange("p a k -> p (a k)"), vec1[:, V_C:V_C + 24], ACT.Silu).then_inc(act_chain.sem, 1)
                    for u in range(12):
                        t, half = u // 2, u % 2
                        act.wait_ge(pe_chain.sem, 2 + u)
                        b = BANK * (1 + u % 4)
                        act.copy(x[:, 4 * half:4 * half + 4, t * P:(t + 1) * P],
                                 ps[:, b:b + 512].rearrange("p (q n) -> p q n", q=4)).then_inc(act_chain.sem, 1)
            ld[0].base += 16
            ld[1].base += 16 * 22
            ld[2].base += 96
            pe_chain.base += 13
            act_chain.base += 13
            dve_chain.base += 1

        def modulation(w, cols, bias, n_vec):
            RING = 8
            with ExitStack() as c:
                ring = sb(c, "mod_w", [P, RING, KT, P])
                rhs = sb(c, "mod_c", [P, KT, 2])
                loads = [ld[n] for n in range(RING)]
                tiles = 6 * KT
                trips = tiles // RING
                wv = w.rearrange("(k p) c -> p k c", p=P)
                block = c.enter_context(nc.Block())

                @block.sync
                def _(sp):
                    for s in range(RING):
                        sp.dma_start(ring[:, s], wv[:, :, s * P:(s + 1) * P]).then_inc(loads[s].sem, 16)
                    with sp.Fori(1, trips) as i:
                        for s in range(RING):
                            sp.wait_ge(pe_chain.sem, i * RING + (pe_chain.base - RING + s + 1))
                            sp.dma_start(ring[:, s], wv[:, :, bass.ds(i * (RING * P) + s * P, P)]).then_inc(loads[s].sem, 16)

                @block.tensor
                def _(pe):
                    pe.wait_ge(dve_chain.sem, dve_chain.base + 1)
                    with pe.Fori(0, trips) as i:
                        for s in range(RING):
                            pe.wait_ge(loads[s].sem, i * 16 + (loads[s].base + 16))
                            for k in range(KT):
                                m = pe.matmul(ps[:, bass.ds(i * (RING * 2) + s * 2, 2)], ring[:, s, k, :], rhs[:, k, :],
                                              start=(k == 0), stop=(k == KT - 1))
                            m.then_inc(pe_chain.sem, 1)

                @block.vector
                def _(dve):
                    a, b = cols
                    ch = Chain(dve, dve_chain)
                    dve.tensor_copy(rhs[:, :, 0], csilu[:, a, :])
                    ch.link(dve.tensor_copy(rhs[:, :, 1], csilu[:, b, :]))
                    dve.wait_ge(pe_chain.sem, pe_chain.base + tiles)
                    for v in range(2):
                        m = dve.tensor_tensor(mod[:, v, :], ps[:, v:2 * tiles:2], bias, ALU.add)
                        ch.mark(m)
                    dve.wait_ge(dve_chain.sem, ch.value())
                    if n_vec == 2:
                        for s in (1, 2, 4, 5):
                            m = dve.tensor_scalar(mod[:, :, s * KT:(s + 1) * KT], mod[:, :, s * KT:(s + 1) * KT], 1.0, None, ALU.add)
                    else:
                        for s in (1, 4):
                            m = dve.tensor_scalar(mod[:, :, s * KT:(s + 1) * KT], mod[:, :, s * KT:(s + 1) * KT], 1.0, None, ALU.add)
                    ch.done()
            for l in loads:
                l.base += 16 * trips
            pe_chain.base += tiles
            finish(dve_chain)

        def normalize(tiles, T, eps, gain, bias=None, center=False, post=None, after=None, src=None):
            n = len(tiles)
            dim = n * P
            tg = groups(T)
            src = src or tiles
            with ExitStack() as c:
                sq = sb(c, "sq", [P, 2, T])
                rstd = sb(c, "rstd", [P, T])
                if post:
                    tmp = sb(c, "tmp", [P, 2, T])
                block = c.enter_context(nc.Block())

                @block.tensor
                def _(pe):
                    if center:
                        for t0, tn in tg:
                            for k in range(n):
                                m = pe.matmul(ps[:, t0:t0 + tn], ones[:], src[k][:, t0:t0 + tn], start=(k == 0), stop=(k == n - 1))
                        m.then_inc(norm_mean.sem, 1)
                    for k in range(n):
                        pe.wait_ge(norm_sq.sem, norm_sq.base + k + 1)
                        for t0, tn in tg:
                            m = pe.matmul(ps[:, 1024 + t0:1024 + t0 + tn], ones[:], sq[:, k % 2, t0:t0 + tn],
                                          start=(k == 0), stop=(k == n - 1), skip_group_check=True)
                        m.then_inc(norm_var.sem, 1)

                @block.scalar
                def _(act):
                    for k in range(n):
                        if center:
                            act.wait_ge(norm_c.sem, norm_c.base + k + 1)
                        if k >= 2:
                            act.wait_ge(norm_var.sem, norm_var.base + k - 1)
                        act.activation(sq[:, k % 2, :], (tiles if center else src)[k], ACT.Square).then_inc(norm_sq.sem, 1)
                    act.wait_ge(norm_rstd.sem, norm_rstd.base + 1)
                    act.activation(rstd[:], rstd[:], ACT.Sqrt).then_inc(norm_sqrt.sem, 1)
                    for k in range(n):
                        act.wait_ge(norm_x.sem, norm_x.base + k + 1)
                        act.activation(tiles[k], tiles[k], ACT.Identity, scale=gain(k), bias=bias(k) if bias else 0.0).then_inc(norm_g.sem, 1)
                    if post:
                        for k in range(n):
                            act.wait_ge(norm_rstd.sem, norm_rstd.base + 2 + k)
                            act.copy(post[0][:, k, 0:T], tmp[:, k % 2, :]).then_inc(norm_hi.sem, 1)

                @block.vector
                def _(dve):
                    ch = Chain(dve, dve_chain)
                    if center:
                        dve.wait_ge(norm_mean.sem, norm_mean.base + 1)
                        for k in range(n):
                            dve.scalar_tensor_tensor(out=tiles[k], in0=ps[:, 0:T], scalar=-1.0 / dim, in1=src[k],
                                                     op0=ALU.mult, op1=ALU.add).then_inc(norm_c.sem, 1)
                    dve.wait_ge(norm_var.sem, norm_var.base + n)
                    dve.tensor_scalar(rstd[:], ps[:, 1024:1024 + T], 1.0 / dim, eps, ALU.mult, ALU.add).then_inc(norm_rstd.sem, 1)
                    dve.wait_ge(norm_sqrt.sem, norm_sqrt.base + 1)
                    ch.link(dve.reciprocal(rstd[:], rstd[:]))
                    for k in range(n):
                        dve.tensor_tensor(tiles[k], (tiles if center else src)[k], rstd[:], ALU.mult).then_inc(norm_x.sem, 1)
                    if post:
                        hi, lo, scale, shift = post

                        def rest(k):
                            dve.wait_ge(norm_hi.sem, norm_hi.base + k + 1)
                            ch.mark(dve.tensor_tensor(lo[:, k, 0:T], tmp[:, k % 2, :], hi[:, k, 0:T].bitcast(F32), ALU.subtract))

                        def scaled(k):
                            dve.wait_ge(norm_rstd.sem, norm_rstd.base + 2 + k)
                            dve.tensor_scalar(tiles[k], tiles[k], after, None, ALU.mult)

                        for k in range(n):
                            dve.wait_ge(norm_g.sem, norm_g.base + k + 1)
                            if k >= 2:
                                dve.wait_ge(dve_chain.sem, ch.value())
                            for v, (t0, tn) in enumerate(tg):
                                m = dve.tensor_scalar(tmp[:, k % 2, t0:t0 + tn], tiles[k][:, t0:t0 + tn],
                                                      scale(v, k), shift(v, k), ALU.mult, ALU.add)
                            m.then_inc(norm_rstd.sem, 1)
                            if k >= 1:
                                rest(k - 1)
                                if after:
                                    scaled(k - 1)
                        rest(n - 1)
                        if after:
                            scaled(n - 1)
                    ch.done()
            finish(dve_chain)
            norm_mean.base += center
            norm_c.base += n if center else 0
            norm_sq.base += n
            norm_var.base += n
            norm_rstd.base += 1 + (n if post else 0)
            norm_sqrt.base += 1
            norm_x.base += n
            norm_g.base += n
            norm_hi.base += n if post else 0

        def dense(ring, chunks, per, blocks, loads, parts, T, act_out, dve_out):
            raw, whi, wlo = ring
            trips = chunks // per
            half = per // 2
            tg = groups(T)

            def use(i, jj):
                return i * half + jj // 2

            n_loads = len(loads(0, 0))
            with ExitStack() as c:
                block = c.enter_context(nc.Block())

                @block.sync
                def _(sp):
                    with sp.Fori(0, trips) as i:
                        for jj in range(per):
                            j = jj % 2
                            sp.wait_ge(lo_ready[j].sem, use(i, jj) + lo_ready[j].base)
                            for b0, nb, src in loads(i, jj):
                                sp.dma_start(raw[:, j, b0:b0 + nb, :], src).then_inc(w_loaded[j].sem, 16)

                @block.tensor
                def _(pe):
                    with pe.Fori(0, trips) as i:
                        for jj in range(per):
                            j = jj % 2
                            pe.wait_ge(lo_ready[j].sem, use(i, jj) + (lo_ready[j].base + 1))
                            pe.wait_ge(psum_free[j].sem, use(i, jj) + psum_free[j].base)
                            for off, b0, nb, hi, lo in parts:
                                for t0, tn in tg:
                                    o = ps[:, 4 * BANK * j + off + t0:4 * BANK * j + off + t0 + tn]
                                    for b in range(nb):
                                        pe.matmul(o, whi[:, j, b0 + b, :], hi[:, b, t0:t0 + tn], start=(b == 0), stop=False)
                                        pe.matmul(o, wlo[:, j, b0 + b, :], hi[:, b, t0:t0 + tn], start=False, stop=False)
                                        m = pe.matmul(o, whi[:, j, b0 + b, :], lo[:, b, t0:t0 + tn], start=False, stop=(b == nb - 1))
                            m.then_inc(mm_done[j].sem, 1)

                def pipelined(eng, split, take, chain, per_links):
                    split(0, 0)
                    if trips > 1:
                        with eng.Fori(0, trips - 1) as i:
                            chain.open(i, per_links)
                            for jj in range(per):
                                split(i + 1 if jj == per - 1 else i, (jj + 1) % per)
                                take(eng, chain, i, jj)
                            chain.close(trips - 1)
                    for jj in range(per):
                        if jj < per - 1:
                            split(trips - 1, jj + 1)
                        take(eng, chain, trips - 1, jj)
                    chain.done()

                @block.scalar
                def _(act):
                    def split_hi(i, jj):
                        j = jj % 2
                        act.wait_ge(w_loaded[j].sem, (use(i, jj) + 1) * (16 * n_loads) + w_loaded[j].base)
                        act.wait_ge(mm_done[j].sem, use(i, jj) + mm_done[j].base)
                        act.copy(whi[:, j, 0:blocks, :], raw[:, j, 0:blocks, :]).then_inc(hi_ready[j].sem, 1)

                    pipelined(act, split_hi, act_out, Chain(act, act_chain), act_out.links)

                @block.vector
                def _(dve):
                    def split_lo(i, jj):
                        j = jj % 2
                        dve.wait_ge(hi_ready[j].sem, use(i, jj) + (hi_ready[j].base + 1))
                        dve.tensor_tensor(wlo[:, j, 0:blocks, :], raw[:, j, 0:blocks, :], whi[:, j, 0:blocks, :].bitcast(F32),
                                          ALU.subtract).then_inc(lo_ready[j].sem, 1)

                    pipelined(dve, split_lo, dve_out, Chain(dve, dve_chain), dve_out.links)
            for j in range(2):
                w_loaded[j].base += 16 * n_loads * chunks // 2
                for t in (hi_ready, lo_ready, mm_done, psum_free):
                    t[j].base += chunks // 2
            finish(act_chain, dve_chain)

        def links(n):
            def mark(f):
                f.links = n
                return f
            return mark

        @links(0)
        def nothing(eng, ch, i, jj):
            pass

        def tile(a, n, T=None):
            v = a[:, bass.ds(n, 1), :] if T is None else a[:, bass.ds(n, 1), 0:T]
            return v.rearrange("p a t -> p (a t)")

        def products(eng, i, jj, half):
            j = jj % 2
            eng.wait_ge(mm_done[j].sem, i * half + jj // 2 + (mm_done[j].base + 1))

        def project(ring, w, dst, first, chunks, T, col0=0, moving=None):
            wv = w.rearrange("(k p) c -> p k c", p=P)
            hi, lo = moving

            def loads(i, jj):
                return [(0, KT, wv[:, :, bass.ds(i * (2 * P) + (col0 + jj * P), P)])]

            @links(0)
            def act_out(act, ch, i, jj):
                products(act, i, jj, 1)
                b = 4 * BANK * jj
                act.copy(dst[:, bass.ds(i * 2 + (first + jj), 1), 0:T].rearrange("p a t -> p (a t)"), ps[:, b:b + T]).then_inc(psum_free[jj].sem, 1)

            dense(ring, chunks, 2, KT, loads, [(0, 0, KT, hi, lo)], T, act_out, nothing)

        def residual(ring, w, gate, chunks, moving, T, row0=0, nk=KT):
            wv = w[row0:row0 + nk * P, :].rearrange("(k p) c -> p k c", p=P)
            hi, lo = moving
            tg = groups(T)

            def loads(i, jj):
                return [(0, nk, wv[:, :, bass.ds(i * (2 * P) + jj * P, P)])]

            @links(0)
            def dve_out(dve, ch, i, jj):
                products(dve, i, jj, 1)
                b = 4 * BANK * jj
                for v, (t0, tn) in enumerate(tg):
                    xo = x[:, bass.ds(i * 2 + jj, 1), t0:t0 + tn].rearrange("p a t -> p (a t)")
                    m = dve.scalar_tensor_tensor(out=xo, in0=ps[:, b + t0:b + t0 + tn], scalar=mod[:, v, bass.ds(i * 2 + (gate + jj), 1)],
                                                 in1=xo, op0=ALU.mult, op1=ALU.add)
                m.then_inc(psum_free[jj].sem, 1)

            dense(ring, chunks, 2, nk, loads, [(0, 0, nk, hi, lo)], T, nothing, dve_out)

        def swiglu(ring, c, loads, per, tiles, moving, h, T, combine=None):
            hi, lo = moving
            hhi, hlo = h
            sg = sb(c, "sg", [P, T])
            hf = sb(c, "hf", [P, T])
            half = per // 2

            @links(0)
            def act_out(act, ch, i, jj):
                j, u = jj % 2, i * half + jj // 2
                if j == 0:
                    products(act, i, jj, half)
                    act.wait_ge(psum_free[1].sem, u + psum_free[1].base)
                    act.activation(sg[:], ps[:, 0:T], ACT.Silu).then_inc(psum_free[0].sem, 1)
                else:
                    act.wait_ge(ready.sem, u + (ready.base + 1))
                    act.copy(tile(hhi, u), hf[:]).then_inc(h_hi_ready.sem, 1)

            ready = psum_free[1] if combine is None else h_scaled

            @links(0)
            def dve_out(dve, ch, i, jj):
                j, u = jj % 2, i * half + jj // 2
                if j == 0:
                    return
                products(dve, i, jj, half)
                dve.wait_ge(psum_free[0].sem, u + (psum_free[0].base + 1))
                dve.tensor_tensor(hf[:], sg[:], ps[:, 4 * BANK:4 * BANK + T], ALU.mult).then_inc(psum_free[1].sem, 1)
                if combine is not None:
                    dve.wait_ge(psum_free[1].sem, u + (psum_free[1].base + 1))
                    dve.tensor_tensor(hf[:], hf[:], combine(i), ALU.mult).then_inc(h_scaled.sem, 1)
                dve.wait_ge(h_hi_ready.sem, u + (h_hi_ready.base + 1))
                dve.tensor_tensor(tile(hlo, u), hf[:], tile(hhi, u).bitcast(F32), ALU.subtract)

            dense(ring, 2 * tiles, per, KT, loads, [(0, 0, KT, hi, lo)], T, act_out, dve_out)
            if combine is not None:
                h_scaled.base += tiles
            h_hi_ready.base += tiles

        def new_ring(c, blocks):
            return (sb(c, "w_raw", [P, 2, blocks, P]), sb(c, "w_hi", [P, 2, blocks, P], F32R), sb(c, "w_lo", [P, 2, blocks, P], F32R))

        def gated_branch(ring, c, w_gate, w_branch, moving, yhl, proj, first, T):
            gv = w_gate.rearrange("(k p) c -> p k c", p=P)
            bv = w_branch.rearrange("(k p) c -> p k c", p=P)
            sg = sb(c, "sg", [P, 2, T])
            gp = sb(c, "gp", [P, 2, T])

            def loads(i, jj):
                cols = bass.ds(i * (2 * P) + jj * P, P)
                return [(0, KT, gv[:, :, cols]), (KT, 4, bv[:, :, cols])]

            @links(0)
            def act_out(act, ch, i, jj):
                products(act, i, jj, 1)
                act.wait_ge(psum_free[jj].sem, i + psum_free[jj].base)
                act.activation(sg[:, jj, :], ps[:, 4 * BANK * jj:4 * BANK * jj + T], ACT.Sigmoid).then_inc(gated.sem, 1)

            @links(0)
            def dve_out(dve, ch, i, jj):
                b = 4 * BANK * jj + 2 * BANK
                m = tile(proj, i * 2 + (T_M + jj), T)
                dve.wait_ge(gated.sem, i * 2 + (gated.base + jj + 1))
                dve.tensor_tensor(m if first else gp[:, jj, :], sg[:, jj, :], ps[:, b:b + T], ALU.mult).then_inc(psum_free[jj].sem, 1)
                if not first:
                    dve.wait_ge(psum_free[jj].sem, i + (psum_free[jj].base + 1))
                    dve.tensor_tensor(m, m, gp[:, jj, :], ALU.add)

            dense(ring, KT, 2, KT + 4, loads, [(0, 0, KT, *moving), (2 * BANK, KT, 4, *yhl)], T, act_out, dve_out)
            gated.base += KT

        def split(src, hi, lo, n, T):
            with ExitStack() as c:
                block = c.enter_context(nc.Block())

                @block.scalar
                def _(act):
                    for k in range(n):
                        act.copy(hi[:, k, 0:T], src[:, k, 0:T]).then_inc(act_chain.sem, 1)

                @block.vector
                def _(dve):
                    for k in range(n):
                        dve.wait_ge(act_chain.sem, act_chain.base + k + 1)
                        dve.tensor_tensor(lo[:, k, 0:T], src[:, k, 0:T], hi[:, k, 0:T].bitcast(F32), ALU.subtract)
            act_chain.base += n

        def fourier(proj, t0, T, seq, chan):
            nt = T // P
            with ExitStack() as c:
                dseq = sb(c, "dft_seq", [P, nt, 2, T])
                dch = sb(c, "dft_chan", [P, 2 * P])
                u = sb(c, "dft_u", [P, 4, nt, 2 * P])
                block = c.enter_context(nc.Block())

                @block.sync
                def _(sp):
                    sp.dma_start(dch[:], chan).then_inc(ld[0].sem, 16)
                    sp.dma_start(dseq[:], seq.rearrange("(k p) s n -> p k s n", p=P)).then_inc(ld[1].sem, 16)

                @block.tensor
                def _(pe):
                    def channels(gr):
                        if gr >= 2:
                            pe.wait_ge(act_chain.sem, act_chain.base + gr - 1)
                        for n in range(nt):
                            b = 2 * BANK * (gr % 2) + n * 2 * P
                            m = pe.matmul(ps[:, b:b + 2 * P], proj[:, T_F + gr, t0 + n * P:t0 + (n + 1) * P], dch[:], start=True, stop=True)
                        m.then_inc(pe_chain.sem, 1)

                    def tokens(gr):
                        pe.wait_ge(act_chain.sem, act_chain.base + gr + 1)
                        if gr >= 2:
                            pe.wait_ge(dve_chain.sem, dve_chain.base + gr - 1)
                        o = ps[:, BANK * (4 + gr % 2):BANK * (4 + gr % 2) + T]
                        for n in range(nt):
                            for s in range(2):
                                m = pe.matmul(o, u[:, gr, n, s * P:(s + 1) * P], dseq[:, n, s, :], start=(n + s == 0), stop=(n == nt - 1 and s == 1))
                        m.then_inc(norm_var.sem, 1)

                    pe.wait_ge(ld[0].sem, ld[0].base + 16)
                    channels(0)
                    pe.wait_ge(ld[1].sem, ld[1].base + 16)
                    for gr in range(4):
                        if gr < 3:
                            channels(gr + 1)
                        tokens(gr)

                @block.scalar
                def _(act):
                    for gr in range(4):
                        act.wait_ge(pe_chain.sem, pe_chain.base + gr + 1)
                        b = 2 * BANK * (gr % 2)
                        act.copy(u[:, gr].rearrange("p n c -> p (n c)"), ps[:, b:b + nt * 2 * P]).then_inc(act_chain.sem, 1)

                @block.vector
                def _(dve):
                    for gr in range(4):
                        dve.wait_ge(norm_var.sem, norm_var.base + gr + 1)
                        b = BANK * (4 + gr % 2)
                        dve.tensor_copy(proj[:, T_Y[0] + gr, t0:t0 + T], ps[:, b:b + T]).then_inc(dve_chain.sem, 1)
            for t in (pe_chain, act_chain, dve_chain, norm_var):
                t.base += 4
            ld[0].base += 16
            ld[1].base += 16

        def attend(c, pairs, q_tiles, spans, key_tiles, q_of, k_of, v_of, out_of, scale, prep,
                   look=2, bias=None, sink=None, v_need=None):
            NT = q_tiles
            width = max(len(key_tiles(t)) for t in range(NT))
            full = all(key_tiles(t) == key_tiles(0) for t in range(NT))
            prob = sb(c, "prob", [P, 2, width * P])
            probT = sb(c, "probT", [P, width, NT * P])
            nm = sb(c, "nm", [P, 2, 4])
            es = sb(c, "sink_e", [P, 2, 1])
            U = 2 * NT

            def unit(i, j, t):
                return i * U + (j * NT + t)

            def following(i, j, t, ahead):
                n = j * NT + t + ahead
                return (i, n // NT, n % NT) if n < U else (i + 1, (n - U) // NT, (n - U) % NT)

            def exists(i, j, t, ahead, last):
                return not (last and j * NT + t + ahead >= U)

            def scores_at(u_static):
                return 2 * BANK * (u_static % 2)

            def run(eng, who, prologue, step, end, chain, per):
                prologue()
                if pairs > 1:
                    with eng.Fori(0, pairs - 1) as i:
                        chain.open(i, per)
                        for j in range(2):
                            for t in range(NT):
                                step(i, j, t, False)
                        end(i)
                        chain.close(pairs - 1)
                for j in range(2):
                    for t in range(NT):
                        step(pairs - 1, j, t, True)
                end(pairs - 1)
                chain.done()

            def pe_program(pe, per=0):
                ch = Chain(pe, pe_chain)

                def scores(i, j, t, first=False):
                    if t == 0:
                        prep.ready(pe, i, j)
                    if not first:
                        pe.wait_ge(p_done.sem, unit(i, j, t) + (p_done.base - 1))
                    b = scores_at(j * NT + t)
                    for c0, cn, k0 in spans(t):
                        m = pe.matmul(ps[:, b + c0:b + c0 + cn], q_of(j, t), k_of(j, k0, cn), start=True, stop=True)
                    m.then_inc(s_done.sem, 1)

                def turn(i, j, t):
                    u = unit(i, j, t)
                    pe.wait_ge(pn_done.sem, u + (pn_done.base + 1))
                    pe.wait_ge(pt_done.sem, u + pt_done.base)
                    for b in range(len(key_tiles(t))):
                        m = pe.transpose(ps[:, 4 * BANK + b * P:4 * BANK + (b + 1) * P], prob[:, (j * NT + t) % 2, b * P:(b + 1) * P], ident[:])
                    m.then_inc(t_done.sem, 1)

                def values(i, j):
                    h = i * 2 + j
                    pe.wait_ge(pt_done.sem, i * U + (pt_done.base + (j + 1) * NT))
                    pe.wait_ge(o_done.sem, h + o_done.base)
                    prep.v_ready(pe, i, j)
                    o = ps[64 * j:64 * j + HD, 6 * BANK:6 * BANK + NT * P]
                    if full:
                        kts = key_tiles(0)
                        for b, kt in enumerate(kts):
                            m = pe.matmul(o, v_of(j, kt), probT[:, b, :], start=(b == 0), stop=(b == len(kts) - 1))
                    else:
                        for t in range(NT):
                            kts = key_tiles(t)
                            for b, kt in enumerate(kts):
                                m = pe.matmul(o[:, t * P:(t + 1) * P], v_of(j, kt), probT[:, b, t * P:(t + 1) * P], start=(b == 0), stop=(b == len(kts) - 1))
                    m.then_inc(pv_done.sem, 1)

                def prologue():
                    prep("pe", pe, ch, 0, 0, None)
                    for a in range(look):
                        scores(*following(0, 0, 0, a), first=True)

                def step(i, j, t, last):
                    if exists(i, j, NT - 1, 1, last):
                        prep("pe", pe, ch, *following(i, j, NT - 1, 1)[:2], t)
                    if exists(i, j, t, look, last):
                        scores(*following(i, j, t, look))
                    if j == 1 and t == 0:
                        values(i, 0)
                    turn(i, j, t)

                run(pe, "pe", prologue, step, lambda i: values(i, 1), ch, per)

            def dve_program(dve, per):
                ch = Chain(dve, dve_chain)

                def maximum(i, j, t):
                    u = unit(i, j, t)
                    dve.wait_ge(s_done.sem, u + (s_done.base + 1))
                    slot = (j * NT + t) % 2
                    n = len(key_tiles(t)) * P
                    s = ps[:, scores_at(slot):scores_at(slot) + n]
                    if bias:
                        bias.chain = ch
                        ch.link(bias(dve, i, j, t, s))
                    ch.link(dve.reduce_max(nm[:, slot, 0:1], s, AX))
                    if sink:
                        ch.link(dve.tensor_tensor(nm[:, slot, 0:1], nm[:, slot, 0:1], sink(i, j), ALU.max))
                    dve.tensor_scalar(nm[:, slot, 1:2], nm[:, slot, 0:1], -scale, None, ALU.mult).then_inc(nm_done.sem, 1)

                def normalised(i, j, t):
                    u = unit(i, j, t)
                    slot = (j * NT + t) % 2
                    n = len(key_tiles(t)) * P
                    dve.wait_ge(p_done.sem, u + (p_done.base + 1))
                    if sink:
                        ch.link(dve.tensor_tensor(nm[:, slot, 2:3], nm[:, slot, 2:3], es[:, slot, :], ALU.add))
                    ch.link(dve.reciprocal(nm[:, slot, 3:4], nm[:, slot, 2:3]))
                    dve.tensor_scalar(prob[:, slot, 0:n], prob[:, slot, 0:n], nm[:, slot, 3:4], None, ALU.mult).then_inc(pn_done.sem, 1)

                def output(i, j):
                    dve.wait_ge(pv_done.sem, i * 2 + (pv_done.base + j + 1))
                    dve.tensor_copy(out_of(i, j), ps[64 * j:64 * j + HD, 6 * BANK:6 * BANK + NT * P]).then_inc(o_done.sem, 1)

                def prologue():
                    prep("dve", dve, ch, 0, 0, None)
                    maximum(0, 0, 0)

                def step(i, j, t, last):
                    if exists(i, j, NT - 1, 1, last):
                        prep("dve", dve, ch, *following(i, j, NT - 1, 1)[:2], t)
                    if exists(i, j, t, 1, last):
                        maximum(*following(i, j, t, 1))
                    normalised(i, j, t)
                    if j == 1 and t == 0:
                        output(i, 0)

                run(dve, "dve", prologue, step, lambda i: output(i, 1), ch, per)

            def act_program(act, per=0):
                ch = Chain(act, act_chain)

                def exps(i, j, t, first=False):
                    u = unit(i, j, t)
                    slot = (j * NT + t) % 2
                    n = len(key_tiles(t)) * P
                    act.wait_ge(nm_done.sem, u + (nm_done.base + 1))
                    if not first:
                        act.wait_ge(t_done.sem, u + (t_done.base - 1))
                    if sink:
                        act.activation(es[:, slot, :], sink(i, j), ACT.Exp, bias=nm[:, slot, 1:2])
                    act.activation(prob[:, slot, 0:n], ps[:, scores_at(slot):scores_at(slot) + n], ACT.Exp, bias=nm[:, slot, 1:2],
                                   scale=scale, accum_out=nm[:, slot, 2:3]).then_inc(p_done.sem, 1)

                def copied(i, j, t):
                    u = unit(i, j, t)
                    nb = len(key_tiles(t))
                    act.wait_ge(t_done.sem, u + (t_done.base + 1))
                    if t == 0:
                        act.wait_ge(pv_done.sem, i * 2 + (pv_done.base + j))
                    act.copy(probT[:, 0:nb, t * P:(t + 1) * P], ps[:, 4 * BANK:4 * BANK + nb * P].rearrange("p (b n) -> p b n", n=P)).then_inc(pt_done.sem, 1)

                def prologue():
                    prep("act", act, ch, 0, 0, None)
                    exps(0, 0, 0, first=True)

                def step(i, j, t, last):
                    if exists(i, j, NT - 1, 1, last):
                        prep("act", act, ch, *following(i, j, NT - 1, 1)[:2], t)
                    if exists(i, j, t, 1, last):
                        exps(*following(i, j, t, 1))
                    copied(i, j, t)

                run(act, "act", prologue, step, lambda i: None, ch, per)

            def ended():
                for t in (s_done, nm_done, p_done, pn_done, t_done, pt_done):
                    t.base += pairs * U
                for t in (pv_done, o_done):
                    t.base += 2 * pairs
                for t in (pe_chain, dve_chain, act_chain):
                    finish(t)

            return pe_program, dve_program, act_program, ended

        class Staged:

            def __init__(self, qk, v, q_tiles):
                self.qk, self.v, self.q_tiles = qk, v, q_tiles

            def __call__(self, who, eng, ch, i, j, t):
                pass

            def ready(self, pe, i, j):
                pe.wait_ge(qk_staged.sem, i * (2 * len(self.qk)) + (qk_staged.base + (j + 1) * len(self.qk)))

            def v_ready(self, pe, i, j):
                if self.v:
                    pe.wait_ge(v_staged.sem, i * 2 + (v_staged.base + j + 1))

            def stage_qk(self, pool, i, j):
                n = len(self.qk)
                for a, f in enumerate(self.qk):
                    f(pool, i, j).then_inc(qk_staged.sem, 1)
                    pool.wait_ge(qk_staged.sem, i * (2 * n) + (qk_staged.base + j * n + a + 1))

            def stage_v(self, pool, i, j):
                self.v[0](pool, i, j).then_inc(v_staged.sem, 1)
                pool.wait_ge(v_staged.sem, i * 2 + (v_staged.base + j + 1))

            def program(self, pool, pairs):
                NT = self.q_tiles

                def stage(i, j, first):
                    if not first:
                        pool.wait_ge(s_done.sem, i * (2 * NT) + (s_done.base + (j - 1) * NT))
                    self.stage_qk(pool, i, j)
                    if self.v:
                        if not first:
                            pool.wait_ge(pv_done.sem, i * 2 + (pv_done.base + j - 1))
                        self.stage_v(pool, i, j)

                for j in range(2):
                    stage(0, j, True)
                if pairs > 1:
                    with pool.Fori(1, pairs) as i:
                        for j in range(2):
                            stage(i, j, False)

            def ended(self, pairs):
                qk_staged.base += 2 * pairs * len(self.qk)
                v_staged.base += 2 * pairs if self.v else 0

        def token_major(proj, first, n, T, dst):
            nt = T // P
            with ExitStack() as c:
                block = c.enter_context(nc.Block())

                @block.tensor
                def _(pe):
                    for t in range(nt):
                        if t >= 4:
                            pe.wait_ge(act_chain.sem, act_chain.base + t - 3)
                        for k in range(n):
                            b = BANK * (t % 4) + k * P
                            m = pe.transpose(ps[:, b:b + P], proj[:, first + k, t * P:(t + 1) * P], ident[:])
                        m.then_inc(pe_chain.sem, 1)

                @block.scalar
                def _(act):
                    for t in range(nt):
                        act.wait_ge(pe_chain.sem, pe_chain.base + t + 1)
                        act.copy(dst[:, t, :], ps[:, BANK * (t % 4):BANK * (t % 4) + n * P]).then_inc(act_chain.sem, 1)
            pe_chain.base += nt
            act_chain.base += nt

        def neighbourhood(proj, l, with_ctx):
            with ExitStack() as c:
                vt = sb(c, "na_v", [P, 6, NA_W])
                token_major(proj, T_NV, 4, ALL, vt)
                qs = sb(c, "na_qs", [P, 2, LAT])
                ks = sb(c, "na_ks", [P, 2, ALL])
                vs = sb(c, "na_vs", [P, 2, 6, HD])
                bt = sb(c, "na_bias", [P, 2, 14, GRID_W])
                mask = sb(c, "na_mask", [P, GRID_W])
                rpb = sb(c, "na_rpb", [HEADS * 15, P])
                table = nc.dram_tensor(f"rpb_rows_{l}", [HEADS, 15, GRID_W, P], F32)
                with ExitStack() as c1:
                    block = c1.enter_context(nc.Block())

                    @block.vector
                    def _(dve):
                        dve.memset(rpb[:], 0.0).then_inc(dve_chain.sem, 1)

                    @block.sync
                    def _(sp):
                        sp.dma_start(mask[:], g["k_na_mask"]).then_inc(ld[0].sem, 16)
                        sp.wait_ge(dve_chain.sem, dve_chain.base + 1)
                        sp.dma_start(rpb[:, 48:79], g["na_rpb"][l].rearrange("h r c -> (h r) c")).then_inc(ld[1].sem, 16)
                        sp.wait_ge(ld[1].sem, ld[1].base + 16)
                        sp.dma_start(table[:].rearrange("h r w c -> (h r) w c"), rpb[:].unsqueeze(1).to_broadcast([HEADS * 15, GRID_W, P])).then_inc(ld[2].sem, 16)
                        sp.wait_ge(ld[2].sem, ld[2].base + 16)
                        sp.wait_ge(ld[0].sem, ld[0].base + 16)
                dve_chain.base += 1
                for n in range(3):
                    ld[n].base += 16

                def half(a, j):
                    return a[64 * j:64 * j + HD]

                def stage_q(tok, n):
                    return lambda pool, i, j: pool.tensor_tensor(half(qs, j)[:, j, 0:n], tile(half(proj, j), i + T_NQ)[:, tok:tok + n],
                                                                 half(scale_row, j).to_broadcast([HD, n]), ALU.mult)

                def stage_k(tok, n):
                    return lambda pool, i, j: pool.tensor_copy(half(ks, j)[:, j, 0:n], tile(half(proj, j), i + T_NK)[:, tok:tok + n])

                def stage_v(kt0, n):
                    return lambda pool, i, j: pool.tensor_copy(vs[:, j, 0:n, :], vt[:, kt0:kt0 + n, bass.ds(i * P + j * HD, HD)])

                def q_of(j, t):
                    return half(qs, j)[:, j, t * P:(t + 1) * P]

                def k_of(j, k0, n):
                    return half(ks, j)[:, j, k0:k0 + n]

                v_of = lambda j, kt: vs[:, j, kt, :]

                with ExitStack() as c1:
                    def bias(dve, i, j, t, s):
                        if t == 0:
                            dve.wait_ge(bias_masked.sem, i * 2 + (bias_masked.base + j + 1))
                        e = ROWS - 2 - 2 * t
                        return dve.tensor_tensor(s[:, 0:LAT], s[:, 0:LAT], bt[:, j, e:e + KH, :].rearrange("p r w -> p (r w)"), ALU.add)

                    prep = Staged([stage_q(0, LAT), stage_k(0, ALL)], [stage_v(0, 6)], 4)
                    pe_p, dve_p, act_p, ended = attend(
                        c1, 4, 4, lambda t: [(0, LAT, 0), (LAT, CTX, LAT)], lambda t: list(range(6)), q_of, k_of, v_of,
                        lambda i, j: tile(half(proj, j), i + T_Y[1], LAT), 1.0, prep, bias=bias)
                    block = c1.enter_context(nc.Block())

                    @block.sync
                    def _(sp):
                        def load(i, j, first):
                            if not first:
                                sp.wait_ge(nm_done.sem, i * 8 + (nm_done.base + (j - 1) * 4))
                            for r in range(2):
                                R = GRID_W * P
                                src = bass.AP(tensor=table, offset=i * (2 * 15 * R) + (j * 15 * R + (1 - r) * R + GRID_W - 1),
                                              ap=[[P - 1, GRID_W], [R, 14], [1, GRID_W]])
                                sp.dma_start(bt[64 * r:64 * r + 64, j], src).then_inc(head_w[j].sem, 16)

                        for j in range(2):
                            load(0, j, True)
                        with sp.Fori(1, 4) as i:
                            for j in range(2):
                                load(i, j, False)

                    @block.gpsimd
                    def _(pool):
                        NT = 4

                        def one(i, j, first):
                            if not first:
                                pool.wait_ge(s_done.sem, i * (2 * NT) + (s_done.base + (j - 1) * NT))
                            prep.stage_qk(pool, i, j)
                            pool.wait_ge(head_w[j].sem, i * 32 + (head_w[j].base + 32))
                            pool.tensor_tensor(bt[:, j], bt[:, j], mask[:].unsqueeze(1).to_broadcast([P, 14, GRID_W]), ALU.add).then_inc(bias_masked.sem, 1)
                            pool.wait_ge(bias_masked.sem, i * 2 + (bias_masked.base + j + 1))
                            if not first:
                                pool.wait_ge(pv_done.sem, i * 2 + (pv_done.base + j - 1))
                            prep.stage_v(pool, i, j)

                        for j in range(2):
                            one(0, j, True)
                        with pool.Fori(1, 4) as i:
                            for j in range(2):
                                one(i, j, False)

                    @block.tensor
                    def _(pe):
                        pe_p(pe)

                    @block.vector
                    def _(dve):
                        dve_p(dve, 8 * 3)

                    @block.scalar
                    def _(act):
                        act_p(act)
                ended()
                prep.ended(4)
                bias_masked.base += 8
                for j in range(2):
                    head_w[j].base += 4 * 32

                if with_ctx:
                    with ExitStack() as c1:
                        prep = Staged([stage_q(LAT, CTX), stage_k(LAT, CTX)], [stage_v(4, 2)], 2)
                        pe_p, dve_p, act_p, ended = attend(
                            c1, 4, 2, lambda t: [(0, CTX, 0)], lambda t: [0, 1], q_of, k_of, v_of,
                            lambda i, j: tile(half(proj, j), i + T_Y[1])[:, LAT:ALL], 1.0, prep, look=1)
                        simple_attention(c1, prep, 4, pe_p, dve_p, act_p, 4 * 2)
                    ended()
                    prep.ended(4)

        def simple_attention(c1, prep, pairs, pe_p, dve_p, act_p, per):
            block = c1.enter_context(nc.Block())

            @block.gpsimd
            def _(pool):
                prep.program(pool, pairs)

            @block.tensor
            def _(pe):
                pe_p(pe)

            @block.vector
            def _(dve):
                dve_p(dve, per)

            @block.scalar
            def _(act):
                act_p(act)

        class Latent:

            def __init__(self, pieces, at):
                self.pieces, self.at = pieces, at

            def which(self, t):
                return range(len(self.pieces)) if t is None else [n for n, a in enumerate(self.at) if a == t]

            def __call__(self, who, eng, ch, i, j, t):
                n = len(self.pieces)
                for p in self.which(t):
                    mm, on, copies = self.pieces[p]
                    before = i * (2 * n) + (j * n + p)
                    if who == "pe":
                        if p == 0:
                            eng.wait_ge(head_w[j].sem, i * 96 + (head_w[j].base + 96))
                        eng.wait_ge(prep_out.sem, before + prep_out.base)
                        mm(eng, j).then_inc(prep_mm.sem, 1)
                    elif who == on:
                        eng.wait_ge(prep_mm.sem, before + (prep_mm.base + 1))
                        copies(eng, ch, j)

            def ready(self, pe, i, j):
                n = len(self.pieces)
                pe.wait_ge(prep_out.sem, i * (2 * n) + (prep_out.base + (j + 1) * n - 1))
                pe.wait_ge(prep_rope.sem, i * 2 + (prep_rope.base + j + 1))

            def v_ready(self, pe, i, j):
                n = len(self.pieces)
                pe.wait_ge(prep_out.sem, i * (2 * n) + (prep_out.base + (j + 1) * n))

        def latent_attention(proj, l, with_ctx):
            with ExitStack() as c:
                gain = vec3
                T = ALL if with_ctx else LAT
                normalize([proj[:, T_CQ + k, 0:T] for k in range(2)], T, LN_EPS, lambda k: col(gain, V3_QN + 2 * l + k))
                normalize([proj[:, T_CKV, :]], ALL, LN_EPS, lambda k: col(gain, V3_KVN + l))
                wq = sb(c, "mla_wq", [P, 2, 2, P])
                wk = sb(c, "mla_wk", [P, 2, HD])
                wv = sb(c, "mla_wv", [P, 2, HD])
                q = sb(c, "mla_q", [P, 2, LAT])
                k = sb(c, "mla_k", [P, 2, ALL])
                v = sb(c, "mla_v", [P, 2, 6, HD])
                ra = sb(c, "mla_ra", [P, LAT])
                rb = sb(c, "mla_rb", [P, LAT])
                rope = sb(c, "mla_rope", [P, LAT])
                spread = sb(c, "mla_spread", [ROPE, P])
                R0, R1, R2 = HD, HD + ROPE, HD + 2 * ROPE

                with ExitStack() as c1:
                    block = c1.enter_context(nc.Block())

                    @block.sync
                    def _(sp):
                        sp.dma_start(rope[:], g["k_rope"]).then_inc(ld[0].sem, 16)
                        sp.dma_start(spread[:], g["k_spread"]).then_inc(ld[1].sem, 16)

                    @block.tensor
                    def _(pe):
                        pe.wait_ge(ld[1].sem, ld[1].base + 16)
                        for t0, tn in groups(ALL):
                            m = pe.matmul(ps[:, t0:t0 + tn], spread[:], proj[0:ROPE, T_KR, t0:t0 + tn], start=True, stop=True)
                        m.then_inc(pe_chain.sem, 1)

                    @block.vector
                    def _(dve):
                        ch = Chain(dve, dve_chain)
                        dve.wait_ge(pe_chain.sem, pe_chain.base + 1)
                        dve.wait_ge(ld[0].sem, ld[0].base + 16)
                        dve.tensor_tensor(ra[R0:R1, :], ps[R0:R1, 0:LAT], rope[R0:R1, :], ALU.mult)
                        ch.link(dve.tensor_tensor(rb[R0:R1, :], ps[R1:R2, 0:LAT], rope[R1:R2, :], ALU.mult))
                        for j in range(2):
                            dve.tensor_tensor(k[R0:R1, j, 0:LAT], ra[R0:R1, :], rb[R0:R1, :], ALU.add)
                            dve.tensor_copy(k[R0:R1, j, LAT:ALL], ps[R0:R1, LAT:ALL])
                        ch.done()
                finish(dve_chain)
                pe_chain.base += 1
                ld[0].base += 16
                ld[1].base += 16

                bank = 7 * BANK

                def run(q_tiles, tok, nk, kt0, rotate, pieces, at, look, links_per_prep, out_of):
                    prep = Latent(pieces, at)
                    with ExitStack() as c1:
                        pe_p, dve_p, act_p, ended = attend(
                            c1, 4, q_tiles,
                            (lambda t: [(0, LAT, 0), (LAT, CTX, LAT)]) if nk == ALL else (lambda t: [(0, CTX, LAT)]),
                            lambda t: list(range(nk // P)), lambda j, t: q[0:MLA_K, j, t * P:(t + 1) * P],
                            lambda j, k0, n: k[0:MLA_K, j, k0:k0 + n], lambda j, kt: v[:, j, kt, :],
                            out_of, MLA_SCALE, prep, look=look)
                        block = c1.enter_context(nc.Block())

                        @block.sync
                        def _(sp):
                            uq = g["w_uq"][l].rearrange("(k p) c -> p k c", p=P)
                            qr = g["w_qr"][l].rearrange("(k p) c -> p k c", p=P)

                            def load(i, j, first):
                                if not first:
                                    sp.wait_ge(prep_mm.sem, i * (2 * len(pieces)) + (prep_mm.base + (j - 1) * len(pieces)))
                                s = head_w[j].sem
                                h64 = lambda o, n: bass.ds(i * P + (j * HD + o), n)
                                h32 = lambda o, n: bass.ds(i * (2 * ROPE) + (j * ROPE + o), n)
                                sp.dma_start(wq[:, j, :, 0:R0], uq[:, :, h64(0, HD)]).then_inc(s, 16)
                                sp.dma_start(wq[:, j, :, R0:R1], qr[:, :, h32(0, ROPE)]).then_inc(s, 16)
                                sp.dma_start(wq[:, j, :, R1:R1 + 16], qr[:, :, h32(16, 16)]).then_inc(s, 16)
                                sp.dma_start(wq[:, j, :, R1 + 16:R2], qr[:, :, h32(0, 16)]).then_inc(s, 16)
                                sp.dma_start(wk[:, j, :], g["w_uk"][l][:, h64(0, HD)]).then_inc(s, 16)
                                sp.dma_start(wv[:, j, :], g["w_uv"][l][:, h64(0, HD)]).then_inc(s, 16)

                            for j in range(2):
                                load(0, j, True)
                            with sp.Fori(1, 4) as i:
                                for j in range(2):
                                    load(i, j, False)

                        @block.tensor
                        def _(pe):
                            pe_p(pe)

                        @block.vector
                        def _(dve):
                            dve_p(dve, 2 * q_tiles * 2 + 2 * links_per_prep)

                        @block.scalar
                        def _(act):
                            act_p(act)
                    ended()
                    prep_out.base += 8 * len(pieces)
                    prep_mm.base += 8 * len(pieces)
                    prep_rope.base += 8
                    for j in range(2):
                        head_w[j].base += 4 * 96

                def mm_q(tok, n):
                    def f(pe, j):
                        for kk in range(2):
                            m = pe.matmul(ps[:, bank:bank + n], wq[:, j, kk, :], proj[:, T_CQ + kk, tok:tok + n], start=(kk == 0), stop=(kk == 1))
                        return m
                    return f

                def mm_k(tok, n):
                    return lambda pe, j: pe.matmul(ps[0:HD, bank:bank + n], wk[:, j, :], proj[:, T_CKV, tok:tok + n], start=True, stop=True)

                def mm_v(tok, n):
                    def f(pe, j):
                        for t in range(n):
                            m = pe.matmul(ps[:, bank + t * HD:bank + (t + 1) * HD], proj[:, T_CKV, tok + t * P:tok + (t + 1) * P], wv[:, j, :], start=True, stop=True)
                        return m
                    return f

                def out_q_rotated(dve, ch, j):
                    dve.tensor_copy(q[0:HD, j, :], ps[0:HD, bank:bank + LAT])
                    dve.tensor_tensor(ra[R0:R1, :], ps[R0:R1, bank:bank + LAT], rope[R0:R1, :], ALU.mult)
                    ch.link(dve.tensor_tensor(rb[R0:R1, :], ps[R1:R2, bank:bank + LAT], rope[R1:R2, :], ALU.mult))
                    dve.sem_inc(prep_out.sem, 1)
                    dve.tensor_tensor(q[R0:R1, j, :], ra[R0:R1, :], rb[R0:R1, :], ALU.add).then_inc(prep_rope.sem, 1)

                def out_q_plain(dve, ch, j):
                    ch.link(dve.tensor_copy(q[0:MLA_K, j, 0:CTX], ps[0:MLA_K, bank:bank + CTX]))
                    dve.sem_inc(prep_out.sem, 1)
                    dve.sem_inc(prep_rope.sem, 1)

                def out_k(tok, n):
                    return lambda act, ch, j: act.copy(k[0:HD, j, tok:tok + n], ps[0:HD, bank:bank + n]).then_inc(prep_out.sem, 1)

                def out_v(n):
                    return lambda act, ch, j: act.copy(v[:, j, 0:n, :].rearrange("p t d -> p (t d)"), ps[:, bank:bank + n * HD]).then_inc(prep_out.sem, 1)

                def half(a, j):
                    return a[64 * j:64 * j + HD]

                run(4, 0, ALL, 0, True,
                    [(mm_q(0, LAT), "dve", out_q_rotated), (mm_k(0, LAT), "act", out_k(0, LAT)), (mm_k(LAT, CTX), "act", out_k(LAT, CTX)), (mm_v(0, 6), "act", out_v(6))],
                    (0, 0, 1, 1), 2, 1, lambda i, j: tile(half(proj, j), i + T_Y[2], LAT))
                if with_ctx:
                    run(2, LAT, CTX, 4, False,
                        [(mm_q(LAT, CTX), "dve", out_q_plain), (mm_k(LAT, CTX), "act", out_k(LAT, CTX)), (mm_v(LAT, 2), "act", out_v(2))],
                        (0, 0, 1), 1, 1, lambda i, j: tile(half(proj, j), i + T_Y[2])[:, LAT:ALL])

        def modulate_by(s):
            return (lambda v, k: mod[:, v, (s + 1) * KT + k:(s + 1) * KT + k + 1]), (lambda v, k: mod[:, v, s * KT + k:s * KT + k + 1])

        def xt(T):
            return [x[:, k, 0:T] for k in range(KT)]

        def layer(l, ahi, alo):
            last = l == DEPTH - 1
            T = LAT if last else ALL
            w_in = g["w_in"][l]
            with ExitStack() as c:
                proj = sb(c, "proj", [P, 20, ALL])
                with ExitStack() as c1:
                    ring = new_ring(c1, KT)
                    for first, n, t in ((T_F, 8, T), (T_NK, 8, ALL), (T_CQ, 2, T), (T_CKV, 2, ALL)):
                        project(ring, w_in, proj, first, n, t, first * P, (ahi, alo))
                fourier(proj, 0, LAT, g["k_dft_lat"], g["k_dft_chan"])
                if not last:
                    fourier(proj, LAT, CTX, g["k_dft_ctx"], g["k_dft_chan"])
                neighbourhood(proj, l, not last)
                latent_attention(proj, l, not last)
                with ExitStack() as c1:
                    ring = new_ring(c1, KT + 4)
                    yhi = sb(c1, "yhi", [P, 4, T], F32R)
                    ylo = sb(c1, "ylo", [P, 4, T], F32R)
                    for b in range(3):
                        split(proj[:, T_Y[b]:T_Y[b] + 4, :], yhi, ylo, 4, T)
                        with ExitStack() as c2:
                            gated_branch(ring, c2, w_in[:, GATE_COL + b * D:GATE_COL + (b + 1) * D], g["w_branch"][l, b], (ahi, alo), (yhi, ylo),
                                         proj, b == 0, T)
                with ExitStack() as c1:
                    split(proj[:, T_M:T_M + KT, :], ahi, alo, KT, T)
                    ring = new_ring(c1, KT)
                    residual(ring, g["w_out"][l], 2 * KT, KT, (ahi, alo), T)
            g1, b1 = V_LN1_G + l * KT, V_LN1_B + l * KT
            normalize(xt(T), T, LN_EPS, lambda k: col(vec1, g1 + k), lambda k: col(vec1, b1 + k), center=True,
                      post=(ahi, alo, *modulate_by(3)), after=ALPHA)
            NH = FFN // P // 2
            with ExitStack() as c:
                ring = new_ring(c, NH)
                hhi = sb(c, "hhi", [P, NH, T], F32R)
                hlo = sb(c, "hlo", [P, NH, T], F32R)
                for half in range(2):
                    views = [g[n][l].rearrange("(k p) c -> p k c", p=P) for n in ("w_ffn_gate", "w_ffn_up")]
                    with ExitStack() as c1:
                        swiglu(ring, c1, lambda i, jj: [(0, KT, views[jj][:, :, bass.ds(i * P + half * NH * P, P)])], 2, NH,
                               (ahi, alo), (hhi, hlo), T)
                    residual(ring, g["w_ffn_down"][l], 5 * KT, KT, (hhi, hlo), T, row0=half * NH * P, nk=NH)
            if not last:
                modulation(g["w_mod"][l + 1], (0, 1), vec2[:, (l + 1) * 48:(l + 2) * 48], 2)
            g2, b2 = V_LN2_G + l * KT, V_LN2_B + l * KT
            normalize(xt(T), T, LN_EPS, lambda k: col(vec1, g2 + k), lambda k: col(vec1, b2 + k), center=True,
                      post=None if last else (ahi, alo, *modulate_by(0)), after=ALPHA)


        def narrow(c, name, sources, n, ahi, alo):
            o = sb(c, name, [P, 4, n])
            with ExitStack() as c1:
                w = sb(c1, "nw", [P, KT, n])
                whi = sb(c1, "nw_hi", [P, KT, n], F32R)
                wlo = sb(c1, "nw_lo", [P, KT, n], F32R)
                block = c1.enter_context(nc.Block())

                @block.sync
                def _(sp):
                    at = 0
                    for src, m in sources:
                        sp.dma_start(w[:, :, at:at + m], src.rearrange("(k p) c -> p k c", p=P)).then_inc(ld[0].sem, 16)
                        at += m

                @block.scalar
                def _(act):
                    act.wait_ge(ld[0].sem, ld[0].base + 16 * len(sources))
                    act.copy(whi[:], w[:]).then_inc(act_chain.sem, 1)

                @block.vector
                def _(dve):
                    dve.wait_ge(act_chain.sem, act_chain.base + 1)
                    dve.tensor_tensor(wlo[:], w[:], whi[:].bitcast(F32), ALU.subtract).then_inc(dve_chain.sem, 1)
                    dve.wait_ge(pe_chain.sem, pe_chain.base + 1)
                    dve.tensor_copy(o[:], ps[:, 0:4 * n].rearrange("p (t n) -> p t n", n=n))

                @block.tensor
                def _(pe):
                    pe.wait_ge(dve_chain.sem, dve_chain.base + 1)
                    for t in range(4):
                        for k in range(KT):
                            tok = slice(t * P, (t + 1) * P)
                            out_ = ps[:, t * n:(t + 1) * n]
                            pe.matmul(out_, ahi[:, k, tok], whi[:, k, :], start=(k == 0), stop=False)
                            pe.matmul(out_, alo[:, k, tok], whi[:, k, :], start=False, stop=False)
                            m = pe.matmul(out_, ahi[:, k, tok], wlo[:, k, :], start=False, stop=(k == KT - 1))
                    m.then_inc(pe_chain.sem, 1)
            ld[0].base += 16 * len(sources)
            for t in (act_chain, dve_chain, pe_chain):
                t.base += 1
            return o

        def softplus_neg(c, n, load):
            dst = sb(c, "softplus", [P, n])
            with ExitStack() as c1:
                neg, e, z, z2, acc = (sb(c1, s, [P, n]) for s in ("sp_neg", "sp_e", "sp_z", "sp_z2", "sp_acc"))
                block = c1.enter_context(nc.Block())

                @block.vector
                def _(dve):
                    ch = Chain(dve, dve_chain)
                    load(dve, ch, neg)
                    ch.link(dve.tensor_scalar(z[:], neg[:], -1.0, None, ALU.mult))
                    ch.link(dve.tensor_tensor(e[:], neg[:], z[:], ALU.min))
                    pe_n = ch.value()
                    dve.wait_ge(act_chain.sem, act_chain.base + 1)
                    ch.link(dve.tensor_scalar(z2[:], e[:], 2.0, None, ALU.add))
                    ch.link(dve.reciprocal(z2[:], z2[:]))
                    ch.link(dve.tensor_tensor(z[:], e[:], z2[:], ALU.mult))
                    ch.link(dve.tensor_tensor(z2[:], z[:], z[:], ALU.mult))
                    ch.link(dve.tensor_scalar(acc[:], z2[:], 1.0 / 17, 1.0 / 15, ALU.mult, ALU.add))
                    for d in (13, 11, 9, 7, 5, 3, 1):
                        ch.link(dve.tensor_tensor(acc[:], acc[:], z2[:], ALU.mult))
                        ch.link(dve.tensor_scalar(acc[:], acc[:], 1.0 / d, None, ALU.add))
                    ch.link(dve.tensor_tensor(acc[:], acc[:], z[:], ALU.mult))
                    ch.link(dve.tensor_scalar(neg[:], neg[:], 0.0, None, ALU.max))
                    ch.mark(dve.scalar_tensor_tensor(out=dst[:], in0=acc[:], scalar=2.0, in1=neg[:], op0=ALU.mult, op1=ALU.add))
                    ch.done()
                    softplus_neg.at = pe_n

                @block.scalar
                def _(act):
                    act.wait_ge(dve_chain.sem, softplus_neg.at)
                    act.activation(e[:], e[:], ACT.Exp).then_inc(act_chain.sem, 1)
            finish(dve_chain)
            act_chain.base += 1
            return dst

        def banded_attention(proj):
            with ExitStack() as c:
                vt = sb(c, "swa_v", [P, 4, P])
                token_major(proj, S_VA, 1, LAT, vt)
                kd = sb(c, "swa_k", [P, 2, LAT])
                qs = sb(c, "swa_q", [P, 2, LAT])
                bt = sb(c, "swa_bias", [P, SWA_H, 2 * P])
                sinks = sb(c, "swa_sinks", [P, SWA_H])
                with ExitStack() as c1:
                    block = c1.enter_context(nc.Block())

                    @block.sync
                    def _(sp):
                        sp.dma_start(bt[:], g["k_swa"]).then_inc(ld[0].sem, 16)
                        sp.dma_start(sinks[:], g["sinks_2"][0].partition_broadcast(P)).then_inc(ld[1].sem, 16)
                        sp.wait_ge(ld[0].sem, ld[0].base + 16)
                        sp.wait_ge(ld[1].sem, ld[1].base + 16)

                    @block.vector
                    def _(dve):
                        for kv in range(2):
                            for j in range(2):
                                dve.tensor_copy(kd[64 * j:64 * j + HD, kv, :], proj[64 * kv:64 * kv + HD, S_KA, 0:LAT])
                ld[0].base += 16
                ld[1].base += 16

                def half(a, j):
                    return a[64 * j:64 * j + HD]

                for kv in range(2):
                    with ExitStack() as c1:
                        def bias(dve, i, j, t, s):
                            h = bass.ds(i * 2 + (4 * kv + j), 1)
                            b = bt[:, h, P:2 * P] if t == 0 else bt[:, h, :]
                            return dve.tensor_tensor(s, s, b.rearrange("p a n -> p (a n)"), ALU.add)

                        prep = Staged([lambda pool, i, j: pool.tensor_tensor(half(qs, j)[:, j, :], tile(half(proj, j), i + (S_QA + 2 * kv)),
                                                                             half(scale_row, j).to_broadcast([HD, LAT]), ALU.mult)], [], 4)
                        pe_p, dve_p, act_p, ended = attend(
                            c1, 2, 4, lambda t: [(0, P, 0)] if t == 0 else [(0, 2 * P, (t - 1) * P)],
                            lambda t: [0] if t == 0 else [t - 1, t],
                            lambda j, t: half(qs, j)[:, j, t * P:(t + 1) * P], lambda j, k0, n: half(kd, j)[:, kv, k0:k0 + n],
                            lambda j, kt: vt[:, kt, kv * HD:(kv + 1) * HD],
                            lambda i, j: tile(half(proj, j), i + (S_QA + 2 * kv)), 1.0, prep, bias=bias,
                            sink=lambda i, j: sinks[:, bass.ds(i * 2 + (4 * kv + j), 1)])
                        simple_attention(c1, prep, 2, pe_p, dve_p, act_p, 8 * 5)
                    ended()
                    prep.ended(2)

        def recurrence(proj):
            with ExitStack() as c:
                def load(dve, ch, neg):
                    ch.link(dve.tensor_scalar(neg[:], vec3[:, V3_LAM:V3_LAM + 2], -1.0, None, ALU.mult))

                sp_lam = softplus_neg(c, 2, load)
                wbd = sb(c, "lru_w", [P, 2, 2, P])
                xc, r, ig, a0, a1, tmp = (sb(c, s, [P, 2, LAT]) for s in ("lru_x", "lru_r", "lru_i", "lru_a0", "lru_a1", "lru_tmp"))
                sc = sb(c, "lru_sc", [P, 4])
                block = c.enter_context(nc.Block())
                c0, d0, a_0 = pe_chain.base, dve_chain.base, act_chain.base
                at = {}

                @block.vector
                def _(dve):
                    ch = Chain(dve, dve_chain)
                    ch.mark(dve.memset(wbd[:], 0.0))
                    ch.mark(dve.tensor_scalar(sc[:, 0:2], sp_lam[:], -8.0, None, ALU.mult))
                    ch.link(dve.tensor_scalar(sc[:, 2:4], sp_lam[:], 8.0, None, ALU.mult))
                    at["scales"] = ch.value()
                    for k in range(2):
                        xb = proj[:, S_XB + k, :]
                        w = lambda s: col(vec3, V3_CONVW + 2 * s + k)
                        ch.link(dve.tensor_scalar(xc[:, k, :], xb[:, 0:LAT], w(3), col(vec3, V3_CONVB + k), ALU.mult, ALU.add))
                        for d in (1, 2, 3):
                            ch.link(dve.scalar_tensor_tensor(out=xc[:, k, d:], in0=xb[:, 0:LAT - d], scalar=w(3 - d), in1=xc[:, k, d:],
                                                             op0=ALU.mult, op1=ALU.add))
                    at["conv"] = ch.value()
                    dve.wait_ge(act_chain.sem, a_0 + 6 + 2)
                    ch.link(dve.tensor_tensor(ig[:], ig[:], xc[:], ALU.mult))
                    ch.link(dve.tensor_scalar(a1[:], tmp[:], 1.0, None, ALU.add))
                    ch.link(dve.reciprocal(a1[:], a1[:]))
                    ch.link(dve.scalar_tensor_tensor(out=tmp[:], in0=tmp[:], scalar=2.0, in1=a1[:], op0=ALU.mult, op1=ALU.mult))
                    at["square"] = ch.value()
                    dve.wait_ge(act_chain.sem, a_0 + 9)
                    h = xc
                    ch.link(dve.tensor_tensor(h[:], tmp[:], ig[:], ALU.mult))
                    a, b, d = a0, a1, 1
                    while d < LAT:
                        ch.link(dve.tensor_tensor(tmp[:, :, d:], a[:, :, d:], h[:, :, 0:LAT - d], ALU.mult))
                        if 2 * d < LAT:
                            ch.mark(dve.tensor_tensor(b[:, :, d:], a[:, :, d:], a[:, :, 0:LAT - d], ALU.mult))
                        ch.link(dve.tensor_tensor(h[:, :, d:], h[:, :, d:], tmp[:, :, d:], ALU.add))
                        a, b, d = b, a, 2 * d
                    gb = proj[:, S_GB:S_GB + 2, 0:LAT]
                    ch.link(dve.tensor_tensor(r[:], gb, gb, ALU.mult))
                    ch.link(dve.tensor_scalar(r[:], r[:], 0.044715, 1.0, ALU.mult, ALU.add))
                    ch.link(dve.tensor_tensor(r[:], r[:], gb, ALU.mult))
                    at["gelu"] = ch.value()
                    dve.wait_ge(act_chain.sem, a_0 + 10)
                    ch.link(dve.tensor_scalar(r[:], r[:], 0.5, 0.5, ALU.mult, ALU.add))
                    ch.link(dve.tensor_tensor(r[:], r[:], gb, ALU.mult))
                    ch.mark(dve.tensor_tensor(proj[:, 4:6, 0:LAT], h[:], r[:], ALU.mult))
                    ch.done()

                @block.sync
                def _(sp):
                    sp.wait_ge(dve_chain.sem, d0 + 1)
                    for s, name in enumerate(("lru_wa_2", "lru_wx_2")):
                        for n in range(8):
                            q = 32 * (n % 4)
                            sp.dma_start(wbd[q:q + 32, s, n // 4, q:q + 32], g[name][0, n]).then_inc(ld[0].sem, 16)

                @block.tensor
                def _(pe):
                    pe.wait_ge(ld[0].sem, ld[0].base + 256)
                    pe.wait_ge(dve_chain.sem, at["conv"])
                    for s in range(2):
                        for k in range(2):
                            pe.matmul(ps[:, BANK * (2 * s + k):BANK * (2 * s + k) + LAT], wbd[:, s, k, :], xc[:, k, :],
                                      start=True, stop=True).then_inc(pe_chain.sem, 1)

                @block.scalar
                def _(act):
                    n = 0
                    for s, dst, b in ((0, r, V3_BA), (1, ig, V3_BX)):
                        for k in range(2):
                            act.wait_ge(pe_chain.sem, c0 + n + 1)
                            act.activation(dst[:, k, :], ps[:, BANK * n:BANK * n + LAT], ACT.Sigmoid, bias=col(vec3, b + k)).then_inc(act_chain.sem, 1)
                            n += 1
                    act.wait_ge(act_chain.sem, a_0 + 4)
                    act.wait_ge(dve_chain.sem, at["scales"])
                    for k in range(2):
                        act.activation(a0[:, k, :], r[:, k, :], ACT.Exp, scale=sc[:, k:k + 1]).then_inc(act_chain.sem, 1)
                    for k in range(2):
                        act.activation(tmp[:, k, :], r[:, k, :], ACT.Tanh, scale=sc[:, 2 + k:3 + k]).then_inc(act_chain.sem, 1)
                    act.wait_ge(dve_chain.sem, at["square"])
                    act.activation(tmp[:], tmp[:], ACT.Sqrt).then_inc(act_chain.sem, 1)
                    act.wait_ge(dve_chain.sem, at["gelu"])
                    act.activation(r[:], r[:], ACT.Tanh, scale=0.7978845608028654).then_inc(act_chain.sem, 1)
            finish(dve_chain)
            pe_chain.base += 4
            act_chain.base += 10
            ld[0].base += 256

        def forgetting_attention(proj, ahi, alo):
            with ExitStack() as c:
                f = narrow(c, "fox_f", [(g["w_in_2"][0][:, 16 * P:16 * P + FOX_H], FOX_H)], FOX_H, ahi, alo)
                bf = sb(c, "fox_bf", [P, FOX_H])
                upto = sb(c, "fox_upto", [P, 4, LAT])
                causal = sb(c, "fox_causal", [P, P])
                with ExitStack() as c1:
                    block = c1.enter_context(nc.Block())

                    @block.sync
                    def _(sp):
                        sp.dma_start(bf[:], g["fox_bf_2"][0].partition_broadcast(P)).then_inc(ld[0].sem, 16)
                        sp.dma_start(upto[:], g["k_upto"].rearrange("(k p) n -> p k n", p=P)).then_inc(ld[1].sem, 16)
                        sp.dma_start(causal[:], g["k_causal"]).then_inc(ld[2].sem, 16)
                        for n in range(3):
                            sp.wait_ge(ld[n].sem, ld[n].base + 16)
                for n in range(3):
                    ld[n].base += 16

                def load(dve, ch, neg):
                    ch.link(dve.scalar_tensor_tensor(out=neg[:].rearrange("p (t h) -> p t h", h=FOX_H), in0=f[:], scalar=-1.0,
                                                     in1=bf[:].unsqueeze(1).to_broadcast([P, 4, FOX_H]), op0=ALU.mult, op1=ALU.subtract))

                lf = softplus_neg(c, 4 * FOX_H, load)[:].rearrange("p (t h) -> p t h", h=FOX_H)
                cq = sb(c, "fox_cq", [P, 4, FOX_H])
                ck = sb(c, "fox_ck", [P, FOX_H, LAT])
                with ExitStack() as c1:
                    wide = sb(c1, "fox_wide", [P, 4, FOX_H, P])
                    block = c1.enter_context(nc.Block())

                    @block.vector
                    def _(dve):
                        for t in range(4):
                            dve.tensor_copy(wide[:, t], lf[:, t, :].unsqueeze(2).to_broadcast([P, FOX_H, P])).then_inc(dve_chain.sem, 1)
                        dve.wait_ge(pe_chain.sem, pe_chain.base + 1)
                        dve.tensor_copy(cq[:], ps[:, 4 * BANK:4 * BANK + 16].rearrange("p (t h) -> p t h", h=FOX_H))

                    @block.tensor
                    def _(pe):
                        for t in range(4):
                            for k in range(t + 1):
                                m = pe.matmul(ps[:, 4 * BANK + 4 * t:4 * BANK + 4 * t + 4], upto[:, k, t * P:(t + 1) * P], lf[:, k, :],
                                              start=(k == 0), stop=(k == t))
                        m.then_inc(pe_chain.sem, 1)
                        pe.wait_ge(dve_chain.sem, dve_chain.base + 4)
                        for h in range(FOX_H):
                            for k in range(4):
                                m = pe.matmul(ps[:, BANK * h:BANK * h + LAT], wide[:, k, h, :], upto[:, k, :], start=(k == 0), stop=(k == 3))
                            m.then_inc(pe_chain.sem, 1)

                    @block.scalar
                    def _(act):
                        for h in range(FOX_H):
                            act.wait_ge(pe_chain.sem, pe_chain.base + 2 + h)
                            act.copy(ck[:, h, :], ps[:, BANK * h:BANK * h + LAT])
                dve_chain.base += 4
                pe_chain.base += 5

                vt = sb(c, "fox_vt", [P, 4, 2 * P])
                token_major(proj, S_VC, 2, LAT, vt)
                qs = sb(c, "fox_q", [P, 2, LAT])
                ks = sb(c, "fox_k", [P, 2, LAT])
                vs = sb(c, "fox_v", [P, 2, 4, HD])

                def half(a, j):
                    return a[64 * j:64 * j + HD]

                def bias(dve, i, j, t, s):
                    ch = bias.chain
                    n = (t + 1) * P
                    m = dve.scalar_tensor_tensor(out=s, in0=s, scalar=cq[:, t, bass.ds(i * 2 + j, 1)],
                                                 in1=ck[:, bass.ds(i * 2 + j, 1), 0:n].rearrange("p a n -> p (a n)"), op0=ALU.subtract, op1=ALU.add)
                    ch.link(m)
                    return dve.tensor_tensor(s[:, n - P:n], s[:, n - P:n], causal[:], ALU.add)

                prep = Staged([lambda pool, i, j: pool.tensor_tensor(half(qs, j)[:, j, :], tile(half(proj, j), i + S_QC), half(scale_row, j).to_broadcast([HD, LAT]), ALU.mult),
                               lambda pool, i, j: pool.tensor_copy(half(ks, j)[:, j, :], tile(half(proj, j), i + S_KC))],
                              [lambda pool, i, j: pool.tensor_copy(vs[:, j], vt[:, :, bass.ds(i * P + j * HD, HD)])], 4)
                pe_p, dve_p, act_p, ended = attend(
                    c, 2, 4, lambda t: [(0, (t + 1) * P, 0)], lambda t: list(range(t + 1)),
                    lambda j, t: half(qs, j)[:, j, t * P:(t + 1) * P], lambda j, k0, n: half(ks, j)[:, j, k0:k0 + n],
                    lambda j, kt: vs[:, j, kt, :], lambda i, j: tile(half(proj, j), i + 6), 1.0, prep, bias=bias)
                simple_attention(c, prep, 2, pe_p, dve_p, act_p, 8 * 4)
            ended()
            prep.ended(2)

        def route(c, ahi, alo):
            weights = sb(c, "experts_w", [P, N_EXP, LAT])
            with ExitStack() as c0:
                NG, EG = 4, 4
                logits = narrow(c0, "logits", [(g["w_router_group_2"][0], NG), (g["w_router_expert_2"][0], N_EXP)], NG + N_EXP, ahi, alo)
                lb = sb(c0, "route_b", [P, NG + N_EXP])
                rank = sb(c0, "route_rank", [P, 4])
                sel = sb(c0, "route_sel", [N_EXP, N_EXP * P])
                comb = sb(c0, "route_comb", [P, 4, N_EXP])
                combT = sb(c0, "route_combT", [N_EXP, LAT])
                s1, s2, s3, s4, s5 = (sb(c0, f"route_s{n}", [P, 4, 1]) for n in range(5))
                g1, g2, hot, l1, l2, hot1, hot2 = (sb(c0, f"route_t{n}", [P, 4, 4]) for n in range(7))
                wide = sb(c0, "route_wide", [P, 4, N_EXP])
                block = c0.enter_context(nc.Block())
                a_0, d0 = act_chain.base, dve_chain.base
                at = {}

                @block.sync
                def _(sp):
                    sp.dma_start(lb[:, 0:NG], g["b_router_group_2"][0].partition_broadcast(P)).then_inc(ld[0].sem, 16)
                    sp.dma_start(lb[:, NG:], g["b_router_expert_2"][0].partition_broadcast(P)).then_inc(ld[0].sem, 16)
                    sp.dma_start(rank[:], g["k_rank"]).then_inc(ld[0].sem, 16)
                    sp.dma_start(sel[:], g["k_select"]).then_inc(ld[1].sem, 16)

                @block.vector
                def _(dve):
                    ch = Chain(dve, dve_chain)
                    b4 = lambda a: a[:].to_broadcast([P, 4, 4])
                    rk = rank[:].unsqueeze(1).to_broadcast([P, 4, 4])

                    def first_max(values, top, onehot, scratch):
                        ch.link(dve.tensor_reduce(top[:], values, AX, ALU.max))
                        ch.link(dve.tensor_tensor(onehot[:], values, b4(top), ALU.is_ge))
                        ch.link(dve.tensor_tensor(onehot[:], onehot[:], rk, ALU.mult))
                        ch.link(dve.tensor_reduce(scratch[:], onehot[:], AX, ALU.max))
                        ch.link(dve.tensor_tensor(onehot[:], onehot[:], b4(scratch), ALU.is_equal))

                    dve.wait_ge(ld[0].sem, ld[0].base + 48)
                    ch.link(dve.tensor_tensor(logits[:], logits[:], lb[:].unsqueeze(1).to_broadcast([P, 4, NG + N_EXP]), ALU.add))
                    gl = logits[:, :, 0:NG]
                    first_max(gl, s1, hot, s2)
                    ch.link(dve.tensor_tensor(g1[:], gl, b4(s1), ALU.subtract))
                    at["group"] = ch.value()
                    for q in range(NG):
                        ch.link(dve.tensor_tensor(wide[:, :, 4 * q:4 * q + 4], logits[:, :, NG + 4 * q:NG + 4 * q + 4],
                                                  hot[:, :, q:q + 1].to_broadcast([P, 4, 4]), ALU.mult))
                    ch.link(dve.tensor_reduce(l1[:], wide[:].rearrange("p t (g e) -> p t e g", g=NG), AX, ALU.add))
                    first_max(l1[:], s3, hot1, s4)
                    ch.link(dve.scalar_tensor_tensor(out=l2[:], in0=hot1[:], scalar=MASKED, in1=l1[:], op0=ALU.mult, op1=ALU.add))
                    first_max(l2[:], s4, hot2, s5)
                    ch.link(dve.tensor_tensor(s4[:], s4[:], s3[:], ALU.subtract))
                    at["second"] = ch.value()
                    dve.wait_ge(act_chain.sem, a_0 + 2)
                    ch.link(dve.tensor_reduce(s1[:], g2[:], AX, ALU.add))
                    ch.link(dve.tensor_scalar(s5[:], s2[:], 1.0, None, ALU.add))
                    ch.link(dve.tensor_tensor(s1[:], s1[:], s5[:], ALU.mult))
                    ch.link(dve.reciprocal(s1[:], s1[:]))
                    ch.link(dve.tensor_tensor(s2[:], s1[:], s2[:], ALU.mult))
                    ch.link(dve.tensor_tensor(hot1[:], hot1[:], b4(s1), ALU.mult))
                    ch.link(dve.tensor_tensor(hot2[:], hot2[:], b4(s2), ALU.mult))
                    ch.link(dve.tensor_tensor(hot1[:], hot1[:], hot2[:], ALU.add))
                    for q in range(NG):
                        ch.link(dve.tensor_tensor(comb[:, :, 4 * q:4 * q + 4], hot1[:], hot[:, :, q:q + 1].to_broadcast([P, 4, 4]), ALU.mult))
                    at["comb"] = ch.value()
                    dve.wait_ge(pe_chain.sem, pe_chain.base + 1)
                    ch.link(dve.tensor_copy(combT[:], ps[0:N_EXP, 0:LAT]))
                    at["combT"] = ch.value()
                    ch.done()

                @block.scalar
                def _(act):
                    act.wait_ge(dve_chain.sem, at["group"])
                    act.activation(g2[:], g1[:], ACT.Exp).then_inc(act_chain.sem, 1)
                    act.wait_ge(dve_chain.sem, at["second"])
                    act.activation(s2[:], s4[:], ACT.Exp).then_inc(act_chain.sem, 1)
                    for e in range(N_EXP):
                        act.wait_ge(pe_chain.sem, pe_chain.base + 2 + e)
                        b = BANK * (1 + e % 4)
                        act.copy(weights[:, e, :], ps[:, b:b + LAT]).then_inc(act_chain.sem, 1)

                @block.tensor
                def _(pe):
                    pe.wait_ge(dve_chain.sem, at["comb"])
                    for t in range(4):
                        m = pe.transpose(ps[0:N_EXP, t * P:(t + 1) * P], comb[:, t, :], ident[:])
                    m.then_inc(pe_chain.sem, 1)
                    pe.wait_ge(dve_chain.sem, at["combT"])
                    pe.wait_ge(ld[1].sem, ld[1].base + 16)
                    for e in range(N_EXP):
                        if e >= 4:
                            pe.wait_ge(act_chain.sem, a_0 + 2 + e - 3)
                        b = BANK * (1 + e % 4)
                        pe.matmul(ps[:, b:b + LAT], sel[:, e * P:(e + 1) * P], combT[:], start=True, stop=True).then_inc(pe_chain.sem, 1)
            finish(dve_chain)
            act_chain.base += 2 + N_EXP
            pe_chain.base += 1 + N_EXP
            ld[0].base += 48
            ld[1].base += 16
            return weights

        def write_out(tiles):
            with ExitStack() as c:
                o = sb(c, "o", [P, 4, D])
                block = c.enter_context(nc.Block())

                @block.tensor
                def _(pe):
                    for u in range(8):
                        t, half = u // 2, u % 2
                        if u >= 4:
                            pe.wait_ge(act_chain.sem, act_chain.base + u - 3)
                        for q in range(4):
                            b = BANK * (u % 4) + q * P
                            m = pe.transpose(ps[:, b:b + P], tiles[4 * half + q][:, t * P:(t + 1) * P], ident[:])
                        m.then_inc(pe_chain.sem, 1)

                @block.scalar
                def _(act):
                    for u in range(8):
                        t, half = u // 2, u % 2
                        act.wait_ge(pe_chain.sem, pe_chain.base + u + 1)
                        act.copy(o[:, t, half * 512:(half + 1) * 512], ps[:, BANK * (u % 4):BANK * (u % 4) + 512]).then_inc(act_chain.sem, 1)

                @block.sync
                def _(sp):
                    for t in range(4):
                        sp.wait_ge(act_chain.sem, act_chain.base + 2 * t + 2)
                        sp.dma_start(out[0, t * P:(t + 1) * P, :], o[:, t, :]).then_inc(ld[3].sem, 16)
                    sp.wait_ge(ld[3].sem, ld[3].base + 64)

        def second_block():
            modulation(g["w_mod_2"][0], (2, 2), vec3[:, 0:48], 1)
            with ExitStack() as c:
                ahi = sb(c, "a2hi", [P, KT, LAT], F32R)
                alo = sb(c, "a2lo", [P, KT, LAT], F32R)

                def prenorm(v, s):
                    with ExitStack() as c1:
                        h = sb(c1, "h", [P, KT, LAT])
                        normalize([h[:, k, :] for k in range(KT)], LAT, RMS_EPS, lambda k: col(vec1, v + k), post=(ahi, alo, *modulate_by(s)), src=xt(LAT))

                prenorm(V_MIX, 0)
                with ExitStack() as c1:
                    proj = sb(c1, "proj2", [P, 16, LAT])
                    with ExitStack() as c2:
                        project(new_ring(c2, KT), g["w_in_2"][0], proj, 0, 16, LAT, 0, (ahi, alo))
                    banded_attention(proj)
                    recurrence(proj)
                    forgetting_attention(proj, ahi, alo)
                    for first, n in ((0, 4), (4, 2), (6, 2)):
                        normalize([proj[:, first + k, :] for k in range(n)], LAT, RMS_EPS, lambda k: col(vec3, V3_GAIN + first + k))
                    split(proj, ahi, alo, KT, LAT)
                    with ExitStack() as c2:
                        residual(new_ring(c2, KT), g["w_out_2"][0], 2 * KT, KT, (ahi, alo), LAT)
                prenorm(V_FFN, 3)
                weights = route(c, ahi, alo)
                ring = new_ring(c, 2 * KT)
                GE = 8
                hhi = sb(c, "ehi", [P, 2 * GE, LAT], F32R)
                hlo = sb(c, "elo", [P, 2 * GE, LAT], F32R)
                down = g["w_down_2"][0].rearrange("e h d -> (e h) d")
                for part in range(N_EXP // GE):
                    views = [g[n][0].rearrange("e (k p) c -> p e k c", p=P) for n in ("w_gate_2", "w_up_2")]
                    with ExitStack() as c1:
                        swiglu(ring, c1, lambda i, jj: [(0, KT, views[jj % 2][:, bass.ds(i + part * GE, 1), :, (jj // 2) * P:(jj // 2 + 1) * P]
                                                         .rearrange("p a k c -> p (a k) c"))],
                               4, 2 * GE, (ahi, alo), (hhi, hlo), LAT, combine=lambda i: tile(weights, i + part * GE))
                    residual(ring, down, 5 * KT, KT, (hhi, hlo), LAT, row0=part * GE * D_EXP, nk=2 * GE)
            normalize(xt(LAT), LAT, RMS_EPS, lambda k: col(vec1, V_FINAL + k))
            write_out(xt(LAT))
        setup()
        modulation(g["w_mod"][0], (0, 1), vec2[:, 0:48], 2)
        with ExitStack() as c:
            ahi = sb(c, "ahi", [P, KT, ALL], F32R)
            alo = sb(c, "alo", [P, KT, ALL], F32R)
            normalize(xt(ALL), ALL, LN_EPS, lambda k: col(vec1, V_LN_IN_G + k), lambda k: col(vec1, V_LN_IN_B + k), center=True,
                      post=(ahi, alo, *modulate_by(0)), after=ALPHA)
            for l in range(DEPTH):
                layer(l, ahi, alo)
        second_block()


def constants():
    f = np.float32
    k = {"k_ident": np.eye(P, dtype=f)}
    w = np.arange(GRID_W)
    start = np.clip(w - KW // 2, 0, GRID_W - KW)
    inside = (w[None, :] >= start[:, None]) & (w[None, :] < start[:, None] + KW)
    k["k_na_mask"] = np.tile(np.where(inside, 0.0, MASKED), (2, 1)).astype(f)
    t = np.arange(LAT)
    freq = 10000.0 ** (-np.arange(ROPE // 4) / (ROPE // 4))
    ang = np.concatenate([(t // GRID_W)[:, None] * freq, (t % GRID_W)[:, None] * freq], -1).T
    rope = np.zeros((P, LAT))
    rope[64:80] = rope[80:96] = np.cos(ang)
    rope[96:112], rope[112:128] = -np.sin(ang), np.sin(ang)
    k["k_rope"] = rope.astype(f)
    spread = np.zeros((ROPE, P))
    for r in range(ROPE):
        spread[r, HD + r] = 1.0
        spread[(r + 16) % 32, HD + ROPE + r] = 1.0
    k["k_spread"] = spread.astype(f)

    def dft(n):
        a = 2 * np.pi * (np.outer(np.arange(n), np.arange(n)) % n) / n
        return np.cos(a), np.sin(a)

    cc, sc = dft(P)
    k["k_dft_chan"] = (np.concatenate([cc, sc], 1) / np.sqrt(P)).astype(f)
    for name, n in (("k_dft_lat", LAT), ("k_dft_ctx", CTX)):
        cs, ss = dft(n)
        k[name] = (np.stack([cs, -ss], 1) / np.sqrt(n)).astype(f)
    q, kk = np.arange(P)[:, None] + P, np.arange(2 * P)[None, :]
    dist = q - kk
    valid = (dist >= 0) & (dist < P)
    slopes = 2.0 ** (-8.0 * np.arange(1, SWA_H + 1) / SWA_H)
    k["k_swa"] = np.where(valid[:, None, :], -slopes[None, :, None] * dist[:, None, :], MASKED).astype(f)
    k["k_upto"] = (t[:, None] <= t[None, :]).astype(f)
    k["k_causal"] = np.where(np.arange(P)[None, :] <= np.arange(P)[:, None], 0.0, MASKED).astype(f)
    sel = np.zeros((N_EXP, N_EXP, P))
    for e in range(N_EXP):
        sel[e, e] = 1.0
    k["k_select"] = sel.reshape(N_EXP, N_EXP * P).astype(f)
    k["k_rank"] = np.tile(np.arange(4, 0, -1), (P, 1)).astype(f)
    return k


_INS = ("x c ctx c_ctx ln_in_g ln_in_b w_mod b_mod w_in mla_q_norm_g mla_kv_norm_g w_uq w_qr w_uk w_uv na_rpb w_branch w_out "
        "ln1_g ln1_b ln2_g ln2_b w_ffn_gate w_ffn_up w_ffn_down c_2 w_mod_2 b_mod_2 norm_mix_2 norm_ffn_2 w_in_2 w_out_2 out_gain_2 "
        "sinks_2 conv_w_2 conv_b_2 lru_wa_2 lru_ba_2 lru_wx_2 lru_bx_2 lru_lam_2 fox_bf_2 w_router_group_2 b_router_group_2 "
        "w_router_expert_2 b_router_expert_2 w_gate_2 w_up_2 w_down_2 norm_final_2").split()


def kernel(**inputs):
    import concourse.bacc as bacc
    from concourse.bass_utils import run_bass_kernel_spmd

    nc = bacc.Bacc("TRN2", target_bir_lowering=False, num_devices=1)
    arrays, aps = {}, {}
    every = {**{n: inputs[n] for n in _INS}, **constants()}
    for name, a in every.items():
        a = np.ascontiguousarray(a)
        arrays[f"in_{name}"] = a
        aps[name] = nc.dram_tensor(f"in_{name}", a.shape, mybir.dt.from_np(a.dtype), kind="ExternalInput").ap()
    out = nc.dram_tensor("out", (1, LAT, D), F32, kind="ExternalOutput").ap()
    program(nc, aps, out)
    r = run_bass_kernel_spmd(nc, [arrays], core_ids=[0])
    return r.results[0]["out"]
```

```python
from contextlib import ExitStack

import numpy as np

import concourse.bass as bass
from concourse import mybir

F32 = mybir.dt.float32
F32R = mybir.dt.float32r
ALU = mybir.AluOpType
ACT = mybir.ActivationFunctionType
AX = mybir.AxisListType.X

P = 128
D = 1024
KT = D // P
LAT, CTX = 512, 256
ALL = LAT + CTX
DEPTH = 2
GRID_W = 64
ROWS = LAT // GRID_W
FNET_W, NA_W = 512, 512
HEADS = 8
HD = 64
KH, KW = 8, 16
Q_LORA, KV_LORA, ROPE = 256, 128, 32
MLA_K = HD + ROPE
MLA_SCALE = float(MLA_K) ** -0.5
NA_SCALE = float(HD) ** -0.5
FFN = 2816
ALPHA = float((2 * DEPTH) ** 0.25)
LN_EPS = 1e-5
RMS_EPS = 1e-6
GATE_COL = FNET_W + 3 * NA_W + Q_LORA + KV_LORA + ROPE
MASKED = -1.0e30
N_EXP, D_EXP = 16, 256
FOX_H, SWA_H = 4, 8
LRU_W = 256
BANK = 512

T_F, T_NQ, T_NK, T_NV, T_CQ, T_CKV, T_KR = 0, 4, 8, 12, 16, 18, 19
T_Y = (0, 4, 8)
T_M = 12
S_QA, S_KA, S_VA, S_XB, S_GB, S_QC, S_KC, S_VC = 0, 4, 5, 6, 8, 10, 12, 14


class Tally:

    def __init__(self, sem):
        self.sem, self.base = sem, 0


class Chain:

    def __init__(self, eng, tally):
        self.eng, self.tally, self.n, self.i, self.per = eng, tally, 0, None, 0

    def value(self):
        v = self.tally.base + self.n
        return v if self.i is None else self.i * self.per + v

    def mark(self, ins):
        ins.then_inc(self.tally.sem, 1)
        self.n += 1
        return ins

    def link(self, ins):
        self.mark(ins)
        self.eng.wait_ge(self.tally.sem, self.value())

    def open(self, i, per):
        self.i, self.per, self.start = i, per, self.n

    def close(self, trips):
        assert self.n - self.start == self.per, (self.n - self.start, self.per)
        self.n += (trips - 1) * self.per
        self.i = None

    def done(self):
        self.tally.final = self.n


def groups(T):
    return [(0, min(T, LAT))] + ([(LAT, T - LAT)] if T > LAT else [])


def program(nc, g, out):
    root = ExitStack()
    with root:
        names = [0]

        def sb(ctx, name, shape, dt=F32):
            names[0] += 1
            return ctx.enter_context(nc.sbuf_tensor(f"{name}_{names[0]}", shape, dt))

        def tally(name):
            return Tally(root.enter_context(nc.semaphore(name)))

        ps = root.enter_context(nc.psum_tensor("ps", [P, 8 * BANK], F32))

        w_loaded = [tally(f"w_loaded{j}") for j in range(2)]
        hi_ready = [tally(f"hi_ready{j}") for j in range(2)]
        lo_ready = [tally(f"lo_ready{j}") for j in range(2)]
        mm_done = [tally(f"mm_done{j}") for j in range(2)]
        psum_free = [tally(f"psum_free{j}") for j in range(2)]
        h_scaled, h_hi_ready, h_ready, gated, merged, y_hi, y_ready = (
            tally(n) for n in ("h_scaled", "h_hi_ready", "h_ready", "gated", "merged", "y_hi", "y_ready"))
        dve_chain, act_chain, pool_chain, pe_chain = (tally(n) for n in ("dve_chain", "act_chain", "pool_chain", "pe_chain"))
        ld = [tally(f"ld{n}") for n in range(16)]
        s_done, nm_done, p_done, pn_done, t_done, pt_done, pv_done, o_done = (
            tally(n) for n in ("s_done", "nm_done", "p_done", "pn_done", "t_done", "pt_done", "pv_done", "o_done"))
        qk_staged, v_staged, prep_mm, prep_out, prep_rope = (tally(n) for n in ("qk_staged", "v_staged", "prep_mm", "prep_out", "prep_rope"))
        head_w = [tally(f"head_w{j}") for j in range(2)]
        bias_masked = tally("bias_masked")
        norm_mean, norm_c, norm_sq, norm_var, norm_rstd = (tally(n) for n in ("norm_mean", "norm_c", "norm_sq", "norm_var", "norm_rstd"))
        norm_sqrt, norm_x, norm_g, norm_hi = (tally(n) for n in ("norm_sqrt", "norm_x", "norm_g", "norm_hi"))

        from_one = [*mm_done, *psum_free, h_scaled, h_hi_ready, h_ready, gated, merged, y_hi, y_ready, s_done, nm_done, p_done, pn_done,
                    t_done, pt_done, pv_done, o_done, qk_staged, v_staged, prep_mm, prep_out, prep_rope, bias_masked]

        def finish(*tallies):
            for t in tallies:
                t.base += t.final
                t.final = 0

        ident = sb(root, "ident", [P, P])
        ones = sb(root, "ones", [P, P])
        vec1 = sb(root, "vec1", [P, 128])
        vec2 = sb(root, "vec2", [P, 96])
        vec3 = sb(root, "vec3", [P, 78])
        csilu = sb(root, "csilu", [P, 3, KT])
        mod = sb(root, "mod", [P, 2, 48])
        x = sb(root, "x", [P, KT, ALL])
        warm = sb(root, "warm", [P, 1])
        na_mask = sb(root, "na_mask", [P, GRID_W])
        rpb = sb(root, "na_rpb", [HEADS * 15, P])
        scale_row = sb(root, "scale_row", [P, 1])

        V_LN_IN_G, V_LN_IN_B = 0, 8
        V_LN1_G, V_LN1_B, V_LN2_G, V_LN2_B = 16, 32, 48, 64
        V_C, V_MIX, V_FFN, V_FINAL = 80, 104, 112, 120
        V3_QN, V3_KVN, V3_GAIN, V3_CONVW, V3_CONVB, V3_BA, V3_BX, V3_LAM = 48, 52, 54, 62, 70, 72, 74, 76

        def col(v, n):
            return v[:, n:n + 1]

        def setup():
            with ExitStack() as c:
                rows = sb(c, "rows", [P, 3, P])
                xin = sb(c, "xin", [P, 6, D])
                block = c.enter_context(nc.Block())

                @block.sync
                def _(sp):
                    sp.dma_start(ident[:], g["k_ident"]).then_inc(ld[0].sem, 16)
                    for t in range(4):
                        sp.dma_start(xin[:, t, :], g["x"][0, t * P:(t + 1) * P, :]).then_inc(ld[2].sem, 16)
                    for t in range(2):
                        sp.dma_start(xin[:, 4 + t, :], g["ctx"][0, t * P:(t + 1) * P, :]).then_inc(ld[2].sem, 16)
                    at = 0

                    def put(tile, src, n):
                        nonlocal at
                        sp.dma_start(rows[at:at + n, tile, :], src).then_inc(ld[1].sem, 16)
                        at += n

                    r8 = lambda a: a.rearrange("(k p) -> k p", p=P)
                    r2 = lambda a: a.rearrange("l (k p) -> (l k) p", p=P)
                    for a in ("ln_in_g", "ln_in_b"):
                        put(0, r8(g[a]), 8)
                    for a in ("ln1_g", "ln1_b", "ln2_g", "ln2_b"):
                        put(0, r2(g[a]), 16)
                    put(0, r2(g["c"]), 8)
                    put(0, r8(g["c_ctx"]), 8)
                    put(0, r2(g["c_2"]), 8)
                    put(0, r2(g["norm_mix_2"]), 8)
                    put(0, r2(g["norm_ffn_2"]), 8)
                    put(0, r8(g["norm_final_2"]), 8)
                    at = 0
                    put(1, r2(g["b_mod"]), 96)
                    at = 0
                    put(2, r2(g["b_mod_2"]), 48)
                    put(2, r2(g["mla_q_norm_g"]), 4)
                    put(2, r2(g["mla_kv_norm_g"]), 2)
                    put(2, r2(g["out_gain_2"]), 8)
                    put(2, g["conv_w_2"].rearrange("l w (k p) -> (l w k) p", p=P), 8)
                    for a in ("conv_b_2", "lru_ba_2", "lru_bx_2", "lru_lam_2"):
                        put(2, r2(g[a]), 2)
                    sp.dma_start(na_mask[:], g["k_na_mask"]).then_inc(ld[3].sem, 16)
                    for t in from_one:
                        sp.sem_inc(t.sem, 1)
                    sp.wait_ge(ld[3].sem, 16)

                n_rows = 12 + 1 + 9

                @block.tensor
                def _(pe):
                    pe.wait_ge(ld[0].sem, 16)
                    pe.wait_ge(ld[2].sem, 96)
                    for u in range(12):
                        k, half = u // 2, u % 2
                        if u >= 4:
                            pe.wait_ge(act_chain.sem, u - 3)
                        for q in range(4):
                            m = pe.transpose(ps[:, BANK * (1 + u % 4) + q * P:BANK * (1 + u % 4) + (q + 1) * P],
                                             xin[:, u // 2, (4 * half + q) * P:(4 * half + q + 1) * P], ident[:])
                        m.then_inc(pe_chain.sem, 1)
                    pe.wait_ge(ld[1].sem, 16 * n_rows)
                    for t, n in enumerate((128, 96, 78)):
                        m = pe.transpose(ps[:, t * P:t * P + n], rows[0:n, t, :], ident[0:n, 0:n])
                    m.then_inc(pe_chain.sem, 1)

                @block.vector
                def _(dve):
                    dve.memset(ones[:], 1.0)
                    dve.memset(rpb[:], 0.0)
                    dve.memset(scale_row[:], NA_SCALE)
                    dve.wait_ge(pe_chain.sem, 13)
                    for t, (v, n) in enumerate(((vec1, 128), (vec2, 96), (vec3, 78))):
                        m = dve.tensor_copy(v[:], ps[:, t * P:t * P + n])
                    m.then_inc(dve_chain.sem, 1)

                @block.scalar
                def _(act):
                    for u in range(12):
                        t, half = u // 2, u % 2
                        act.wait_ge(pe_chain.sem, 1 + u)
                        b = BANK * (1 + u % 4)
                        act.copy(x[:, 4 * half:4 * half + 4, t * P:(t + 1) * P],
                                 ps[:, b:b + 512].rearrange("p (q n) -> p q n", q=4)).then_inc(act_chain.sem, 1)
                    act.wait_ge(dve_chain.sem, 1)
                    act.activation(csilu[:].rearrange("p a k -> p (a k)"), vec1[:, V_C:V_C + 24], ACT.Silu).then_inc(act_chain.sem, 1)
            for t in from_one:
                t.base += 1
            ld[0].base += 16
            ld[3].base += 16
            ld[1].base += 16 * 22
            ld[2].base += 96
            pe_chain.base += 13
            act_chain.base += 13
            dve_chain.base += 1

        def modulation(w, cols, bias, n_vec):
            RING, CN = 4, 256
            tiles = 6 * KT
            trips = 6 * D // CN // RING
            with ExitStack() as c:
                raw = sb(c, "mod_w", [P, RING, KT, CN])
                whi = sb(c, "mod_w_hi", [P, 2, KT, CN], F32R)
                wlo = sb(c, "mod_w_lo", [P, 2, KT, CN], F32R)
                cs = sb(c, "mod_c", [P, KT, 2])
                cr = sb(c, "mod_c_hi_lo", [P, KT, 4], F32R)
                rows = sb(c, "mod_rows", [4, 6 * D])
                turned = sb(c, "mod_turned", [2 * tiles, 2, P])
                loads = [ld[n] for n in range(RING)]
                wv = w.rearrange("(k p) c -> p k c", p=P)
                block = c.enter_context(nc.Block())

                def use(i, s):
                    return i * 2 + s // 2

                def all_trips(eng, step):
                    for s in range(RING):
                        step(0, s, True)
                    with eng.Fori(1, trips) as i:
                        for s in range(RING):
                            step(i, s, False)

                @block.sync
                def _(sp):
                    def step(i, s, first):
                        if not first:
                            sp.wait_ge(lo_ready[s % 2].sem, i * 2 + (lo_ready[s % 2].base + s // 2 - 1))
                        sp.dma_start(raw[:, s], wv[:, :, bass.ds(i * (RING * CN) + s * CN, CN)]).then_inc(loads[s].sem, 16)

                    all_trips(sp, step)
                    for j in range(2):
                        sp.wait_ge(psum_free[j].sem, psum_free[j].base + 2 * trips)
                    for part in range(2):
                        sp.dma_start(turned[:, part, :], rows[2 * part:2 * part + 2, :].rearrange("v (t p) -> v t p", p=P)).then_inc(ld[RING].sem, 16)

                @block.tensor
                def _(pe):
                    pe.wait_ge(dve_chain.sem, dve_chain.base + 3)

                    def step(i, s, first):
                        j = s % 2
                        if not first:
                            pe.wait_ge(psum_free[j].sem, i * 2 + (psum_free[j].base + s // 2 - 1))
                        for ready, part in ((hi_ready[j], whi), (lo_ready[j], wlo)):
                            pe.wait_ge(ready.sem, use(i, s) + (ready.base + 1))
                            for k in range(KT):
                                m = pe.matmul(ps[0:4, s * BANK:s * BANK + CN], cr[:, k, :], part[:, j, k, :],
                                              start=(part is whi and k == 0), stop=(part is wlo and k == KT - 1))
                        m.then_inc(mm_done[j].sem, 1)

                    all_trips(pe, step)
                    pe.wait_ge(ld[RING].sem, ld[RING].base + 32)
                    for part in range(2):
                        m = pe.matmul(ps[:, RING * BANK:RING * BANK + 2 * tiles], turned[:, part, :], ident[0:2 * tiles, 0:2 * tiles],
                                      start=(part == 0), stop=(part == 1))
                    m.then_inc(pe_chain.sem, 1)

                @block.scalar
                def _(act):
                    def out(i, s):
                        j = s % 2
                        act.wait_ge(mm_done[j].sem, use(i, s) + (mm_done[j].base + 1))
                        act.copy(rows[:, bass.ds(i * (RING * CN) + s * CN, CN)], ps[0:4, s * BANK:s * BANK + CN]).then_inc(psum_free[j].sem, 1)

                    def step(i, s, first):
                        j = s % 2
                        act.wait_ge(loads[s].sem, i * 16 + (loads[s].base + 16))
                        if not first or s >= 2:
                            act.wait_ge(mm_done[j].sem, use(i, s) + mm_done[j].base)
                        act.copy(whi[:, j], raw[:, s]).then_inc(hi_ready[j].sem, 1)
                        if s >= 1:
                            out(i, s - 1)
                        elif not first:
                            out(i - 1, RING - 1)

                    all_trips(act, step)
                    out(trips - 1, RING - 1)

                @block.vector
                def _(dve):
                    a, b = cols
                    ch = Chain(dve, dve_chain)
                    dve.tensor_copy(cs[:, :, 0], csilu[:, a, :])
                    ch.link(dve.tensor_copy(cs[:, :, 1], csilu[:, b, :]))
                    ch.link(dve.tensor_copy(cr[:, :, 0:2], cs[:]))
                    ch.mark(dve.tensor_tensor(cr[:, :, 2:4], cs[:], cr[:, :, 0:2].bitcast(F32), ALU.subtract))

                    def step(i, s, first):
                        j = s % 2
                        if not first or s >= 2:
                            dve.wait_ge(mm_done[j].sem, use(i, s) + mm_done[j].base)
                        dve.wait_ge(hi_ready[j].sem, use(i, s) + (hi_ready[j].base + 1))
                        dve.tensor_tensor(wlo[:, j], raw[:, s], whi[:, j].bitcast(F32), ALU.subtract).then_inc(lo_ready[j].sem, 1)

                    all_trips(dve, step)
                    dve.wait_ge(pe_chain.sem, pe_chain.base + 1)
                    for v in range(2):
                        at = RING * BANK + v * tiles
                        ch.mark(dve.tensor_tensor(mod[:, v, :], ps[:, at:at + tiles], bias, ALU.add))
                    dve.wait_ge(dve_chain.sem, ch.value())
                    for s in (1, 2, 4, 5) if n_vec == 2 else (1, 4):
                        dve.tensor_scalar(mod[:, :, s * KT:(s + 1) * KT], mod[:, :, s * KT:(s + 1) * KT], 1.0, None, ALU.add)
                    ch.done()
            for l in loads:
                l.base += 16 * trips
            ld[RING].base += 32
            pe_chain.base += 1
            for j in range(2):
                for t in (hi_ready, lo_ready, mm_done, psum_free):
                    t[j].base += 2 * trips
            finish(dve_chain)

        def normalize(tiles, T, eps, gain, bias=None, center=False, post=None, after=None, src=None):
            n = len(tiles)
            dim = n * P
            tg = groups(T)
            src = src or tiles
            with ExitStack() as c:
                sq = sb(c, "sq", [P, 2, T])
                rstd = sb(c, "rstd", [P, T])
                xn = sq
                if post:
                    tmp = sb(c, "tmp", [P, 2, T])
                    co = sb(c, "norm_co", [P, 6, n])
                block = c.enter_context(nc.Block())

                @block.tensor
                def _(pe):
                    if center:
                        for t0, tn in tg:
                            for k in range(n):
                                m = pe.matmul(ps[:, t0:t0 + tn], ones[:], src[k][:, t0:t0 + tn], start=(k == 0), stop=(k == n - 1))
                        m.then_inc(norm_mean.sem, 1)
                    for k in range(n):
                        pe.wait_ge(norm_sq.sem, norm_sq.base + k + 1)
                        for t0, tn in tg:
                            m = pe.matmul(ps[:, 1024 + t0:1024 + t0 + tn], ones[:], sq[:, k % 2, t0:t0 + tn],
                                          start=(k == 0), stop=(k == n - 1), skip_group_check=True)
                        m.then_inc(norm_var.sem, 1)

                @block.scalar
                def _(act):
                    for k in range(n):
                        if center:
                            act.wait_ge(norm_c.sem, norm_c.base + k + 1)
                        if k >= 2:
                            act.wait_ge(norm_var.sem, norm_var.base + k - 1)
                        act.activation(sq[:, k % 2, :], (tiles if center else src)[k], ACT.Square).then_inc(norm_sq.sem, 1)
                    act.wait_ge(norm_rstd.sem, norm_rstd.base + 1)
                    act.activation(rstd[:], rstd[:], ACT.Sqrt).then_inc(norm_sqrt.sem, 1)
                    for k in range(n):
                        act.wait_ge(norm_x.sem, norm_x.base + k + 1)
                        if post:
                            for v, (t0, tn) in enumerate(tg):
                                m = act.activation(post[0][:, k, t0:t0 + tn], xn[:, k % 2, t0:t0 + tn], ACT.Identity,
                                                   scale=co[:, v, k:k + 1], bias=co[:, 2 + v, k:k + 1])
                            m.then_inc(norm_hi.sem, 1)
                        s, b = gain(k), bias(k) if bias else 0.0
                        if post and after:
                            s, b = co[:, 4, k:k + 1], co[:, 5, k:k + 1]
                        act.activation(tiles[k], xn[:, k % 2, :], ACT.Identity, scale=s, bias=b).then_inc(norm_g.sem, 1)

                @block.vector
                def _(dve):
                    ch = Chain(dve, dve_chain)
                    if post:
                        hi, lo, scale, shift = post
                        for k in range(n):
                            for v in range(len(tg)):
                                m = dve.tensor_tensor(co[:, v, k:k + 1], gain(k), scale(v, k), ALU.mult)
                                if bias:
                                    m = dve.scalar_tensor_tensor(out=co[:, 2 + v, k:k + 1], in0=bias(k), scalar=scale(v, k), in1=shift(v, k),
                                                                 op0=ALU.mult, op1=ALU.add)
                                else:
                                    m = dve.tensor_copy(co[:, 2 + v, k:k + 1], shift(v, k))
                            if after:
                                dve.tensor_scalar(co[:, 4, k:k + 1], gain(k), after, None, ALU.mult)
                                m = dve.tensor_scalar(co[:, 5, k:k + 1], bias(k), after, None, ALU.mult)
                        ch.mark(m)
                    if center:
                        dve.wait_ge(norm_mean.sem, norm_mean.base + 1)
                        for k in range(n):
                            dve.scalar_tensor_tensor(out=tiles[k], in0=ps[:, 0:T], scalar=-1.0 / dim, in1=src[k],
                                                     op0=ALU.mult, op1=ALU.add).then_inc(norm_c.sem, 1)
                    dve.wait_ge(norm_var.sem, norm_var.base + n)
                    dve.tensor_scalar(rstd[:], ps[:, 1024:1024 + T], 1.0 / dim, eps, ALU.mult, ALU.add).then_inc(norm_rstd.sem, 1)
                    dve.wait_ge(norm_sqrt.sem, norm_sqrt.base + 1)
                    ch.link(dve.reciprocal(rstd[:], rstd[:]))

                    def rest(k):
                        dve.wait_ge(norm_hi.sem, norm_hi.base + k + 1)
                        dve.wait_ge(norm_rstd.sem, norm_rstd.base + 2 + k)
                        ch.mark(dve.tensor_tensor(lo[:, k, 0:T], tmp[:, k % 2, :], hi[:, k, 0:T].bitcast(F32), ALU.subtract))

                    for k in range(n):
                        if k >= 2:
                            dve.wait_ge(norm_g.sem, norm_g.base + k - 1)
                            if post:
                                dve.wait_ge(norm_rstd.sem, norm_rstd.base + k)
                        dve.tensor_tensor(xn[:, k % 2, :], (tiles if center else src)[k], rstd[:], ALU.mult).then_inc(norm_x.sem, 1)
                        if post:
                            if k >= 1:
                                rest(k - 1)
                            if k >= 2:
                                dve.wait_ge(dve_chain.sem, ch.value() - 1)
                            dve.wait_ge(norm_x.sem, norm_x.base + k + 1)
                            for v, (t0, tn) in enumerate(tg):
                                m = dve.tensor_scalar(tmp[:, k % 2, t0:t0 + tn], xn[:, k % 2, t0:t0 + tn],
                                                      co[:, v, k:k + 1], co[:, 2 + v, k:k + 1], ALU.mult, ALU.add)
                            m.then_inc(norm_rstd.sem, 1)
                    if post:
                        rest(n - 1)
                    ch.done()
            finish(dve_chain)
            norm_mean.base += center
            norm_c.base += n if center else 0
            norm_sq.base += n
            norm_var.base += n
            norm_rstd.base += 1 + (n if post else 0)
            norm_sqrt.base += 1
            norm_x.base += n
            norm_g.base += n
            norm_hi.base += n if post else 0

        class Dense:

            def __init__(self, chunks, per, blocks, loads, parts, T, act_out, dve_out, adds=(), before=None, func=None):
                self.chunks, self.per, self.blocks, self.loads, self.parts, self.T = chunks, per, blocks, loads, parts, T
                self.act_out, self.dve_out, self.before, self.func = act_out, dve_out, before or {}, func
                self.trips, self.half, self.n_loads = chunks // per, per // 2, len(loads(0, 0))
                self.adds = dict(adds)
                for j in range(2):
                    self.adds[w_loaded[j]] = 16 * self.n_loads * chunks // 2
                    for t in (hi_ready, lo_ready, mm_done, psum_free):
                        self.adds[t[j]] = chunks // 2

            def use(self, i, jj):
                return i * self.half + jj // 2

        def run_dense(ring, layers):
            raw, whi, wlo = ring
            tallies = {t for d in layers for t in d.adds}
            value = {t: t.base for t in tallies}
            for d in layers:
                d.start = dict(value)
                for t, n in d.adds.items():
                    value[t] += n

            def enter(d):
                for t, v in d.start.items():
                    t.base = v
                return d

            def pipelined(who, eng, split, take):
                for n, d in enumerate(layers):
                    enter(d)
                    if n == 0:
                        split(d, 0, 0)
                    if who in d.before:
                        d.before[who](eng)
                    if who == "act" and d.func is not None:
                        eng.activation(warm[:], ones[:, 0:1], d.func)
                    if d.trips > 1:
                        with eng.Fori(0, d.trips - 1) as i:
                            for jj in range(d.per):
                                split(d, i + 1 if jj == d.per - 1 else i, (jj + 1) % d.per)
                                take(d)(eng, i, jj)
                    for jj in range(d.per):
                        if jj < d.per - 1:
                            split(d, d.trips - 1, jj + 1)
                        elif n + 1 < len(layers):
                            split(enter(layers[n + 1]), 0, 0)
                            enter(d)
                        take(d)(eng, d.trips - 1, jj)

            with ExitStack() as c:
                block = c.enter_context(nc.Block())

                @block.sync
                def _(sp):
                    for d in layers:
                        enter(d)
                        with sp.Fori(0, d.trips) as i:
                            for jj in range(d.per):
                                j = jj % 2
                                sp.wait_ge(lo_ready[j].sem, d.use(i, jj) + lo_ready[j].base)
                                for b0, nb, src in d.loads(i, jj):
                                    sp.dma_start(raw[:, j, b0:b0 + nb, :], src).then_inc(w_loaded[j].sem, 16)

                @block.tensor
                def _(pe):
                    for d in layers:
                        enter(d)
                        if "pe" in d.before:
                            d.before["pe"](pe)
                        with pe.Fori(0, d.trips) as i:
                            for jj in range(d.per):
                                j = jj % 2
                                pe.wait_ge(lo_ready[j].sem, d.use(i, jj) + (lo_ready[j].base + 1))
                                pe.wait_ge(psum_free[j].sem, d.use(i, jj) + psum_free[j].base)
                                for off, b0, nb, hi, lo in d.parts:
                                    for t0, tn in groups(d.T):
                                        o = ps[:, 4 * BANK * j + off + t0:4 * BANK * j + off + t0 + tn]
                                        for b in range(nb):
                                            pe.matmul(o, whi[:, j, b0 + b, :], hi[:, b, t0:t0 + tn], start=(b == 0), stop=False)
                                            pe.matmul(o, wlo[:, j, b0 + b, :], hi[:, b, t0:t0 + tn], start=False, stop=False)
                                            m = pe.matmul(o, whi[:, j, b0 + b, :], lo[:, b, t0:t0 + tn], start=False, stop=(b == nb - 1))
                                m.then_inc(mm_done[j].sem, 1)

                @block.scalar
                def _(act):
                    def split_hi(d, i, jj):
                        j = jj % 2
                        act.wait_ge(w_loaded[j].sem, (d.use(i, jj) + 1) * (16 * d.n_loads) + w_loaded[j].base)
                        act.wait_ge(mm_done[j].sem, d.use(i, jj) + mm_done[j].base)
                        act.copy(whi[:, j, 0:d.blocks, :], raw[:, j, 0:d.blocks, :]).then_inc(hi_ready[j].sem, 1)

                    pipelined("act", act, split_hi, lambda d: d.act_out)

                @block.vector
                def _(dve):
                    def split_lo(d, i, jj):
                        j = jj % 2
                        dve.wait_ge(hi_ready[j].sem, d.use(i, jj) + (hi_ready[j].base + 1))
                        dve.tensor_tensor(wlo[:, j, 0:d.blocks, :], raw[:, j, 0:d.blocks, :], whi[:, j, 0:d.blocks, :].bitcast(F32),
                                          ALU.subtract).then_inc(lo_ready[j].sem, 1)

                    pipelined("dve", dve, split_lo, lambda d: d.dve_out)
            for t, v in value.items():
                t.base = v

        def nothing(eng, i, jj):
            pass

        def tile(a, n, T=None):
            v = a[:, bass.ds(n, 1), :] if T is None else a[:, bass.ds(n, 1), 0:T]
            return v.rearrange("p a t -> p (a t)")

        def products(eng, i, jj, half):
            j = jj % 2
            eng.wait_ge(mm_done[j].sem, i * half + jj // 2 + (mm_done[j].base + 1))

        def project(w, dst, first, chunks, T, col0, moving):
            wv = w.rearrange("(k p) c -> p k c", p=P)

            def loads(i, jj):
                return [(0, KT, wv[:, :, bass.ds(i * (2 * P) + (col0 + jj * P), P)])]

            def act_out(act, i, jj):
                products(act, i, jj, 1)
                b = 4 * BANK * jj
                act.copy(tile(dst, i * 2 + (first + jj), T), ps[:, b:b + T]).then_inc(psum_free[jj].sem, 1)

            return Dense(chunks, 2, KT, loads, [(0, 0, KT, *moving)], T, act_out, nothing)

        def residual(w, gate, chunks, moving, T, row0=0, nk=KT, before=None, adds=()):
            wv = w[row0:row0 + nk * P, :].rearrange("(k p) c -> p k c", p=P)

            def loads(i, jj):
                return [(0, nk, wv[:, :, bass.ds(i * (2 * P) + jj * P, P)])]

            def dve_out(dve, i, jj):
                products(dve, i, jj, 1)
                b = 4 * BANK * jj
                for v, (t0, tn) in enumerate(groups(T)):
                    xo = x[:, bass.ds(i * 2 + jj, 1), t0:t0 + tn].rearrange("p a t -> p (a t)")
                    m = dve.scalar_tensor_tensor(out=xo, in0=ps[:, b + t0:b + t0 + tn], scalar=mod[:, v, bass.ds(i * 2 + (gate + jj), 1)],
                                                 in1=xo, op0=ALU.mult, op1=ALU.add)
                m.then_inc(psum_free[jj].sem, 1)

            return Dense(chunks, 2, nk, loads, [(0, 0, nk, *moving)], T, nothing, dve_out, adds=adds, before=before)

        def swiglu(temps, loads, per, tiles, moving, h, T, combine=None):
            hhi, hlo = h
            sg, hf = temps
            half = per // 2
            ready = psum_free[1] if combine is None else h_scaled

            def act_out(act, i, jj):
                j, u = jj % 2, i * half + jj // 2
                if j == 0:
                    products(act, i, jj, half)
                    act.wait_ge(psum_free[1].sem, u + psum_free[1].base)
                    act.activation(sg[:], ps[:, 0:T], ACT.Silu).then_inc(psum_free[0].sem, 1)
                else:
                    act.wait_ge(ready.sem, u + (ready.base + 1))
                    act.copy(tile(hhi, u), hf[:]).then_inc(h_hi_ready.sem, 1)

            def dve_out(dve, i, jj):
                j, u = jj % 2, i * half + jj // 2
                if j == 0:
                    return
                products(dve, i, jj, half)
                dve.wait_ge(psum_free[0].sem, u + (psum_free[0].base + 1))
                dve.tensor_tensor(hf[:], sg[:], ps[:, 4 * BANK:4 * BANK + T], ALU.mult).then_inc(psum_free[1].sem, 1)
                if combine is not None:
                    dve.wait_ge(psum_free[1].sem, u + (psum_free[1].base + 1))
                    dve.tensor_tensor(hf[:], hf[:], combine(i), ALU.mult).then_inc(h_scaled.sem, 1)
                dve.wait_ge(h_hi_ready.sem, u + (h_hi_ready.base + 1))
                dve.tensor_tensor(tile(hlo, u), hf[:], tile(hhi, u).bitcast(F32), ALU.subtract).then_inc(h_ready.sem, 1)

            adds = {h_hi_ready: tiles, h_ready: tiles}
            if combine is not None:
                adds[h_scaled] = tiles
            return Dense(2 * tiles, per, KT, loads, [(0, 0, KT, *moving)], T, act_out, dve_out, adds=adds, func=ACT.Silu)

        def when_h_ready():
            return {"pe": lambda pe: pe.wait_ge(h_ready.sem, h_ready.base)}

        def new_ring(c, blocks):
            return (sb(c, "w_raw", [P, 2, blocks, P]), sb(c, "w_hi", [P, 2, blocks, P], F32R), sb(c, "w_lo", [P, 2, blocks, P], F32R))

        def split_before(src, first, hi, lo, n, T, wait=None):
            def act_part(act):
                if wait is not None:
                    act.wait_ge(wait.sem, wait.base)
                for k in range(n):
                    act.copy(hi[:, k, 0:T], src[:, first + k, 0:T]).then_inc(y_hi.sem, 1)

            def dve_part(dve):
                for k in range(n):
                    dve.wait_ge(y_hi.sem, y_hi.base + k + 1)
                    dve.tensor_tensor(lo[:, k, 0:T], src[:, first + k, 0:T], hi[:, k, 0:T].bitcast(F32), ALU.subtract).then_inc(y_ready.sem, 1)

            return {"act": act_part, "dve": dve_part, "pe": lambda pe: pe.wait_ge(y_ready.sem, y_ready.base + n)}

        def gated_branch(temps, w_gate, w_branch, moving, yhl, proj, first, T, before):
            gv = w_gate.rearrange("(k p) c -> p k c", p=P)
            bv = w_branch.rearrange("(k p) c -> p k c", p=P)
            sg, gp = temps

            def loads(i, jj):
                cols = bass.ds(i * (2 * P) + jj * P, P)
                return [(0, KT, gv[:, :, cols]), (KT, 4, bv[:, :, cols])]

            def act_out(act, i, jj):
                products(act, i, jj, 1)
                act.wait_ge(psum_free[jj].sem, i + psum_free[jj].base)
                act.activation(sg[:, jj, :], ps[:, 4 * BANK * jj:4 * BANK * jj + T], ACT.Sigmoid).then_inc(gated.sem, 1)

            def dve_out(dve, i, jj):
                b = 4 * BANK * jj + 2 * BANK
                m = tile(proj, i * 2 + (T_M + jj), T)
                dve.wait_ge(gated.sem, i * 2 + (gated.base + jj + 1))
                dve.tensor_tensor(m if first else gp[:, jj, :], sg[:, jj, :], ps[:, b:b + T], ALU.mult).then_inc(psum_free[jj].sem, 1)
                if not first:
                    dve.wait_ge(psum_free[jj].sem, i + (psum_free[jj].base + 1))
                    dve.tensor_tensor(m, m, gp[:, jj, :], ALU.add).then_inc(merged.sem, 1)

            adds = {gated: KT, y_hi: 4, y_ready: 4}
            if not first:
                adds[merged] = KT
            return Dense(KT, 2, KT + 4, loads, [(0, 0, KT, *moving), (2 * BANK, KT, 4, *yhl)], T, act_out, dve_out,
                         adds=adds, before=before, func=ACT.Sigmoid)

        rpb_rows = [nc.dram_tensor(f"rpb_rows_{l}", [HEADS, 15, GRID_W, P], F32) for l in range(DEPTH)]

        def write_rpb_rows(sp, l):
            sp.dma_start(rpb[:, 48:79], g["na_rpb"][l].rearrange("h r c -> (h r) c")).then_inc(ld[2].sem, 16)
            sp.wait_ge(ld[2].sem, ld[2].base + 16)
            sp.dma_start(rpb_rows[l][:].rearrange("h r w c -> (h r) w c"), rpb[:].unsqueeze(1).to_broadcast([HEADS * 15, GRID_W, P])).then_inc(ld[3].sem, 16)
            sp.wait_ge(ld[3].sem, ld[3].base + 16)

        def fourier(proj, t0, T, seq, chan, rpb_layer=None):
            nt = T // P
            with ExitStack() as c:
                dseq = sb(c, "dft_seq", [P, nt, 2, T])
                dch = sb(c, "dft_chan", [P, 2 * P])
                u = sb(c, "dft_u", [P, 4, nt, 2 * P])
                block = c.enter_context(nc.Block())

                @block.sync
                def _(sp):
                    sp.dma_start(dch[:], chan).then_inc(ld[0].sem, 16)
                    sp.dma_start(dseq[:], seq.rearrange("(k p) s n -> p k s n", p=P)).then_inc(ld[1].sem, 16)
                    if rpb_layer is not None:
                        write_rpb_rows(sp, rpb_layer)

                @block.tensor
                def _(pe):
                    def channels(gr):
                        if gr >= 2:
                            pe.wait_ge(act_chain.sem, act_chain.base + gr - 1)
                        for n in range(nt):
                            b = 2 * BANK * (gr % 2) + n * 2 * P
                            m = pe.matmul(ps[:, b:b + 2 * P], proj[:, T_F + gr, t0 + n * P:t0 + (n + 1) * P], dch[:], start=True, stop=True)
                        m.then_inc(pe_chain.sem, 1)

                    def tokens(gr):
                        pe.wait_ge(act_chain.sem, act_chain.base + gr + 1)
                        if gr >= 2:
                            pe.wait_ge(dve_chain.sem, dve_chain.base + gr - 1)
                        o = ps[:, BANK * (4 + gr % 2):BANK * (4 + gr % 2) + T]
                        for n in range(nt):
                            for s in range(2):
                                m = pe.matmul(o, u[:, gr, n, s * P:(s + 1) * P], dseq[:, n, s, :], start=(n + s == 0), stop=(n == nt - 1 and s == 1))
                        m.then_inc(norm_var.sem, 1)

                    pe.wait_ge(ld[0].sem, ld[0].base + 16)
                    channels(0)
                    pe.wait_ge(ld[1].sem, ld[1].base + 16)
                    for gr in range(4):
                        if gr < 3:
                            channels(gr + 1)
                        tokens(gr)

                @block.scalar
                def _(act):
                    for gr in range(4):
                        act.wait_ge(pe_chain.sem, pe_chain.base + gr + 1)
                        b = 2 * BANK * (gr % 2)
                        act.copy(u[:, gr].rearrange("p n c -> p (n c)"), ps[:, b:b + nt * 2 * P]).then_inc(act_chain.sem, 1)

                @block.vector
                def _(dve):
                    for gr in range(4):
                        dve.wait_ge(norm_var.sem, norm_var.base + gr + 1)
                        b = BANK * (4 + gr % 2)
                        dve.tensor_copy(proj[:, T_Y[0] + gr, t0:t0 + T], ps[:, b:b + T]).then_inc(dve_chain.sem, 1)
            for t in (pe_chain, act_chain, dve_chain, norm_var):
                t.base += 4
            if rpb_layer is not None:
                ld[2].base += 16
                ld[3].base += 16
            ld[0].base += 16
            ld[1].base += 16

        def attend(c, pairs, q_tiles, spans, key_tiles, q_of, k_of, v_of, out_of, scale, prep,
                   look=2, bias=None, sink=None, v_need=None):
            NT = q_tiles
            width = max(len(key_tiles(t)) for t in range(NT))
            full = all(key_tiles(t) == key_tiles(0) for t in range(NT))
            prob = sb(c, "prob", [P, 2, width * P])
            probT = sb(c, "probT", [P, width, NT * P])
            nm = sb(c, "nm", [P, 2, 4])
            es = sb(c, "sink_e", [P, 2, 1])
            U = 2 * NT

            def unit(i, j, t):
                return i * U + (j * NT + t)

            def following(i, j, t, ahead):
                n = j * NT + t + ahead
                return (i, n // NT, n % NT) if n < U else (i + 1, (n - U) // NT, (n - U) % NT)

            def exists(i, j, t, ahead, last):
                return not (last and j * NT + t + ahead >= U)

            def scores_at(u_static):
                return 2 * BANK * (u_static % 2)

            def run(eng, who, prologue, step, end, chain, per):
                prologue()
                if pairs > 1:
                    with eng.Fori(0, pairs - 1) as i:
                        chain.open(i, per)
                        for j in range(2):
                            for t in range(NT):
                                step(i, j, t, False)
                        end(i)
                        chain.close(pairs - 1)
                for j in range(2):
                    for t in range(NT):
                        step(pairs - 1, j, t, True)
                end(pairs - 1)
                chain.done()

            def pe_program(pe, per=0):
                ch = Chain(pe, pe_chain)

                def scores(i, j, t, first=False):
                    if t == 0:
                        prep.ready(pe, i, j)
                    if not first:
                        pe.wait_ge(p_done.sem, unit(i, j, t) + (p_done.base - 1))
                    b = scores_at(j * NT + t)
                    for c0, cn, k0 in spans(t):
                        m = pe.matmul(ps[:, b + c0:b + c0 + cn], q_of(j, t), k_of(j, k0, cn), start=True, stop=True)
                    m.then_inc(s_done.sem, 1)

                def turn(i, j, t):
                    u = unit(i, j, t)
                    pe.wait_ge(pn_done.sem, u + (pn_done.base + 1))
                    pe.wait_ge(pt_done.sem, u + pt_done.base)
                    for b in range(len(key_tiles(t))):
                        m = pe.transpose(ps[:, 4 * BANK + b * P:4 * BANK + (b + 1) * P], prob[:, (j * NT + t) % 2, b * P:(b + 1) * P], ident[:])
                    m.then_inc(t_done.sem, 1)

                def values(i, j):
                    h = i * 2 + j
                    pe.wait_ge(pt_done.sem, i * U + (pt_done.base + (j + 1) * NT))
                    pe.wait_ge(o_done.sem, h + o_done.base)
                    prep.v_ready(pe, i, j)
                    o = ps[64 * j:64 * j + HD, 6 * BANK:6 * BANK + NT * P]
                    if full:
                        kts = key_tiles(0)
                        for b, kt in enumerate(kts):
                            m = pe.matmul(o, v_of(j, kt), probT[:, b, :], start=(b == 0), stop=(b == len(kts) - 1))
                    else:
                        for t in range(NT):
                            kts = key_tiles(t)
                            for b, kt in enumerate(kts):
                                m = pe.matmul(o[:, t * P:(t + 1) * P], v_of(j, kt), probT[:, b, t * P:(t + 1) * P], start=(b == 0), stop=(b == len(kts) - 1))
                    m.then_inc(pv_done.sem, 1)

                def prologue():
                    prep("pe", pe, ch, 0, 0, None)
                    for a in range(look):
                        scores(*following(0, 0, 0, a), first=True)

                def step(i, j, t, last):
                    if exists(i, j, NT - 1, 1, last):
                        prep("pe", pe, ch, *following(i, j, NT - 1, 1)[:2], t)
                    if exists(i, j, t, look, last):
                        scores(*following(i, j, t, look))
                    if j == 1 and t == 0:
                        values(i, 0)
                    turn(i, j, t)

                run(pe, "pe", prologue, step, lambda i: values(i, 1), ch, per)

            def dve_program(dve, per):
                ch = Chain(dve, dve_chain)

                def maximum(i, j, t):
                    u = unit(i, j, t)
                    dve.wait_ge(s_done.sem, u + (s_done.base + 1))
                    slot = (j * NT + t) % 2
                    n = len(key_tiles(t)) * P
                    s = ps[:, scores_at(slot):scores_at(slot) + n]
                    if bias:
                        bias.chain = ch
                        ch.link(bias(dve, i, j, t, s))
                    ch.link(dve.reduce_max(nm[:, slot, 0:1], s, AX))
                    if sink:
                        ch.link(dve.tensor_tensor(nm[:, slot, 0:1], nm[:, slot, 0:1], sink(i, j), ALU.max))
                    dve.tensor_scalar(nm[:, slot, 1:2], nm[:, slot, 0:1], -scale, None, ALU.mult).then_inc(nm_done.sem, 1)

                def normalised(i, j, t):
                    u = unit(i, j, t)
                    slot = (j * NT + t) % 2
                    n = len(key_tiles(t)) * P
                    dve.wait_ge(p_done.sem, u + (p_done.base + 1))
                    if sink:
                        ch.link(dve.tensor_tensor(nm[:, slot, 2:3], nm[:, slot, 2:3], es[:, slot, :], ALU.add))
                    ch.link(dve.reciprocal(nm[:, slot, 3:4], nm[:, slot, 2:3]))
                    dve.tensor_scalar(prob[:, slot, 0:n], prob[:, slot, 0:n], nm[:, slot, 3:4], None, ALU.mult).then_inc(pn_done.sem, 1)

                def output(i, j):
                    dve.wait_ge(pv_done.sem, i * 2 + (pv_done.base + j + 1))
                    dve.tensor_copy(out_of(i, j), ps[64 * j:64 * j + HD, 6 * BANK:6 * BANK + NT * P]).then_inc(o_done.sem, 1)

                def prologue():
                    prep("dve", dve, ch, 0, 0, None)
                    maximum(0, 0, 0)

                def step(i, j, t, last):
                    if exists(i, j, NT - 1, 1, last):
                        prep("dve", dve, ch, *following(i, j, NT - 1, 1)[:2], t)
                    if exists(i, j, t, 1, last):
                        maximum(*following(i, j, t, 1))
                    normalised(i, j, t)
                    if j == 1 and t == 0:
                        output(i, 0)

                run(dve, "dve", prologue, step, lambda i: output(i, 1), ch, per)

            def act_program(act, per=0):
                ch = Chain(act, act_chain)

                def exps(i, j, t, first=False):
                    u = unit(i, j, t)
                    slot = (j * NT + t) % 2
                    n = len(key_tiles(t)) * P
                    act.wait_ge(nm_done.sem, u + (nm_done.base + 1))
                    if not first:
                        act.wait_ge(t_done.sem, u + (t_done.base - 1))
                    if sink:
                        act.activation(es[:, slot, :], sink(i, j), ACT.Exp, bias=nm[:, slot, 1:2])
                    act.activation(prob[:, slot, 0:n], ps[:, scores_at(slot):scores_at(slot) + n], ACT.Exp, bias=nm[:, slot, 1:2],
                                   scale=scale, accum_out=nm[:, slot, 2:3]).then_inc(p_done.sem, 1)

                def copied(i, j, t):
                    u = unit(i, j, t)
                    nb = len(key_tiles(t))
                    act.wait_ge(t_done.sem, u + (t_done.base + 1))
                    if t == 0:
                        act.wait_ge(pv_done.sem, i * 2 + (pv_done.base + j))
                    act.copy(probT[:, 0:nb, t * P:(t + 1) * P], ps[:, 4 * BANK:4 * BANK + nb * P].rearrange("p (b n) -> p b n", n=P)).then_inc(pt_done.sem, 1)

                def prologue():
                    prep("act", act, ch, 0, 0, None)
                    exps(0, 0, 0, first=True)

                def step(i, j, t, last):
                    if exists(i, j, NT - 1, 1, last):
                        prep("act", act, ch, *following(i, j, NT - 1, 1)[:2], t)
                    if exists(i, j, t, 1, last):
                        exps(*following(i, j, t, 1))
                    copied(i, j, t)

                run(act, "act", prologue, step, lambda i: None, ch, per)

            def ended():
                for t in (s_done, nm_done, p_done, pn_done, t_done, pt_done):
                    t.base += pairs * U
                for t in (pv_done, o_done):
                    t.base += 2 * pairs
                for t in (pe_chain, dve_chain, act_chain):
                    finish(t)

            return pe_program, dve_program, act_program, ended

        class Staged:

            def __init__(self, qk, v, q_tiles):
                self.qk, self.v, self.q_tiles = qk, v, q_tiles

            def __call__(self, who, eng, ch, i, j, t):
                pass

            def ready(self, pe, i, j):
                pe.wait_ge(qk_staged.sem, i * (2 * len(self.qk)) + (qk_staged.base + (j + 1) * len(self.qk)))

            def v_ready(self, pe, i, j):
                if self.v:
                    pe.wait_ge(v_staged.sem, i * 2 + (v_staged.base + j + 1))

            def stage_qk(self, pool, i, j):
                n = len(self.qk)
                for a, f in enumerate(self.qk):
                    f(pool, i, j).then_inc(qk_staged.sem, 1)
                    pool.wait_ge(qk_staged.sem, i * (2 * n) + (qk_staged.base + j * n + a + 1))

            def stage_v(self, pool, i, j):
                self.v[0](pool, i, j).then_inc(v_staged.sem, 1)
                pool.wait_ge(v_staged.sem, i * 2 + (v_staged.base + j + 1))

            def program(self, pool, pairs):
                NT = self.q_tiles

                def stage(i, j, first):
                    if not first:
                        pool.wait_ge(s_done.sem, i * (2 * NT) + (s_done.base + (j - 1) * NT))
                    self.stage_qk(pool, i, j)
                    if self.v:
                        if not first:
                            pool.wait_ge(pv_done.sem, i * 2 + (pv_done.base + j - 1))
                        self.stage_v(pool, i, j)

                for j in range(2):
                    stage(0, j, True)
                if pairs > 1:
                    with pool.Fori(1, pairs) as i:
                        for j in range(2):
                            stage(i, j, False)

            def ended(self, pairs):
                qk_staged.base += 2 * pairs * len(self.qk)
                v_staged.base += 2 * pairs if self.v else 0

        def token_major(proj, first, n, T, dst):
            nt = T // P
            with ExitStack() as c:
                block = c.enter_context(nc.Block())

                @block.tensor
                def _(pe):
                    for t in range(nt):
                        if t >= 4:
                            pe.wait_ge(act_chain.sem, act_chain.base + t - 3)
                        for k in range(n):
                            b = BANK * (t % 4) + k * P
                            m = pe.transpose(ps[:, b:b + P], proj[:, first + k, t * P:(t + 1) * P], ident[:])
                        m.then_inc(pe_chain.sem, 1)

                @block.scalar
                def _(act):
                    for t in range(nt):
                        act.wait_ge(pe_chain.sem, pe_chain.base + t + 1)
                        act.copy(dst[:, t, :], ps[:, BANK * (t % 4):BANK * (t % 4) + n * P]).then_inc(act_chain.sem, 1)
            pe_chain.base += nt
            act_chain.base += nt

        def neighbourhood(proj, l, with_ctx):
            with ExitStack() as c:
                vt = sb(c, "na_v", [P, 6, NA_W])
                token_major(proj, T_NV, 4, ALL, vt)
                qs = sb(c, "na_qs", [P, 2, LAT])
                ks = sb(c, "na_ks", [P, 2, ALL])
                vs = sb(c, "na_vs", [P, 2, 6, HD])
                bt = sb(c, "na_bias", [P, 2, 14, GRID_W])
                def half(a, j):
                    return a[64 * j:64 * j + HD]

                def stage_q(tok, n):
                    return lambda pool, i, j: pool.tensor_tensor(half(qs, j)[:, j, 0:n], tile(half(proj, j), i + T_NQ)[:, tok:tok + n],
                                                                 half(scale_row, j).to_broadcast([HD, n]), ALU.mult)

                def stage_k(tok, n):
                    return lambda pool, i, j: pool.tensor_copy(half(ks, j)[:, j, 0:n], tile(half(proj, j), i + T_NK)[:, tok:tok + n])

                def stage_v(kt0, n):
                    return lambda pool, i, j: pool.tensor_copy(vs[:, j, 0:n, :], vt[:, kt0:kt0 + n, bass.ds(i * P + j * HD, HD)])

                def q_of(j, t):
                    return half(qs, j)[:, j, t * P:(t + 1) * P]

                def k_of(j, k0, n):
                    return half(ks, j)[:, j, k0:k0 + n]

                v_of = lambda j, kt: vs[:, j, kt, :]

                with ExitStack() as c1:
                    def bias(dve, i, j, t, s):
                        if t == 0:
                            dve.wait_ge(bias_masked.sem, i * 2 + (bias_masked.base + j + 1))
                        e = ROWS - 2 - 2 * t
                        return dve.tensor_tensor(s[:, 0:LAT], s[:, 0:LAT], bt[:, j, e:e + KH, :].rearrange("p r w -> p (r w)"), ALU.add)

                    prep = Staged([stage_q(0, LAT), stage_k(0, ALL)], [stage_v(0, 6)], 4)
                    pe_p, dve_p, act_p, ended = attend(
                        c1, 4, 4, lambda t: [(0, LAT, 0), (LAT, CTX, LAT)], lambda t: list(range(6)), q_of, k_of, v_of,
                        lambda i, j: tile(half(proj, j), i + T_Y[1], LAT), 1.0, prep, bias=bias)
                    block = c1.enter_context(nc.Block())

                    @block.sync
                    def _(sp):
                        def load(i, j, first):
                            if not first:
                                sp.wait_ge(nm_done.sem, i * 8 + (nm_done.base + (j - 1) * 4))
                            for r in range(2):
                                R = GRID_W * P
                                src = bass.AP(tensor=rpb_rows[l], offset=i * (2 * 15 * R) + (j * 15 * R + (1 - r) * R + GRID_W - 1),
                                              ap=[[P - 1, GRID_W], [R, 14], [1, GRID_W]])
                                sp.dma_start(bt[64 * r:64 * r + 64, j], src).then_inc(head_w[j].sem, 16)

                        for j in range(2):
                            load(0, j, True)
                        with sp.Fori(1, 4) as i:
                            for j in range(2):
                                load(i, j, False)

                    @block.gpsimd
                    def _(pool):
                        NT = 4

                        def one(i, j, first):
                            if not first:
                                pool.wait_ge(s_done.sem, i * (2 * NT) + (s_done.base + (j - 1) * NT))
                            prep.stage_qk(pool, i, j)
                            pool.wait_ge(head_w[j].sem, i * 32 + (head_w[j].base + 32))
                            pool.tensor_tensor(bt[:, j], bt[:, j], na_mask[:].unsqueeze(1).to_broadcast([P, 14, GRID_W]), ALU.add).then_inc(bias_masked.sem, 1)
                            pool.wait_ge(bias_masked.sem, i * 2 + (bias_masked.base + j + 1))
                            if not first:
                                pool.wait_ge(pv_done.sem, i * 2 + (pv_done.base + j - 1))
                            prep.stage_v(pool, i, j)

                        for j in range(2):
                            one(0, j, True)
                        with pool.Fori(1, 4) as i:
                            for j in range(2):
                                one(i, j, False)

                    @block.tensor
                    def _(pe):
                        pe_p(pe)

                    @block.vector
                    def _(dve):
                        dve_p(dve, 8 * 3)

                    @block.scalar
                    def _(act):
                        act_p(act)
                ended()
                prep.ended(4)
                bias_masked.base += 8
                for j in range(2):
                    head_w[j].base += 4 * 32

                if with_ctx:
                    with ExitStack() as c1:
                        prep = Staged([stage_q(LAT, CTX), stage_k(LAT, CTX)], [stage_v(4, 2)], 2)
                        pe_p, dve_p, act_p, ended = attend(
                            c1, 4, 2, lambda t: [(0, CTX, 0)], lambda t: [0, 1], q_of, k_of, v_of,
                            lambda i, j: tile(half(proj, j), i + T_Y[1])[:, LAT:ALL], 1.0, prep, look=2)
                        simple_attention(c1, prep, 4, pe_p, dve_p, act_p, 4 * 2)
                    ended()
                    prep.ended(4)

        def simple_attention(c1, prep, pairs, pe_p, dve_p, act_p, per):
            block = c1.enter_context(nc.Block())

            @block.gpsimd
            def _(pool):
                prep.program(pool, pairs)

            @block.tensor
            def _(pe):
                pe_p(pe)

            @block.vector
            def _(dve):
                dve_p(dve, per)

            @block.scalar
            def _(act):
                act_p(act)

        class Latent:

            def __init__(self, pieces, at):
                self.pieces, self.at = pieces, at

            def which(self, t):
                return range(len(self.pieces)) if t is None else [n for n, a in enumerate(self.at) if a == t]

            def __call__(self, who, eng, ch, i, j, t):
                n = len(self.pieces)
                for p in self.which(t):
                    mm, on, copies = self.pieces[p]
                    before = i * (2 * n) + (j * n + p)
                    if who == "pe":
                        if p == 0:
                            eng.wait_ge(head_w[j].sem, i * 80 + (head_w[j].base + 80))
                        eng.wait_ge(prep_out.sem, before + prep_out.base)
                        mm(eng, j).then_inc(prep_mm.sem, 1)
                    elif who == on:
                        eng.wait_ge(prep_mm.sem, before + (prep_mm.base + 1))
                        copies(eng, ch, j)

            def ready(self, pe, i, j):
                n = len(self.pieces)
                pe.wait_ge(prep_out.sem, i * (2 * n) + (prep_out.base + (j + 1) * n))
                pe.wait_ge(prep_rope.sem, i * 2 + (prep_rope.base + j + 1))

            def v_ready(self, pe, i, j):
                pe.wait_ge(v_staged.sem, i * 2 + (v_staged.base + j + 1))

        def latent_attention(proj, l, with_ctx):
            with ExitStack() as c:
                gain = vec3
                T = ALL if with_ctx else LAT
                normalize([proj[:, T_CQ + k, 0:T] for k in range(2)], T, LN_EPS, lambda k: col(gain, V3_QN + 2 * l + k))
                normalize([proj[:, T_CKV, :]], ALL, LN_EPS, lambda k: col(gain, V3_KVN + l))
                wq = sb(c, "mla_wq", [P, 2, 2, P])
                wk = sb(c, "mla_wk", [P, 2, HD])
                wv = sb(c, "mla_wv", [P, HEADS * HD])
                vt = sb(c, "mla_vt", [P, 6, HEADS * HD])
                q = sb(c, "mla_q", [P, 2, LAT])
                k = sb(c, "mla_k", [P, 2, ALL])
                v = sb(c, "mla_v", [P, 2, 6, HD])
                ra = sb(c, "mla_ra", [P, LAT])
                rb = sb(c, "mla_rb", [P, LAT])
                rope = sb(c, "mla_rope", [P, LAT])
                spread = sb(c, "mla_spread", [ROPE, P])
                R0, R1, R2 = HD, HD + ROPE, HD + 2 * ROPE

                with ExitStack() as c1:
                    block = c1.enter_context(nc.Block())

                    @block.sync
                    def _(sp):
                        sp.dma_start(rope[:], g["k_rope"]).then_inc(ld[0].sem, 16)
                        sp.dma_start(spread[:], g["k_spread"]).then_inc(ld[1].sem, 16)
                        sp.dma_start(wv[:], g["w_uv"][l]).then_inc(ld[2].sem, 16)

                    @block.tensor
                    def _(pe):
                        pe.wait_ge(ld[1].sem, ld[1].base + 16)
                        for t0, tn in groups(ALL):
                            m = pe.matmul(ps[:, t0:t0 + tn], spread[:], proj[0:ROPE, T_KR, t0:t0 + tn], start=True, stop=True)
                        m.then_inc(pe_chain.sem, 1)
                        pe.wait_ge(ld[2].sem, ld[2].base + 16)
                        for t in range(6):
                            pe.matmul(ps[:, BANK * (2 + t):BANK * (3 + t)], proj[:, T_CKV, t * P:(t + 1) * P], wv[:], start=True, stop=True).then_inc(pe_chain.sem, 1)

                    @block.scalar
                    def _(act):
                        for t in range(6):
                            act.wait_ge(pe_chain.sem, pe_chain.base + 2 + t)
                            act.copy(vt[:, t, :], ps[:, BANK * (2 + t):BANK * (3 + t)])

                    @block.vector
                    def _(dve):
                        ch = Chain(dve, dve_chain)
                        dve.wait_ge(pe_chain.sem, pe_chain.base + 1)
                        dve.wait_ge(ld[0].sem, ld[0].base + 16)
                        dve.tensor_tensor(ra[R0:R1, :], ps[R0:R1, 0:LAT], rope[R0:R1, :], ALU.mult)
                        ch.link(dve.tensor_tensor(rb[R0:R1, :], ps[R1:R2, 0:LAT], rope[R1:R2, :], ALU.mult))
                        for j in range(2):
                            dve.tensor_tensor(k[R0:R1, j, 0:LAT], ra[R0:R1, :], rb[R0:R1, :], ALU.add)
                            dve.tensor_copy(k[R0:R1, j, LAT:ALL], ps[R0:R1, LAT:ALL])
                        ch.done()
                finish(dve_chain)
                pe_chain.base += 7
                for n in range(3):
                    ld[n].base += 16

                bank = 7 * BANK

                def run(q_tiles, tok, nk, kt0, rotate, pieces, at, look, links_per_prep, out_of):
                    prep = Latent(pieces, at)
                    with ExitStack() as c1:
                        pe_p, dve_p, act_p, ended = attend(
                            c1, 4, q_tiles,
                            (lambda t: [(0, LAT, 0), (LAT, CTX, LAT)]) if nk == ALL else (lambda t: [(0, CTX, LAT)]),
                            lambda t: list(range(nk // P)), lambda j, t: q[0:MLA_K, j, t * P:(t + 1) * P],
                            lambda j, k0, n: k[0:MLA_K, j, k0:k0 + n], lambda j, kt: v[:, j, kt, :],
                            out_of, MLA_SCALE, prep, look=look)
                        block = c1.enter_context(nc.Block())

                        @block.sync
                        def _(sp):
                            uq = g["w_uq"][l].rearrange("(k p) c -> p k c", p=P)
                            qr = g["w_qr"][l].rearrange("(k p) c -> p k c", p=P)

                            def load(i, j, first):
                                if not first:
                                    sp.wait_ge(prep_mm.sem, i * (2 * len(pieces)) + (prep_mm.base + (j - 1) * len(pieces)))
                                s = head_w[j].sem
                                h64 = lambda o, n: bass.ds(i * P + (j * HD + o), n)
                                h32 = lambda o, n: bass.ds(i * (2 * ROPE) + (j * ROPE + o), n)
                                sp.dma_start(wq[:, j, :, 0:R0], uq[:, :, h64(0, HD)]).then_inc(s, 16)
                                sp.dma_start(wq[:, j, :, R0:R1], qr[:, :, h32(0, ROPE)]).then_inc(s, 16)
                                sp.dma_start(wq[:, j, :, R1:R1 + 16], qr[:, :, h32(16, 16)]).then_inc(s, 16)
                                sp.dma_start(wq[:, j, :, R1 + 16:R2], qr[:, :, h32(0, 16)]).then_inc(s, 16)
                                sp.dma_start(wk[:, j, :], g["w_uk"][l][:, h64(0, HD)]).then_inc(s, 16)

                            for j in range(2):
                                load(0, j, True)
                            with sp.Fori(1, 4) as i:
                                for j in range(2):
                                    load(i, j, False)

                        @block.gpsimd
                        def _(pool):
                            def stage_v(i, j, first):
                                if not first:
                                    pool.wait_ge(pv_done.sem, i * 2 + (pv_done.base + j - 1))
                                pool.tensor_copy(v[:, j, 0:nk // P, :], vt[:, kt0:kt0 + nk // P, bass.ds(i * P + j * HD, HD)]).then_inc(v_staged.sem, 1)
                                pool.wait_ge(v_staged.sem, i * 2 + (v_staged.base + j + 1))

                            for j in range(2):
                                stage_v(0, j, True)
                            with pool.Fori(1, 4) as i:
                                for j in range(2):
                                    stage_v(i, j, False)

                        @block.tensor
                        def _(pe):
                            pe_p(pe)

                        @block.vector
                        def _(dve):
                            dve_p(dve, 2 * q_tiles * 2 + 2 * links_per_prep)

                        @block.scalar
                        def _(act):
                            act_p(act)
                    ended()
                    prep_out.base += 8 * len(pieces)
                    prep_mm.base += 8 * len(pieces)
                    prep_rope.base += 8
                    v_staged.base += 8
                    for j in range(2):
                        head_w[j].base += 4 * 80

                def mm_q(tok, n):
                    def f(pe, j):
                        for kk in range(2):
                            m = pe.matmul(ps[:, bank:bank + n], wq[:, j, kk, :], proj[:, T_CQ + kk, tok:tok + n], start=(kk == 0), stop=(kk == 1))
                        return m
                    return f

                def mm_k(tok, n):
                    return lambda pe, j: pe.matmul(ps[0:HD, bank:bank + n], wk[:, j, :], proj[:, T_CKV, tok:tok + n], start=True, stop=True)

                def out_q_rotated(dve, ch, j):
                    dve.tensor_copy(q[0:HD, j, :], ps[0:HD, bank:bank + LAT])
                    dve.tensor_tensor(ra[R0:R1, :], ps[R0:R1, bank:bank + LAT], rope[R0:R1, :], ALU.mult)
                    ch.link(dve.tensor_tensor(rb[R0:R1, :], ps[R1:R2, bank:bank + LAT], rope[R1:R2, :], ALU.mult))
                    dve.sem_inc(prep_out.sem, 1)
                    dve.tensor_tensor(q[R0:R1, j, :], ra[R0:R1, :], rb[R0:R1, :], ALU.add).then_inc(prep_rope.sem, 1)

                def out_q_plain(dve, ch, j):
                    ch.link(dve.tensor_copy(q[0:MLA_K, j, 0:CTX], ps[0:MLA_K, bank:bank + CTX]))
                    dve.sem_inc(prep_out.sem, 1)
                    dve.sem_inc(prep_rope.sem, 1)

                def out_k(tok, n):
                    return lambda act, ch, j: act.copy(k[0:HD, j, tok:tok + n], ps[0:HD, bank:bank + n]).then_inc(prep_out.sem, 1)

                def half(a, j):
                    return a[64 * j:64 * j + HD]

                run(4, 0, ALL, 0, True,
                    [(mm_q(0, LAT), "dve", out_q_rotated), (mm_k(0, LAT), "act", out_k(0, LAT)), (mm_k(LAT, CTX), "act", out_k(LAT, CTX))],
                    (0, 0, 1), 2, 1, lambda i, j: tile(half(proj, j), i + T_Y[2], LAT))
                if with_ctx:
                    run(2, LAT, CTX, 4, False,
                        [(mm_q(LAT, CTX), "dve", out_q_plain), (mm_k(LAT, CTX), "act", out_k(LAT, CTX))],
                        (0, 0), 2, 1, lambda i, j: tile(half(proj, j), i + T_Y[2])[:, LAT:ALL])

        def modulate_by(s):
            return (lambda v, k: mod[:, v, (s + 1) * KT + k:(s + 1) * KT + k + 1]), (lambda v, k: mod[:, v, s * KT + k:s * KT + k + 1])

        def xt(T):
            return [x[:, k, 0:T] for k in range(KT)]

        def layer(l, ahi, alo):
            last = l == DEPTH - 1
            T = LAT if last else ALL
            w_in = g["w_in"][l]
            with ExitStack() as c:
                proj = sb(c, "proj", [P, 20, ALL])
                with ExitStack() as c1:
                    run_dense(new_ring(c1, KT), [project(w_in, proj, first, n, t, first * P, (ahi, alo))
                                                 for first, n, t in ((T_F, 8, T), (T_NK, 8, ALL), (T_CQ, 2, T), (T_CKV, 2, ALL))])
                fourier(proj, 0, LAT, g["k_dft_lat"], g["k_dft_chan"], rpb_layer=l)
                if not last:
                    fourier(proj, LAT, CTX, g["k_dft_ctx"], g["k_dft_chan"])
                neighbourhood(proj, l, not last)
                latent_attention(proj, l, not last)
                with ExitStack() as c1:
                    y = (sb(c1, "yhi", [P, 4, T], F32R), sb(c1, "ylo", [P, 4, T], F32R))
                    temps = (sb(c1, "sg", [P, 2, T]), sb(c1, "gp", [P, 2, T]))
                    run_dense(new_ring(c1, KT + 4), [
                        gated_branch(temps, w_in[:, GATE_COL + b * D:GATE_COL + (b + 1) * D], g["w_branch"][l, b], (ahi, alo), y, proj, b == 0, T,
                                     split_before(proj, T_Y[b], *y, 4, T)) for b in range(3)
                    ] + [residual(g["w_out"][l], 2 * KT, KT, (ahi, alo), T, before=split_before(proj, T_M, ahi, alo, KT, T, wait=merged),
                                  adds={y_hi: KT, y_ready: KT})])
            g1, b1 = V_LN1_G + l * KT, V_LN1_B + l * KT
            normalize(xt(T), T, LN_EPS, lambda k: col(vec1, g1 + k), lambda k: col(vec1, b1 + k), center=True,
                      post=(ahi, alo, *modulate_by(3)), after=ALPHA)
            NH = FFN // P // 2
            with ExitStack() as c:
                h = (sb(c, "hhi", [P, NH, T], F32R), sb(c, "hlo", [P, NH, T], F32R))
                temps = (sb(c, "sg", [P, T]), sb(c, "hf", [P, T]))
                views = [g[n][l].rearrange("(k p) c -> p k c", p=P) for n in ("w_ffn_gate", "w_ffn_up")]
                layers = []
                for half in range(2):
                    def loads(i, jj, half=half):
                        return [(0, KT, views[jj][:, :, bass.ds(i * P + half * NH * P, P)])]

                    layers += [swiglu(temps, loads, 2, NH, (ahi, alo), h, T),
                               residual(g["w_ffn_down"][l], 5 * KT, KT, h, T, row0=half * NH * P, nk=NH, before=when_h_ready())]
                run_dense(new_ring(c, NH), layers)
            if not last:
                modulation(g["w_mod"][l + 1], (0, 1), vec2[:, (l + 1) * 48:(l + 2) * 48], 2)
            g2, b2 = V_LN2_G + l * KT, V_LN2_B + l * KT
            normalize(xt(T), T, LN_EPS, lambda k: col(vec1, g2 + k), lambda k: col(vec1, b2 + k), center=True,
                      post=None if last else (ahi, alo, *modulate_by(0)), after=ALPHA)


        def narrow(c, name, sources, n, ahi, alo):
            o = sb(c, name, [P, 4, n])
            with ExitStack() as c1:
                w = sb(c1, "nw", [P, KT, n])
                whi = sb(c1, "nw_hi", [P, KT, n], F32R)
                wlo = sb(c1, "nw_lo", [P, KT, n], F32R)
                block = c1.enter_context(nc.Block())

                @block.sync
                def _(sp):
                    at = 0
                    for src, m in sources:
                        sp.dma_start(w[:, :, at:at + m], src.rearrange("(k p) c -> p k c", p=P)).then_inc(ld[0].sem, 16)
                        at += m

                @block.scalar
                def _(act):
                    act.wait_ge(ld[0].sem, ld[0].base + 16 * len(sources))
                    act.copy(whi[:], w[:]).then_inc(act_chain.sem, 1)

                @block.vector
                def _(dve):
                    dve.wait_ge(act_chain.sem, act_chain.base + 1)
                    dve.tensor_tensor(wlo[:], w[:], whi[:].bitcast(F32), ALU.subtract).then_inc(dve_chain.sem, 1)
                    dve.wait_ge(pe_chain.sem, pe_chain.base + 1)
                    dve.tensor_copy(o[:], ps[:, 0:4 * n].rearrange("p (t n) -> p t n", n=n))

                @block.tensor
                def _(pe):
                    pe.wait_ge(dve_chain.sem, dve_chain.base + 1)
                    for t in range(4):
                        for k in range(KT):
                            tok = slice(t * P, (t + 1) * P)
                            out_ = ps[:, t * n:(t + 1) * n]
                            pe.matmul(out_, ahi[:, k, tok], whi[:, k, :], start=(k == 0), stop=False)
                            pe.matmul(out_, alo[:, k, tok], whi[:, k, :], start=False, stop=False)
                            m = pe.matmul(out_, ahi[:, k, tok], wlo[:, k, :], start=False, stop=(k == KT - 1))
                    m.then_inc(pe_chain.sem, 1)
            ld[0].base += 16 * len(sources)
            for t in (act_chain, dve_chain, pe_chain):
                t.base += 1
            return o

        def softplus_neg(c, n, load):
            dst = sb(c, "softplus", [P, n])
            with ExitStack() as c1:
                neg, e, z, z2, acc = (sb(c1, s, [P, n]) for s in ("sp_neg", "sp_e", "sp_z", "sp_z2", "sp_acc"))
                block = c1.enter_context(nc.Block())

                @block.vector
                def _(dve):
                    ch = Chain(dve, dve_chain)
                    load(dve, ch, neg)
                    ch.link(dve.tensor_scalar(z[:], neg[:], -1.0, None, ALU.mult))
                    ch.link(dve.tensor_tensor(e[:], neg[:], z[:], ALU.min))
                    pe_n = ch.value()
                    dve.wait_ge(act_chain.sem, act_chain.base + 1)
                    ch.link(dve.tensor_scalar(z2[:], e[:], 2.0, None, ALU.add))
                    ch.link(dve.reciprocal(z2[:], z2[:]))
                    ch.link(dve.tensor_tensor(z[:], e[:], z2[:], ALU.mult))
                    ch.link(dve.tensor_tensor(z2[:], z[:], z[:], ALU.mult))
                    ch.link(dve.tensor_scalar(acc[:], z2[:], 1.0 / 17, 1.0 / 15, ALU.mult, ALU.add))
                    for d in (13, 11, 9, 7, 5, 3, 1):
                        ch.link(dve.tensor_tensor(acc[:], acc[:], z2[:], ALU.mult))
                        ch.link(dve.tensor_scalar(acc[:], acc[:], 1.0 / d, None, ALU.add))
                    ch.link(dve.tensor_tensor(acc[:], acc[:], z[:], ALU.mult))
                    ch.link(dve.tensor_scalar(neg[:], neg[:], 0.0, None, ALU.max))
                    ch.mark(dve.scalar_tensor_tensor(out=dst[:], in0=acc[:], scalar=2.0, in1=neg[:], op0=ALU.mult, op1=ALU.add))
                    ch.done()
                    softplus_neg.at = pe_n

                @block.scalar
                def _(act):
                    act.wait_ge(dve_chain.sem, softplus_neg.at)
                    act.activation(e[:], e[:], ACT.Exp).then_inc(act_chain.sem, 1)
            finish(dve_chain)
            act_chain.base += 1
            return dst

        def banded_attention(proj):
            with ExitStack() as c:
                vt = sb(c, "swa_v", [P, 4, P])
                token_major(proj, S_VA, 1, LAT, vt)
                kd = sb(c, "swa_k", [P, 2, LAT])
                qs = sb(c, "swa_q", [P, 2, LAT])
                bt = sb(c, "swa_bias", [P, SWA_H, 2 * P])
                sinks = sb(c, "swa_sinks", [P, SWA_H])
                with ExitStack() as c1:
                    block = c1.enter_context(nc.Block())

                    @block.sync
                    def _(sp):
                        sp.dma_start(bt[:], g["k_swa"]).then_inc(ld[0].sem, 16)
                        sp.dma_start(sinks[:], g["sinks_2"][0].partition_broadcast(P)).then_inc(ld[1].sem, 16)
                        sp.wait_ge(ld[0].sem, ld[0].base + 16)
                        sp.wait_ge(ld[1].sem, ld[1].base + 16)

                    @block.vector
                    def _(dve):
                        for kv in range(2):
                            for j in range(2):
                                dve.tensor_copy(kd[64 * j:64 * j + HD, kv, :], proj[64 * kv:64 * kv + HD, S_KA, 0:LAT])
                ld[0].base += 16
                ld[1].base += 16

                def half(a, j):
                    return a[64 * j:64 * j + HD]

                for kv in range(2):
                    with ExitStack() as c1:
                        def bias(dve, i, j, t, s):
                            h = bass.ds(i * 2 + (4 * kv + j), 1)
                            b = bt[:, h, P:2 * P] if t == 0 else bt[:, h, :]
                            return dve.tensor_tensor(s, s, b.rearrange("p a n -> p (a n)"), ALU.add)

                        prep = Staged([lambda pool, i, j: pool.tensor_tensor(half(qs, j)[:, j, :], tile(half(proj, j), i + (S_QA + 2 * kv)),
                                                                             half(scale_row, j).to_broadcast([HD, LAT]), ALU.mult)], [], 4)
                        pe_p, dve_p, act_p, ended = attend(
                            c1, 2, 4, lambda t: [(0, P, 0)] if t == 0 else [(0, 2 * P, (t - 1) * P)],
                            lambda t: [0] if t == 0 else [t - 1, t],
                            lambda j, t: half(qs, j)[:, j, t * P:(t + 1) * P], lambda j, k0, n: half(kd, j)[:, kv, k0:k0 + n],
                            lambda j, kt: vt[:, kt, kv * HD:(kv + 1) * HD],
                            lambda i, j: tile(half(proj, j), i + (S_QA + 2 * kv)), 1.0, prep, bias=bias,
                            sink=lambda i, j: sinks[:, bass.ds(i * 2 + (4 * kv + j), 1)])
                        simple_attention(c1, prep, 2, pe_p, dve_p, act_p, 8 * 5)
                    ended()
                    prep.ended(2)

        def recurrence(proj):
            with ExitStack() as c:
                def load(dve, ch, neg):
                    ch.link(dve.tensor_scalar(neg[:], vec3[:, V3_LAM:V3_LAM + 2], -1.0, None, ALU.mult))

                sp_lam = softplus_neg(c, 2, load)
                wbd = sb(c, "lru_w", [P, 2, 2, P])
                xc, r, ig, a0, a1, tmp = (sb(c, s, [P, 2, LAT]) for s in ("lru_x", "lru_r", "lru_i", "lru_a0", "lru_a1", "lru_tmp"))
                sc = sb(c, "lru_sc", [P, 4])
                block = c.enter_context(nc.Block())
                c0, d0, a_0 = pe_chain.base, dve_chain.base, act_chain.base
                at = {}

                @block.vector
                def _(dve):
                    ch = Chain(dve, dve_chain)
                    ch.mark(dve.memset(wbd[:], 0.0))
                    ch.mark(dve.tensor_scalar(sc[:, 0:2], sp_lam[:], -8.0, None, ALU.mult))
                    ch.link(dve.tensor_scalar(sc[:, 2:4], sp_lam[:], 8.0, None, ALU.mult))
                    at["scales"] = ch.value()
                    for k in range(2):
                        xb = proj[:, S_XB + k, :]
                        w = lambda s: col(vec3, V3_CONVW + 2 * s + k)
                        ch.link(dve.tensor_scalar(xc[:, k, :], xb[:, 0:LAT], w(3), col(vec3, V3_CONVB + k), ALU.mult, ALU.add))
                        for d in (1, 2, 3):
                            ch.link(dve.scalar_tensor_tensor(out=xc[:, k, d:], in0=xb[:, 0:LAT - d], scalar=w(3 - d), in1=xc[:, k, d:],
                                                             op0=ALU.mult, op1=ALU.add))
                    at["conv"] = ch.value()
                    dve.wait_ge(act_chain.sem, a_0 + 6 + 2)
                    ch.link(dve.tensor_tensor(ig[:], ig[:], xc[:], ALU.mult))
                    ch.link(dve.tensor_scalar(a1[:], tmp[:], 1.0, None, ALU.add))
                    ch.link(dve.reciprocal(a1[:], a1[:]))
                    ch.link(dve.scalar_tensor_tensor(out=tmp[:], in0=tmp[:], scalar=2.0, in1=a1[:], op0=ALU.mult, op1=ALU.mult))
                    at["square"] = ch.value()
                    dve.wait_ge(act_chain.sem, a_0 + 9)
                    ch.link(dve.tensor_tensor(ig[:], tmp[:], ig[:], ALU.mult))
                    h = xc
                    for k in range(2):
                        m = dve.tensor_tensor_scan(h[:, k, :], a0[:, k, :], ig[:, k, :], 0.0, ALU.mult, ALU.add)
                    ch.link(m)
                    gb = proj[:, S_GB:S_GB + 2, 0:LAT]
                    ch.link(dve.tensor_tensor(r[:], gb, gb, ALU.mult))
                    ch.link(dve.tensor_scalar(r[:], r[:], 0.044715, 1.0, ALU.mult, ALU.add))
                    ch.link(dve.tensor_tensor(r[:], r[:], gb, ALU.mult))
                    at["gelu"] = ch.value()
                    dve.wait_ge(act_chain.sem, a_0 + 10)
                    ch.link(dve.tensor_scalar(r[:], r[:], 0.5, 0.5, ALU.mult, ALU.add))
                    ch.link(dve.tensor_tensor(r[:], r[:], gb, ALU.mult))
                    ch.mark(dve.tensor_tensor(proj[:, 4:6, 0:LAT], h[:], r[:], ALU.mult))
                    ch.done()

                @block.sync
                def _(sp):
                    sp.wait_ge(dve_chain.sem, d0 + 1)
                    for s, name in enumerate(("lru_wa_2", "lru_wx_2")):
                        for n in range(8):
                            q = 32 * (n % 4)
                            sp.dma_start(wbd[q:q + 32, s, n // 4, q:q + 32], g[name][0, n]).then_inc(ld[0].sem, 16)

                @block.tensor
                def _(pe):
                    pe.wait_ge(ld[0].sem, ld[0].base + 256)
                    pe.wait_ge(dve_chain.sem, at["conv"])
                    for s in range(2):
                        for k in range(2):
                            pe.matmul(ps[:, BANK * (2 * s + k):BANK * (2 * s + k) + LAT], wbd[:, s, k, :], xc[:, k, :],
                                      start=True, stop=True).then_inc(pe_chain.sem, 1)

                @block.scalar
                def _(act):
                    n = 0
                    for s, dst, b in ((0, r, V3_BA), (1, ig, V3_BX)):
                        for k in range(2):
                            act.wait_ge(pe_chain.sem, c0 + n + 1)
                            act.activation(dst[:, k, :], ps[:, BANK * n:BANK * n + LAT], ACT.Sigmoid, bias=col(vec3, b + k)).then_inc(act_chain.sem, 1)
                            n += 1
                    act.wait_ge(act_chain.sem, a_0 + 4)
                    act.wait_ge(dve_chain.sem, at["scales"])
                    for k in range(2):
                        act.activation(a0[:, k, :], r[:, k, :], ACT.Exp, scale=sc[:, k:k + 1]).then_inc(act_chain.sem, 1)
                    for k in range(2):
                        act.activation(tmp[:, k, :], r[:, k, :], ACT.Tanh, scale=sc[:, 2 + k:3 + k]).then_inc(act_chain.sem, 1)
                    act.wait_ge(dve_chain.sem, at["square"])
                    act.activation(tmp[:], tmp[:], ACT.Sqrt).then_inc(act_chain.sem, 1)
                    act.wait_ge(dve_chain.sem, at["gelu"])
                    act.activation(r[:], r[:], ACT.Tanh, scale=0.7978845608028654).then_inc(act_chain.sem, 1)
            finish(dve_chain)
            pe_chain.base += 4
            act_chain.base += 10
            ld[0].base += 256

        def forgetting_attention(proj, ahi, alo):
            with ExitStack() as c:
                f = narrow(c, "fox_f", [(g["w_in_2"][0][:, 16 * P:16 * P + FOX_H], FOX_H)], FOX_H, ahi, alo)
                bf = sb(c, "fox_bf", [P, FOX_H])
                upto = sb(c, "fox_upto", [P, 4, LAT])
                causal = sb(c, "fox_causal", [P, P])
                with ExitStack() as c1:
                    block = c1.enter_context(nc.Block())

                    @block.sync
                    def _(sp):
                        sp.dma_start(bf[:], g["fox_bf_2"][0].partition_broadcast(P)).then_inc(ld[0].sem, 16)
                        sp.dma_start(upto[:], g["k_upto"].rearrange("(k p) n -> p k n", p=P)).then_inc(ld[1].sem, 16)
                        sp.dma_start(causal[:], g["k_causal"]).then_inc(ld[2].sem, 16)
                        for n in range(3):
                            sp.wait_ge(ld[n].sem, ld[n].base + 16)
                for n in range(3):
                    ld[n].base += 16

                def load(dve, ch, neg):
                    ch.link(dve.scalar_tensor_tensor(out=neg[:].rearrange("p (t h) -> p t h", h=FOX_H), in0=f[:], scalar=-1.0,
                                                     in1=bf[:].unsqueeze(1).to_broadcast([P, 4, FOX_H]), op0=ALU.mult, op1=ALU.subtract))

                lf = softplus_neg(c, 4 * FOX_H, load)[:].rearrange("p (t h) -> p t h", h=FOX_H)
                cq = sb(c, "fox_cq", [P, 4, FOX_H])
                ck = sb(c, "fox_ck", [P, FOX_H, LAT])
                with ExitStack() as c1:
                    wide = sb(c1, "fox_wide", [P, 4, FOX_H, P])
                    block = c1.enter_context(nc.Block())

                    @block.vector
                    def _(dve):
                        for t in range(4):
                            dve.tensor_copy(wide[:, t], lf[:, t, :].unsqueeze(2).to_broadcast([P, FOX_H, P])).then_inc(dve_chain.sem, 1)
                        dve.wait_ge(pe_chain.sem, pe_chain.base + 1)
                        dve.tensor_copy(cq[:], ps[:, 4 * BANK:4 * BANK + 16].rearrange("p (t h) -> p t h", h=FOX_H))

                    @block.tensor
                    def _(pe):
                        for t in range(4):
                            for k in range(t + 1):
                                m = pe.matmul(ps[:, 4 * BANK + 4 * t:4 * BANK + 4 * t + 4], upto[:, k, t * P:(t + 1) * P], lf[:, k, :],
                                              start=(k == 0), stop=(k == t))
                        m.then_inc(pe_chain.sem, 1)
                        pe.wait_ge(dve_chain.sem, dve_chain.base + 4)
                        for h in range(FOX_H):
                            for k in range(4):
                                m = pe.matmul(ps[:, BANK * h:BANK * h + LAT], wide[:, k, h, :], upto[:, k, :], start=(k == 0), stop=(k == 3))
                            m.then_inc(pe_chain.sem, 1)

                    @block.scalar
                    def _(act):
                        for h in range(FOX_H):
                            act.wait_ge(pe_chain.sem, pe_chain.base + 2 + h)
                            act.copy(ck[:, h, :], ps[:, BANK * h:BANK * h + LAT])
                dve_chain.base += 4
                pe_chain.base += 5

                vt = sb(c, "fox_vt", [P, 4, 2 * P])
                token_major(proj, S_VC, 2, LAT, vt)
                qs = sb(c, "fox_q", [P, 2, LAT])
                ks = sb(c, "fox_k", [P, 2, LAT])
                vs = sb(c, "fox_v", [P, 2, 4, HD])

                def half(a, j):
                    return a[64 * j:64 * j + HD]

                def bias(dve, i, j, t, s):
                    ch = bias.chain
                    n = (t + 1) * P
                    m = dve.scalar_tensor_tensor(out=s, in0=s, scalar=cq[:, t, bass.ds(i * 2 + j, 1)],
                                                 in1=ck[:, bass.ds(i * 2 + j, 1), 0:n].rearrange("p a n -> p (a n)"), op0=ALU.subtract, op1=ALU.add)
                    ch.link(m)
                    return dve.tensor_tensor(s[:, n - P:n], s[:, n - P:n], causal[:], ALU.add)

                prep = Staged([lambda pool, i, j: pool.tensor_tensor(half(qs, j)[:, j, :], tile(half(proj, j), i + S_QC), half(scale_row, j).to_broadcast([HD, LAT]), ALU.mult),
                               lambda pool, i, j: pool.tensor_copy(half(ks, j)[:, j, :], tile(half(proj, j), i + S_KC))],
                              [lambda pool, i, j: pool.tensor_copy(vs[:, j], vt[:, :, bass.ds(i * P + j * HD, HD)])], 4)
                pe_p, dve_p, act_p, ended = attend(
                    c, 2, 4, lambda t: [(0, (t + 1) * P, 0)], lambda t: list(range(t + 1)),
                    lambda j, t: half(qs, j)[:, j, t * P:(t + 1) * P], lambda j, k0, n: half(ks, j)[:, j, k0:k0 + n],
                    lambda j, kt: vs[:, j, kt, :], lambda i, j: tile(half(proj, j), i + 6), 1.0, prep, bias=bias)
                simple_attention(c, prep, 2, pe_p, dve_p, act_p, 8 * 4)
            ended()
            prep.ended(2)

        def route(c, ahi, alo):
            weights = sb(c, "experts_w", [P, N_EXP, LAT])
            with ExitStack() as c0:
                NG, EG = 4, 4
                logits = narrow(c0, "logits", [(g["w_router_group_2"][0], NG), (g["w_router_expert_2"][0], N_EXP)], NG + N_EXP, ahi, alo)
                lb = sb(c0, "route_b", [P, NG + N_EXP])
                rank = sb(c0, "route_rank", [P, 4])
                sel = sb(c0, "route_sel", [N_EXP, N_EXP * P])
                comb = sb(c0, "route_comb", [P, 4, N_EXP])
                sel_r = sb(c0, "route_sel_r", [N_EXP, N_EXP * P], F32R)
                combT = sb(c0, "route_combT", [N_EXP, 3, LAT], F32R)
                rest = sb(c0, "route_rest", [N_EXP, LAT])
                whole = sb(c0, "route_whole", [N_EXP, LAT])
                s1, s2, s3, s4, s5 = (sb(c0, f"route_s{n}", [P, 4, 1]) for n in range(5))
                g1, g2, hot, l1, l2, hot1, hot2 = (sb(c0, f"route_t{n}", [P, 4, 4]) for n in range(7))
                wide = sb(c0, "route_wide", [P, 4, N_EXP])
                block = c0.enter_context(nc.Block())
                a_0, d0 = act_chain.base, dve_chain.base
                at = {}

                @block.sync
                def _(sp):
                    sp.dma_start(lb[:, 0:NG], g["b_router_group_2"][0].partition_broadcast(P)).then_inc(ld[0].sem, 16)
                    sp.dma_start(lb[:, NG:], g["b_router_expert_2"][0].partition_broadcast(P)).then_inc(ld[0].sem, 16)
                    sp.dma_start(rank[:], g["k_rank"]).then_inc(ld[0].sem, 16)
                    sp.dma_start(sel[:], g["k_select"]).then_inc(ld[1].sem, 16)

                @block.vector
                def _(dve):
                    ch = Chain(dve, dve_chain)
                    b4 = lambda a: a[:].to_broadcast([P, 4, 4])
                    rk = rank[:].unsqueeze(1).to_broadcast([P, 4, 4])

                    def first_max(values, top, onehot, scratch):
                        ch.link(dve.tensor_reduce(top[:], values, AX, ALU.max))
                        ch.link(dve.tensor_tensor(onehot[:], values, b4(top), ALU.is_ge))
                        ch.link(dve.tensor_tensor(onehot[:], onehot[:], rk, ALU.mult))
                        ch.link(dve.tensor_reduce(scratch[:], onehot[:], AX, ALU.max))
                        ch.link(dve.tensor_tensor(onehot[:], onehot[:], b4(scratch), ALU.is_equal))

                    dve.wait_ge(ld[1].sem, ld[1].base + 16)
                    ch.mark(dve.tensor_copy(sel_r[:], sel[:]))
                    dve.wait_ge(ld[0].sem, ld[0].base + 48)
                    ch.link(dve.tensor_tensor(logits[:], logits[:], lb[:].unsqueeze(1).to_broadcast([P, 4, NG + N_EXP]), ALU.add))
                    gl = logits[:, :, 0:NG]
                    first_max(gl, s1, hot, s2)
                    ch.link(dve.tensor_tensor(g1[:], gl, b4(s1), ALU.subtract))
                    at["group"] = ch.value()
                    for q in range(NG):
                        ch.link(dve.tensor_tensor(wide[:, :, 4 * q:4 * q + 4], logits[:, :, NG + 4 * q:NG + 4 * q + 4],
                                                  hot[:, :, q:q + 1].to_broadcast([P, 4, 4]), ALU.mult))
                    ch.link(dve.tensor_reduce(l1[:], wide[:].rearrange("p t (g e) -> p t e g", g=NG), AX, ALU.add))
                    first_max(l1[:], s3, hot1, s4)
                    ch.link(dve.scalar_tensor_tensor(out=l2[:], in0=hot1[:], scalar=MASKED, in1=l1[:], op0=ALU.mult, op1=ALU.add))
                    first_max(l2[:], s4, hot2, s5)
                    ch.link(dve.tensor_tensor(s4[:], s4[:], s3[:], ALU.subtract))
                    at["second"] = ch.value()
                    dve.wait_ge(act_chain.sem, a_0 + 2)
                    ch.link(dve.tensor_reduce(s1[:], g2[:], AX, ALU.add))
                    ch.link(dve.tensor_scalar(s5[:], s2[:], 1.0, None, ALU.add))
                    ch.link(dve.tensor_tensor(s1[:], s1[:], s5[:], ALU.mult))
                    ch.link(dve.reciprocal(s1[:], s1[:]))
                    ch.link(dve.tensor_tensor(s2[:], s1[:], s2[:], ALU.mult))
                    ch.link(dve.tensor_tensor(hot1[:], hot1[:], b4(s1), ALU.mult))
                    ch.link(dve.tensor_tensor(hot2[:], hot2[:], b4(s2), ALU.mult))
                    ch.link(dve.tensor_tensor(hot1[:], hot1[:], hot2[:], ALU.add))
                    for q in range(NG):
                        ch.link(dve.tensor_tensor(comb[:, :, 4 * q:4 * q + 4], hot1[:], hot[:, :, q:q + 1].to_broadcast([P, 4, 4]), ALU.mult))
                    at["comb"] = ch.value()
                    dve.wait_ge(pe_chain.sem, pe_chain.base + 1)
                    ch.link(dve.tensor_copy(whole[:], ps[0:N_EXP, 0:LAT]))
                    ch.link(dve.tensor_copy(combT[:, 0, :], whole[:]))
                    ch.link(dve.tensor_tensor(rest[:], whole[:], combT[:, 0, :].bitcast(F32), ALU.subtract))
                    ch.link(dve.tensor_copy(combT[:, 1, :], rest[:]))
                    ch.link(dve.tensor_tensor(combT[:, 2, :], rest[:], combT[:, 1, :].bitcast(F32), ALU.subtract))
                    at["combT"] = ch.value()
                    ch.done()

                @block.scalar
                def _(act):
                    act.wait_ge(dve_chain.sem, at["group"])
                    act.activation(g2[:], g1[:], ACT.Exp).then_inc(act_chain.sem, 1)
                    act.wait_ge(dve_chain.sem, at["second"])
                    act.activation(s2[:], s4[:], ACT.Exp).then_inc(act_chain.sem, 1)
                    for e in range(N_EXP):
                        act.wait_ge(pe_chain.sem, pe_chain.base + 2 + e)
                        b = BANK * (1 + e % 4)
                        act.copy(weights[:, e, :], ps[:, b:b + LAT]).then_inc(act_chain.sem, 1)

                @block.tensor
                def _(pe):
                    pe.wait_ge(dve_chain.sem, at["comb"])
                    for t in range(4):
                        m = pe.transpose(ps[0:N_EXP, t * P:(t + 1) * P], comb[:, t, :], ident[:])
                    m.then_inc(pe_chain.sem, 1)
                    pe.wait_ge(dve_chain.sem, at["combT"])
                    for e in range(N_EXP):
                        if e >= 4:
                            pe.wait_ge(act_chain.sem, a_0 + 2 + e - 3)
                        b = BANK * (1 + e % 4)
                        for part in range(3):
                            m = pe.matmul(ps[:, b:b + LAT], sel_r[:, e * P:(e + 1) * P], combT[:, part, :], start=(part == 0), stop=(part == 2))
                        m.then_inc(pe_chain.sem, 1)
            finish(dve_chain)
            act_chain.base += 2 + N_EXP
            pe_chain.base += 1 + N_EXP
            ld[0].base += 48
            ld[1].base += 16
            return weights

        def write_out(tiles):
            with ExitStack() as c:
                o = sb(c, "o", [P, 4, D])
                block = c.enter_context(nc.Block())

                @block.tensor
                def _(pe):
                    for u in range(8):
                        t, half = u // 2, u % 2
                        if u >= 4:
                            pe.wait_ge(act_chain.sem, act_chain.base + u - 3)
                        for q in range(4):
                            b = BANK * (u % 4) + q * P
                            m = pe.transpose(ps[:, b:b + P], tiles[4 * half + q][:, t * P:(t + 1) * P], ident[:])
                        m.then_inc(pe_chain.sem, 1)

                @block.scalar
                def _(act):
                    for u in range(8):
                        t, half = u // 2, u % 2
                        act.wait_ge(pe_chain.sem, pe_chain.base + u + 1)
                        act.copy(o[:, t, half * 512:(half + 1) * 512], ps[:, BANK * (u % 4):BANK * (u % 4) + 512]).then_inc(act_chain.sem, 1)

                @block.sync
                def _(sp):
                    for t in range(4):
                        sp.wait_ge(act_chain.sem, act_chain.base + 2 * t + 2)
                        sp.dma_start(out[0, t * P:(t + 1) * P, :], o[:, t, :]).then_inc(ld[3].sem, 16)
                    sp.wait_ge(ld[3].sem, ld[3].base + 64)

        def second_block():
            modulation(g["w_mod_2"][0], (2, 2), vec3[:, 0:48], 1)
            with ExitStack() as c:
                ahi = sb(c, "a2hi", [P, KT, LAT], F32R)
                alo = sb(c, "a2lo", [P, KT, LAT], F32R)

                def prenorm(v, s):
                    with ExitStack() as c1:
                        h = sb(c1, "h", [P, KT, LAT])
                        normalize([h[:, k, :] for k in range(KT)], LAT, RMS_EPS, lambda k: col(vec1, v + k), post=(ahi, alo, *modulate_by(s)), src=xt(LAT))

                prenorm(V_MIX, 0)
                with ExitStack() as c1:
                    proj = sb(c1, "proj2", [P, 16, LAT])
                    with ExitStack() as c2:
                        run_dense(new_ring(c2, KT), [project(g["w_in_2"][0], proj, 0, 16, LAT, 0, (ahi, alo))])
                    banded_attention(proj)
                    recurrence(proj)
                    forgetting_attention(proj, ahi, alo)
                    for first, n in ((0, 4), (4, 2), (6, 2)):
                        normalize([proj[:, first + k, :] for k in range(n)], LAT, RMS_EPS, lambda k: col(vec3, V3_GAIN + first + k))
                    with ExitStack() as c2:
                        run_dense(new_ring(c2, KT), [residual(g["w_out_2"][0], 2 * KT, KT, (ahi, alo), LAT, adds={y_hi: KT, y_ready: KT},
                                                              before=split_before(proj, 0, ahi, alo, KT, LAT))])
                prenorm(V_FFN, 3)
                weights = route(c, ahi, alo)
                GE = 8
                h = (sb(c, "ehi", [P, 2 * GE, LAT], F32R), sb(c, "elo", [P, 2 * GE, LAT], F32R))
                temps = (sb(c, "sg", [P, LAT]), sb(c, "hf", [P, LAT]))
                down = g["w_down_2"][0].rearrange("e h d -> (e h) d")
                views = [g[n][0].rearrange("e (k p) c -> p e k c", p=P) for n in ("w_gate_2", "w_up_2")]
                layers = []
                for part in range(N_EXP // GE):
                    def loads(i, jj, part=part):
                        w = views[jj % 2][:, bass.ds(i + part * GE, 1), :, (jj // 2) * P:(jj // 2 + 1) * P]
                        return [(0, KT, w.rearrange("p a k c -> p (a k) c"))]

                    layers += [swiglu(temps, loads, 4, 2 * GE, (ahi, alo), h, LAT, combine=lambda i, part=part: tile(weights, i + part * GE)),
                               residual(down, 5 * KT, KT, h, LAT, row0=part * GE * D_EXP, nk=2 * GE, before=when_h_ready())]
                run_dense(new_ring(c, 2 * KT), layers)
            normalize(xt(LAT), LAT, RMS_EPS, lambda k: col(vec1, V_FINAL + k))
            write_out(xt(LAT))
        setup()
        modulation(g["w_mod"][0], (0, 1), vec2[:, 0:48], 2)
        with ExitStack() as c:
            ahi = sb(c, "ahi", [P, KT, ALL], F32R)
            alo = sb(c, "alo", [P, KT, ALL], F32R)
            normalize(xt(ALL), ALL, LN_EPS, lambda k: col(vec1, V_LN_IN_G + k), lambda k: col(vec1, V_LN_IN_B + k), center=True,
                      post=(ahi, alo, *modulate_by(0)), after=ALPHA)
            for l in range(DEPTH):
                layer(l, ahi, alo)
        second_block()


def constants():
    f = np.float32
    k = {"k_ident": np.eye(P, dtype=f)}
    w = np.arange(GRID_W)
    start = np.clip(w - KW // 2, 0, GRID_W - KW)
    inside = (w[None, :] >= start[:, None]) & (w[None, :] < start[:, None] + KW)
    k["k_na_mask"] = np.tile(np.where(inside, 0.0, MASKED), (2, 1)).astype(f)
    t = np.arange(LAT)
    freq = 10000.0 ** (-np.arange(ROPE // 4) / (ROPE // 4))
    ang = np.concatenate([(t // GRID_W)[:, None] * freq, (t % GRID_W)[:, None] * freq], -1).T
    rope = np.zeros((P, LAT))
    rope[64:80] = rope[80:96] = np.cos(ang)
    rope[96:112], rope[112:128] = -np.sin(ang), np.sin(ang)
    k["k_rope"] = rope.astype(f)
    spread = np.zeros((ROPE, P))
    for r in range(ROPE):
        spread[r, HD + r] = 1.0
        spread[(r + 16) % 32, HD + ROPE + r] = 1.0
    k["k_spread"] = spread.astype(f)

    def dft(n):
        a = 2 * np.pi * (np.outer(np.arange(n), np.arange(n)) % n) / n
        return np.cos(a), np.sin(a)

    cc, sc = dft(P)
    k["k_dft_chan"] = (np.concatenate([cc, sc], 1) / np.sqrt(P)).astype(f)
    for name, n in (("k_dft_lat", LAT), ("k_dft_ctx", CTX)):
        cs, ss = dft(n)
        k[name] = (np.stack([cs, -ss], 1) / np.sqrt(n)).astype(f)
    q, kk = np.arange(P)[:, None] + P, np.arange(2 * P)[None, :]
    dist = q - kk
    valid = (dist >= 0) & (dist < P)
    slopes = 2.0 ** (-8.0 * np.arange(1, SWA_H + 1) / SWA_H)
    k["k_swa"] = np.where(valid[:, None, :], -slopes[None, :, None] * dist[:, None, :], MASKED).astype(f)
    k["k_upto"] = (t[:, None] <= t[None, :]).astype(f)
    k["k_causal"] = np.where(np.arange(P)[None, :] <= np.arange(P)[:, None], 0.0, MASKED).astype(f)
    sel = np.zeros((N_EXP, N_EXP, P))
    for e in range(N_EXP):
        sel[e, e] = 1.0
    k["k_select"] = sel.reshape(N_EXP, N_EXP * P).astype(f)
    k["k_rank"] = np.tile(np.arange(4, 0, -1), (P, 1)).astype(f)
    return k


_INS = ("x c ctx c_ctx ln_in_g ln_in_b w_mod b_mod w_in mla_q_norm_g mla_kv_norm_g w_uq w_qr w_uk w_uv na_rpb w_branch w_out "
        "ln1_g ln1_b ln2_g ln2_b w_ffn_gate w_ffn_up w_ffn_down c_2 w_mod_2 b_mod_2 norm_mix_2 norm_ffn_2 w_in_2 w_out_2 out_gain_2 "
        "sinks_2 conv_w_2 conv_b_2 lru_wa_2 lru_ba_2 lru_wx_2 lru_bx_2 lru_lam_2 fox_bf_2 w_router_group_2 b_router_group_2 "
        "w_router_expert_2 b_router_expert_2 w_gate_2 w_up_2 w_down_2 norm_final_2").split()


def kernel(**inputs):
    import concourse.bacc as bacc
    from concourse.bass_utils import run_bass_kernel_spmd

    nc = bacc.Bacc("TRN2", target_bir_lowering=False, num_devices=1)
    arrays, aps = {}, {}
    every = {**{n: inputs[n] for n in _INS}, **constants()}
    for name, a in every.items():
        a = np.ascontiguousarray(a)
        arrays[f"in_{name}"] = a
        aps[name] = nc.dram_tensor(f"in_{name}", a.shape, mybir.dt.from_np(a.dtype), kind="ExternalInput").ap()
    out = nc.dram_tensor("out", (1, LAT, D), F32, kind="ExternalOutput").ap()
    program(nc, aps, out)
    r = run_bass_kernel_spmd(nc, [arrays], core_ids=[0])
    return r.results[0]["out"]
```
